# Optimizing a Trainium2 kernel written in Bass

```python
import math
import jax, jax.numpy as jnp
from jax import lax
import numpy as np

D_MODEL = 1024
BATCH = 1
SEQ = 256
DEPTH = 1

D_INNER = D_MODEL
M_WIDTH = D_INNER // 2
M_HEADS = 4
M_HEAD_DIM = M_WIDTH // M_HEADS
H_WIDTH = D_INNER - M_WIDTH
H_GROUPS = 8
HYENA_ORDER = 2
N_DIR = 2
CHUNK = 128
FILTER_EMB = 33
FILTER_HIDDEN = 64
N_SIN = 3
DECAY_TARGET = 1e-2
FAST_DECAY_PCT = 0.3
SLOW_DECAY_PCT = 1.5
D_FF = 4 * D_MODEL
N_GATE = 2 * N_DIR * M_HEADS
EPS = 1e-6

OFF_MQ = 0
OFF_MK = OFF_MQ + M_WIDTH
OFF_HV = OFF_MK + M_WIDTH
OFF_HX1 = OFF_HV + H_WIDTH
OFF_HX2 = OFF_HX1 + H_WIDTH
N_CONV = OFF_HX2 + H_WIDTH
OFF_MV = N_CONV
OFF_MO = OFF_MV + M_WIDTH
OFF_GATE = OFF_MO + M_WIDTH
N_IN = OFF_GATE + N_GATE


def rms_norm(x, w):
    xf = x.astype(jnp.float32)
    y = xf * lax.rsqrt(jnp.mean(xf * xf, axis=-1, keepdims=True) + EPS)
    return (y * w.astype(jnp.float32)).astype(x.dtype)

def short_conv3(u, w, b):
    up = jnp.pad(u, ((0, 0), (1, 1), (0, 0)))
    return up[:, :-2] * w[0] + up[:, 1:-1] * w[1] + up[:, 2:] * w[2] + b

def mlstm_chunkwise(q, k, v, log_i, log_f):
    B, H, S, D = q.shape
    L = CHUNK
    NC = S // L
    qc = q.reshape(B, H, NC, L, D)
    kc = k.reshape(B, H, NC, L, D)
    vc = v.reshape(B, H, NC, L, D)
    li = log_i.reshape(B, H, NC, L)
    bcum = jnp.cumsum(log_f.reshape(B, H, NC, L), axis=-1)
    g = bcum[..., -1]
    a = g[..., None] - bcum + li

    def step(carry, xs):
        C, n, m = carry
        k_c, v_c, a_c, g_c = xs
        m_new = jnp.maximum(g_c + m, jnp.max(a_c, axis=-1))
        decay = jnp.exp(g_c + m - m_new)
        w = jnp.exp(a_c - m_new[..., None])
        C_new = decay[..., None, None] * C + jnp.einsum('bhl,bhld,bhle->bhde', w, k_c, v_c)
        n_new = decay[..., None] * n + jnp.einsum('bhl,bhld->bhd', w, k_c)
        return (C_new, n_new, m_new), (C, n, m)

    init = (jnp.zeros((B, H, D, D), jnp.float32),
            jnp.zeros((B, H, D), jnp.float32),
            jnp.zeros((B, H), jnp.float32))
    xs = (jnp.moveaxis(kc, 2, 0), jnp.moveaxis(vc, 2, 0),
          jnp.moveaxis(a, 2, 0), jnp.moveaxis(g, 2, 0))
    _, (C_s, n_s, m_s) = lax.scan(step, init, xs)
    C_s = jnp.moveaxis(C_s, 0, 2)
    n_s = jnp.moveaxis(n_s, 0, 2)
    m_s = jnp.moveaxis(m_s, 0, 2)

    causal = jnp.tril(jnp.ones((L, L), dtype=bool))
    dmat = bcum[..., :, None] - bcum[..., None, :] + li[..., None, :]
    dmat = jnp.where(causal, dmat, -jnp.inf)
    inter_log = bcum + m_s[..., None]
    m_t = jnp.maximum(inter_log, jnp.max(dmat, axis=-1))
    wts = jnp.exp(dmat - m_t[..., None])
    s_qk = jnp.einsum('bhctd,bhcsd->bhcts', qc, kc) * wts
    inter_scale = jnp.exp(inter_log - m_t)
    num = (jnp.einsum('bhcts,bhcse->bhcte', s_qk, vc)
           + inter_scale[..., None] * jnp.einsum('bhctd,bhcde->bhcte', qc, C_s))
    den = s_qk.sum(-1) + inter_scale * jnp.einsum('bhctd,bhcd->bhct', qc, n_s)
    h = num / jnp.maximum(jnp.abs(den), jnp.exp(-m_t))[..., None]
    return h.reshape(B, H, S, D)

def hyena_filters(L, w1, b1, w2, b2, w3, b3, w4, freq):
    bands = (FILTER_EMB - 1) // 2
    t = jnp.linspace(0.0, 1.0, L, dtype=jnp.float32)[:, None]
    t_resc = jnp.arange(L, dtype=jnp.float32)[:, None]
    ang = 2.0 * math.pi * t_resc / L
    f = jnp.linspace(1e-4, bands - 1, bands, dtype=jnp.float32)[None, :]
    z = jnp.concatenate([t, jnp.cos(f * ang), -jnp.sin(f * ang)], axis=-1)
    fr = freq.astype(jnp.float32)
    h = jnp.sin(fr[0] * (z @ w1.astype(jnp.float32) + b1.astype(jnp.float32)))
    h = jnp.sin(fr[1] * (h @ w2.astype(jnp.float32) + b2.astype(jnp.float32)))
    h = jnp.sin(fr[2] * (h @ w3.astype(jnp.float32) + b3.astype(jnp.float32)))
    h = (h @ w4.astype(jnp.float32)).reshape(L, N_DIR, HYENA_ORDER, H_WIDTH)
    max_decay = math.log(DECAY_TARGET) / FAST_DECAY_PCT
    min_decay = math.log(DECAY_TARGET) / SLOW_DECAY_PCT
    deltas = jnp.linspace(min_decay, max_decay, H_WIDTH, dtype=jnp.float32)
    window = jnp.exp(-t[:, :, None, None] * jnp.abs(deltas))
    return h * window

def two_sided_fft_conv(u, k_fwd, k_bwd, bias):
    S = u.shape[1]
    kern = jnp.concatenate([k_fwd, jnp.zeros_like(k_fwd[:1]), k_bwd[:0:-1]], axis=0)
    K = jnp.fft.rfft(kern, axis=0)
    U = jnp.fft.rfft(u, n=2 * S, axis=1)
    y = jnp.fft.irfft(U * K[None], n=2 * S, axis=1)[:, :S]
    return y + u * bias

def group_rms(u, n_groups, w):
    B, S, C = u.shape
    ug = u.reshape(B, S, n_groups, C // n_groups)
    ug = ug * lax.rsqrt(jnp.mean(ug * ug, axis=-1, keepdims=True) + EPS)
    return ug.reshape(B, S, C) * w.astype(jnp.float32)

def first_inputs(seed: int = 0) -> dict:
    key = jax.random.key(seed)
    ks = jax.random.split(key, 32)
    f32 = jnp.float32
    nrm = lambda k, shape, scale: jax.random.normal(k, shape, f32) * scale
    gain = lambda k, n: 1.0 + 0.05 * jax.random.normal(k, (n,), f32)
    i_bias = nrm(ks[6], (M_HEADS,), 0.1)
    f_bias = jnp.linspace(3.0, 6.0, M_HEADS, dtype=f32) + nrm(ks[7], (M_HEADS,), 0.1)
    i_bias_b = nrm(ks[8], (M_HEADS,), 0.1)
    f_bias_b = jnp.linspace(3.0, 6.0, M_HEADS, dtype=f32) + nrm(ks[9], (M_HEADS,), 0.1)
    return {
        "x": jax.random.normal(ks[0], (BATCH, SEQ, D_MODEL), f32),
        "norm_mix_pre": gain(ks[1], D_MODEL),
        "norm_mix_post": gain(ks[2], D_MODEL),
        "norm_mlp_pre": gain(ks[3], D_MODEL),
        "norm_mlp_post": gain(ks[4], D_MODEL),
        "w_in": nrm(ks[5], (D_MODEL, N_IN), D_MODEL ** -0.5),
        "b_gates": jnp.concatenate([i_bias, f_bias, i_bias_b, f_bias_b]),
        "conv_w": nrm(ks[10], (3, N_CONV), 3 ** -0.5),
        "conv_b": nrm(ks[11], (N_CONV,), 0.02),
        "mlstm_norm_w": gain(ks[12], M_WIDTH),
        "hyena_norm_w": gain(ks[13], H_WIDTH),
        "filt_w1": nrm(ks[14], (FILTER_EMB, FILTER_HIDDEN), FILTER_EMB ** -0.5),
        "filt_b1": nrm(ks[15], (FILTER_HIDDEN,), 0.02),
        "filt_w2": nrm(ks[16], (FILTER_HIDDEN, FILTER_HIDDEN), FILTER_HIDDEN ** -0.5),
        "filt_b2": nrm(ks[17], (FILTER_HIDDEN,), 0.02),
        "filt_w3": nrm(ks[18], (FILTER_HIDDEN, FILTER_HIDDEN), FILTER_HIDDEN ** -0.5),
        "filt_b3": nrm(ks[19], (FILTER_HIDDEN,), 0.02),
        "filt_w4": nrm(ks[20], (FILTER_HIDDEN, N_DIR * HYENA_ORDER * H_WIDTH), FILTER_HIDDEN ** -0.5),
        "filt_freq": 1.0 + 0.05 * jax.random.normal(ks[21], (N_SIN, FILTER_HIDDEN), f32),
        "filt_bias": nrm(ks[22], (HYENA_ORDER, H_WIDTH), 0.1),
        "w_out": nrm(ks[23], (D_INNER, D_MODEL), D_INNER ** -0.5),
        "w_mlp_in": nrm(ks[24], (D_MODEL, D_FF), D_MODEL ** -0.5),
        "w_mlp_out": nrm(ks[25], (D_FF, D_MODEL), D_FF ** -0.5),
    }

def first_block(x, norm_mix_pre, norm_mix_post, norm_mlp_pre, norm_mlp_post, w_in, b_gates,
              conv_w, conv_b, mlstm_norm_w, hyena_norm_w, filt_w1, filt_b1, filt_w2, filt_b2,
              filt_w3, filt_b3, filt_w4, filt_freq, filt_bias, w_out, w_mlp_in, w_mlp_out):
    B, S, _ = x.shape
    f32 = jnp.float32
    for _layer in range(DEPTH):
        hn = rms_norm(x, norm_mix_pre)
        proj = (hn @ w_in).astype(f32)
        cv = short_conv3(proj[..., :N_CONV], conv_w.astype(f32), conv_b.astype(f32))

        def heads(u):
            return u.reshape(B, S, M_HEADS, M_HEAD_DIM).transpose(0, 2, 1, 3)
        q = heads(jax.nn.silu(cv[..., OFF_MQ:OFF_MQ + M_WIDTH]))
        k = heads(jax.nn.silu(cv[..., OFF_MK:OFF_MK + M_WIDTH])) * (M_HEAD_DIM ** -0.5)
        v = heads(proj[..., OFF_MV:OFF_MV + M_WIDTH])
        o_gate = jax.nn.sigmoid(proj[..., OFF_MO:OFF_MO + M_WIDTH])
        gates = (proj[..., OFF_GATE:OFF_GATE + N_GATE] + b_gates.astype(f32)).transpose(0, 2, 1)
        gates = gates.reshape(B, 2 * N_DIR, M_HEADS, S)
        h_fwd = mlstm_chunkwise(q, k, v, gates[:, 0], jax.nn.log_sigmoid(gates[:, 1]))
        flip = lambda u: jnp.flip(u, axis=2)
        h_bwd = flip(mlstm_chunkwise(flip(q), flip(k), flip(v), flip(gates[:, 2]),
                                     flip(jax.nn.log_sigmoid(gates[:, 3]))))
        h_m = (h_fwd + h_bwd).transpose(0, 2, 1, 3).reshape(B, S, M_WIDTH) * o_gate
        y_m = group_rms(h_m, M_HEADS, mlstm_norm_w)

        filt = hyena_filters(S, filt_w1, filt_b1, filt_w2, filt_b2, filt_w3, filt_b3,
                             filt_w4, filt_freq)
        fb = filt_bias.astype(f32)
        z = cv[..., OFF_HV:OFF_HV + H_WIDTH]
        z = cv[..., OFF_HX1:OFF_HX1 + H_WIDTH] * two_sided_fft_conv(z, filt[:, 0, 0], filt[:, 1, 0], fb[0])
        z = cv[..., OFF_HX2:OFF_HX2 + H_WIDTH] * two_sided_fft_conv(z, filt[:, 0, 1], filt[:, 1, 1], fb[1])
        y_h = group_rms(z, H_GROUPS, hyena_norm_w)

        mix = jnp.concatenate([y_m, y_h], axis=-1).astype(x.dtype) @ w_out
        x = x + rms_norm(mix, norm_mix_post)

        hm = rms_norm(x, norm_mlp_pre)
        ff = jnp.square(jax.nn.relu(hm @ w_mlp_in)) @ w_mlp_out
        x = x + rms_norm(ff, norm_mlp_post)
    return x


MIX_WIDTH = D_MODEL
ATTN_WIDTH = MIX_WIDTH // 2
POOL_WIDTH = MIX_WIDTH - ATTN_WIDTH
N_HEADS = 8
HEAD_DIM = ATTN_WIDTH // N_HEADS
DILATED_BRANCHES = ((128, 1), (512, 4), (2048, 16))
MAX_SPAN = 2048
Q_BLOCK = 128
POOL_WINDOWS = (2, 4, 8, 16)
POOL_GROUP = POOL_WIDTH // len(POOL_WINDOWS)
PEER_HEADS = 8
PEER_NKEYS = 128
PEER_EXPERTS = PEER_NKEYS * PEER_NKEYS
PEER_QDIM = 256
PEER_TOPK = 16
TOKEN_CHUNK = 128
N_MOD = 6


def rmsnorm(x, g):
    xf = x.astype(jnp.float32)
    y = xf * lax.rsqrt(jnp.mean(xf * xf, axis=-1, keepdims=True) + EPS)
    return (y * g.astype(jnp.float32)).astype(x.dtype)

def alibi_slopes(n):
    return jnp.asarray([2.0 ** (-8.0 * (h + 1) / n) for h in range(n)], dtype=jnp.float32)

def dilated_attention(q, k, v):
    B, S, H, hd = q.shape
    nblk = S // Q_BLOCK
    pad = ((0, 0), (MAX_SPAN, 0), (0, 0), (0, 0))
    k_pad = jnp.pad(k, pad)
    v_pad = jnp.pad(v, pad)
    slopes = alibi_slopes(H)
    scale = HEAD_DIM ** -0.5
    qi = jnp.arange(Q_BLOCK)
    branches = []
    for w, d in DILATED_BRANCHES:
        j = jnp.arange(w // d + 1)
        gidx = qi[:, None] + MAX_SPAN - j[None, :] * d
        dist = j * d
        branches.append((gidx, dist))

    def block(idx):
        b = idx // nblk
        start = (idx % nblk) * Q_BLOCK
        qb = lax.dynamic_slice(q, (b, start, 0, 0), (1, Q_BLOCK, H, hd))[0].astype(jnp.float32) * scale
        ks = lax.dynamic_slice(k_pad, (b, start, 0, 0), (1, MAX_SPAN + Q_BLOCK, H, hd))[0]
        vs = lax.dynamic_slice(v_pad, (b, start, 0, 0), (1, MAX_SPAN + Q_BLOCK, H, hd))[0]
        pos = start + qi
        lses, outs = [], []
        for gidx, dist in branches:
            kg = jnp.take(ks, gidx, axis=0).astype(jnp.float32)
            vg = jnp.take(vs, gidx, axis=0).astype(jnp.float32)
            distf = dist.astype(jnp.float32)
            s = jnp.einsum('qhd,qjhd->hqj', qb, kg) - slopes[:, None, None] * distf[None, None, :]
            valid = (pos[:, None] - dist[None, :]) >= 0
            s = jnp.where(valid[None], s, -1e30)
            m = jnp.max(s, axis=-1, keepdims=True)
            p = jnp.exp(s - m)
            z = jnp.sum(p, axis=-1, keepdims=True)
            o = jnp.einsum('hqj,qjhd->qhd', p, vg) / jnp.transpose(z, (1, 0, 2))
            lses.append(jnp.transpose((m + jnp.log(z))[..., 0], (1, 0)))
            outs.append(o)
        wts = jax.nn.softmax(jnp.stack(lses, axis=0), axis=0)
        out = jnp.einsum('gqh,gqhd->qhd', wts, jnp.stack(outs, axis=0))
        return out.astype(q.dtype)

    out = lax.map(block, jnp.arange(B * nblk))
    return out.reshape(B, S, H, hd)

def multiscale_pool(u, w_pool, pool_scale):
    B, S, C = u.shape
    uf = u.astype(jnp.float32)
    cs = jnp.pad(jnp.cumsum(uf, axis=1), ((0, 0), (1, 0), (0, 0)))
    pos1 = jnp.arange(1, S + 1, dtype=jnp.float32)
    outs = []
    for g, w in enumerate(POOL_WINDOWS):
        sl = slice(g * POOL_GROUP, (g + 1) * POOL_GROUP)
        cg = cs[:, :, sl]
        upper = cg[:, 1:]
        lower = jnp.pad(cg, ((0, 0), (w - 1, 0), (0, 0)))[:, :S]
        cnt = jnp.minimum(pos1, float(w))[None, :, None]
        mixed = (upper - lower) / cnt - uf[:, :, sl]
        outs.append(jnp.einsum('bsc,ce->bse', mixed, w_pool[g].astype(jnp.float32)))
    y = jnp.concatenate(outs, axis=-1) * pool_scale.astype(jnp.float32)
    return y.astype(u.dtype)

def peer_ffn(h, w_q, sub_keys, expert_u, expert_v):
    B, S, D = h.shape
    T = B * S
    half = PEER_QDIM // 2
    K = PEER_TOPK
    hc = h.reshape(T // TOKEN_CHUNK, TOKEN_CHUNK, D)

    def chunk(xc):
        C = xc.shape[0]
        q = jnp.einsum('cd,de->ce', xc, w_q).astype(jnp.float32).reshape(C, PEER_HEADS, 2, half)
        s = jnp.einsum('chpk,pnk->chpn', q, sub_keys.astype(jnp.float32))
        sv, si = lax.top_k(s, K)
        cand = sv[:, :, 0, :, None] + sv[:, :, 1, None, :]
        cand_id = si[:, :, 0, :, None] * PEER_NKEYS + si[:, :, 1, None, :]
        cand = cand.reshape(C, PEER_HEADS, K * K)
        cand_id = cand_id.reshape(C, PEER_HEADS, K * K)
        top_v, top_pos = lax.top_k(cand, K)
        eid = jnp.take_along_axis(cand_id, top_pos, axis=-1)
        gate = jax.nn.softmax(top_v, axis=-1)
        u = expert_u[eid]
        act = jax.nn.gelu(jnp.einsum('cd,chkd->chk', xc, u).astype(jnp.float32), approximate=False)
        vv = expert_v[eid]
        y = jnp.einsum('chk,chkd->cd', (gate * act).astype(vv.dtype), vv)
        return y.astype(xc.dtype)

    return lax.map(chunk, hc).reshape(B, S, D)

def second_inputs(seed: int = 0) -> dict:
    key = jax.random.key(seed)
    ks = jax.random.split(key, 16)
    D = D_MODEL
    proj_out = 3 * ATTN_WIDTH + POOL_WIDTH
    f32 = jnp.float32
    x = jax.random.normal(ks[0], (BATCH, SEQ, D), f32)
    c = jax.random.normal(ks[1], (BATCH, D), f32)
    w_ada = jax.random.normal(ks[2], (DEPTH, D, N_MOD * D), f32) * (0.5 * D ** -0.5)
    b_ada = jax.random.normal(ks[3], (DEPTH, N_MOD * D), f32) * 0.01
    norm1_g = 1.0 + 0.05 * jax.random.normal(ks[4], (DEPTH, D), f32)
    w_in = jax.random.normal(ks[5], (DEPTH, D, proj_out), f32) * D ** -0.5
    pool_w = jax.random.normal(ks[6], (DEPTH, len(POOL_WINDOWS), POOL_GROUP, POOL_GROUP), f32) * POOL_GROUP ** -0.5
    pool_scale = 1.0 + 0.1 * jax.random.normal(ks[7], (DEPTH, POOL_WIDTH), f32)
    w_out = jax.random.normal(ks[8], (DEPTH, MIX_WIDTH, D), f32) * MIX_WIDTH ** -0.5
    norm2_g = 1.0 + 0.05 * jax.random.normal(ks[9], (DEPTH, D), f32)
    peer_wq = jax.random.normal(ks[10], (DEPTH, D, PEER_HEADS * PEER_QDIM), f32) * D ** -0.5
    peer_subkeys = jax.random.normal(ks[11], (DEPTH, 2, PEER_NKEYS, PEER_QDIM // 2), f32) * (PEER_QDIM // 2) ** -0.5
    peer_u = jax.random.normal(ks[12], (DEPTH, PEER_EXPERTS, D), f32) * D ** -0.5
    peer_v = jax.random.normal(ks[13], (DEPTH, PEER_EXPERTS, D), f32) * 0.5
    final_g = 1.0 + 0.05 * jax.random.normal(ks[14], (D,), f32)
    return {"x": x, "c": c, "w_ada": w_ada, "b_ada": b_ada, "norm1_g": norm1_g,
            "w_in": w_in, "pool_w": pool_w, "pool_scale": pool_scale, "w_out": w_out,
            "norm2_g": norm2_g, "peer_wq": peer_wq, "peer_subkeys": peer_subkeys,
            "peer_u": peer_u, "peer_v": peer_v, "final_g": final_g}

def second_block(x, c, w_ada, b_ada, norm1_g, w_in, pool_w, pool_scale, w_out,
              norm2_g, peer_wq, peer_subkeys, peer_u, peer_v, final_g):
    B, S, D = x.shape
    A = ATTN_WIDTH
    for l in range(DEPTH):
        mod = jnp.einsum('bd,de->be', jax.nn.silu(c), w_ada[l]) + b_ada[l]
        sh1, sc1, g1, sh2, sc2, g2 = jnp.split(mod[:, None, :], N_MOD, axis=-1)
        h = rmsnorm(x, norm1_g[l]) * (1.0 + sc1) + sh1
        proj = jnp.einsum('bsd,de->bse', h, w_in[l])
        q, k, v, u = jnp.split(proj, [A, 2 * A, 3 * A], axis=-1)
        attn = dilated_attention(q.reshape(B, S, N_HEADS, HEAD_DIM),
                                 k.reshape(B, S, N_HEADS, HEAD_DIM),
                                 v.reshape(B, S, N_HEADS, HEAD_DIM)).reshape(B, S, A)
        pool = multiscale_pool(u, pool_w[l], pool_scale[l])
        mixed = jnp.einsum('bse,ed->bsd', jnp.concatenate([attn, pool], axis=-1), w_out[l])
        x = x + g1 * mixed
        h2 = rmsnorm(x, norm2_g[l]) * (1.0 + sc2) + sh2
        x = x + g2 * peer_ffn(h2, peer_wq[l], peer_subkeys[l], peer_u[l], peer_v[l])
    return rmsnorm(x, final_g)


def setup_inputs(seed=0):
    out = dict(first_inputs(seed))
    for name, value in second_inputs(seed + 1).items():
        if name != "x":
            out[name + "_2"] = value
    return out


def reference(
    x, norm_mix_pre, norm_mix_post, norm_mlp_pre, norm_mlp_post, w_in, b_gates, conv_w, conv_b,
    mlstm_norm_w, hyena_norm_w, filt_w1, filt_b1, filt_w2, filt_b2, filt_w3, filt_b3, filt_w4,
    filt_freq, filt_bias, w_out, w_mlp_in, w_mlp_out, c_2, w_ada_2, b_ada_2, norm1_g_2, w_in_2,
    pool_w_2, pool_scale_2, w_out_2, norm2_g_2, peer_wq_2, peer_subkeys_2, peer_u_2, peer_v_2,
    final_g_2,
):
    x = first_block(
        x, norm_mix_pre, norm_mix_post, norm_mlp_pre, norm_mlp_post, w_in, b_gates, conv_w,
        conv_b, mlstm_norm_w, hyena_norm_w, filt_w1, filt_b1, filt_w2, filt_b2, filt_w3,
        filt_b3, filt_w4, filt_freq, filt_bias, w_out, w_mlp_in, w_mlp_out,
    )
    return second_block(
        x, c_2, w_ada_2, b_ada_2, norm1_g_2, w_in_2, pool_w_2, pool_scale_2, w_out_2, norm2_g_2,
        peer_wq_2, peer_subkeys_2, peer_u_2, peer_v_2, final_g_2,
    )


_drawn_inputs = setup_inputs


def setup_inputs(seed=0):
    import zlib

    import numpy as np

    out = dict(_drawn_inputs(seed))
    spreads = {}
    factors = {'b_ada_2': 7.25, 'norm1_g_2': 7.321, 'pool_scale_2': 5.168, 'norm2_g_2': 4.818}
    for name, (base, spread) in spreads.items():
        noise = np.random.default_rng([zlib.crc32(name.encode()), seed]).standard_normal(out[name].shape)
        drawn = base * np.exp(spread * noise) if base else spread * noise
        out[name] = __import__('jax').numpy.asarray(drawn.astype(out[name].dtype))
    for name, factor in factors.items():
        out[name] = (out[name] * factor).astype(out[name].dtype)
    return out
```

```python
import math
from contextlib import ExitStack

import numpy as np

import concourse.bass as bass
import concourse.mybir as mybir

P = 128
T = 256
TT = T // P
D = 1024
DC = D // P
FF = 4 * D
HALF = 512
HC = HALF // P
M_HEADS = 4
FILTER_EMB, FILTER_HIDDEN = 33, 64
A_HEADS, A_DIM = 8, 64
HEAD_ORDER = (0, 2, 4, 6, 1, 3, 5, 7)
BRANCHES = ((128, 1), (512, 4), (2048, 16))
WINDOWS = (2, 4, 8, 16)
PAD = 16
PEER_HEADS, NKEYS, TOPK = 8, 128, 16
SLOTS = PEER_HEADS * TOPK
N_MOD = 6
EPS = 1e-6
NEG = -1e30
LOWEST = -3.0e38
BESIDE = 48
GROUP = 4
RING = 4
TILE = D

F32 = mybir.dt.float32
U32 = mybir.dt.uint32
ALU = mybir.AluOpType
ACT = mybir.ActivationFunctionType
AX = mybir.AxisListType

STREAM = {}
_at = 0
for _name, _n in (("conv", 20), ("ogate", 4), ("value", 4), ("out", 8), ("mlp_in", 32), ("mlp_out", 32),
                  ("qk", 8), ("pool_in", 4), ("value2", 4), ("out2", 8), ("peer_q", 16)):
    STREAM[_name] = _at
    _at += _n
N_TILES = _at

COLS = {}
_at = 0
for _name, _n in (("norm_mix_pre", DC), ("norm_mix_post", DC), ("norm_mlp_pre", DC), ("norm_mlp_post", DC),
                  ("tap0", 20), ("tap1", 20), ("tap2", 20), ("conv_b", 20), ("mlstm_norm", HC),
                  ("hyena_norm", HC), ("norm1", DC), ("pool_scale", HC), ("norm2", DC), ("final", DC),
                  ("b_ada", N_MOD * DC), ("c", DC), ("b_gates", 1), ("filt_b", 3), ("filt_freq", 3)):
    COLS[_name] = _at
    _at += _n
N_COLS = _at

CONST = {}
_at = 0
for _name, _n in (("ident", P), ("ones", P), ("ones_half", P), ("iota", P), ("eps", 1), ("head_rows", M_HEADS * P),
                  ("scan_ones", T), ("zeros", HALF)):
    CONST[_name] = _at
    _at += _n
N_CONST = _at
CONST1 = {}
_at = 0
for _name, _n in (("emb", T), ("window", TT * HALF), ("fwd_cos", TT * T), ("fwd_sin", TT * T),
                  ("fwd_cos_a", TT * P), ("fwd_sin_a", TT * P), ("inv_cos", TT * T), ("inv_sin", TT * T),
                  ("dir_mask", TT * 2 * T)):
    CONST1[_name] = _at
    _at += _n
N_CONST1 = _at
COUNT_AT = A_HEADS * P + A_HEADS * T
ATT_COLS = COUNT_AT + HC * T


class Queue:

    def __init__(self, engine, sem):
        self.engine, self.sem, self.n, self.i, self.per = engine, sem, 0, None, 0

    def after(self, *steps):
        for sem, value in steps:
            self.engine.wait_ge(sem, value)

    def mark(self, instruction):
        instruction.then_inc(self.sem, 1)
        self.n += 1
        return (self.sem, self.n if self.i is None else self.n + self.i * self.per)

    def enter(self, i, per):
        self.i, self.per, self.first = i, per, self.n

    def leave(self, trips):
        assert self.n == self.first + self.per, (self.n - self.first, self.per)
        self.n = self.first + trips * self.per
        self.i = None
        return (self.sem, self.n)

    def before(self, nth):
        assert self.first + nth > self.per
        return (self.sem, self.i * self.per + (self.first + nth - self.per))

    def last(self):
        return (self.sem, self.n)

    def last_at(self, back=0):
        return (self.sem, self.i * self.per + (self.n + back))


def build(nc, x_d, tiles_d, u_d, v_d, ada_d, cols_d, const_d, const1_d, att_d, gate_w_d, f1_d, f23_d, f4_d,
          fbias_d, poolw_d, keys_d, out_d):
    ctx = ExitStack()
    with ctx:
        def sem(name):
            return ctx.enter_context(nc.semaphore(name))

        def sb(name, shape, stack=ctx, dt=F32):
            return stack.enter_context(nc.sbuf_tensor(name, [P, *shape], dt))

        PE = Queue(nc.tensor, sem("pe_steps"))
        VE = Queue(nc.vector, sem("vector_steps"))
        SE = Queue(nc.scalar, sem("scalar_steps"))
        GP = Queue(nc.gpsimd, sem("gpsimd_steps"))

        banks = [ctx.enter_context(nc.psum_tensor(f"bank{n}", [P, 512], F32)) for n in range(8)]

        freed = {}

        def free(*numbers):
            PE.after(*(freed[b] for b in numbers if b in freed))

        ring = sb("ring", [RING, TILE])
        cols = sb("cols", [N_COLS])
        const = sb("const", [N_CONST])
        xT = sb("xT", [DC, T])
        hT = sb("hT", [DC, T])
        rstd = sb("rstd", [T])
        mod = sb("mod", [N_MOD * DC])
        gain = sb("gain", [DC])

        def col(name, c=0, n=1, rows=P):
            return cols[0:rows, COLS[name] + c:COLS[name] + c + n]

        def col_at(name, c):
            return cols[:, bass.ds(c + COLS[name], 1)]

        def cst(name, n, rows=P):
            return const[0:rows, CONST[name]:CONST[name] + n]

        ident, ones = cst("ident", P), cst("ones", P)
        ones_half, iota = cst("ones_half", P), cst("iota", P)
        eps_col = cst("eps", 1)

        def load(engine, name, out, in_):
            s = sem("loaded_" + name)
            engine.dma_start(out, in_).then_inc(s, 16)
            return (s, 16)

        tile_loaded = [sem(f"tile_loaded{k}") for k in range(RING)]
        tile_used = sem("tile_used")
        nc.tensor.sem_inc(tile_used, RING)

        def fetch(k, j, source):
            nc.sync.wait_ge(tile_used, j + 1)
            nc.sync.dma_start(ring[:, k, :], source.rearrange("a p n -> p (a n)")).then_inc(tile_loaded[k], 16)

        def arrived(k, j):
            return (tile_loaded[k], (j - k) * (16 // RING) + 16)

        def used(j):
            return (tile_used, j + 1 + RING)

        def block(k, c):
            return ring[:, k, c * P:(c + 1) * P]

        def product(out, k, j, rhs, first=True, last=True):
            PE.after(arrived(k, j))
            for c in range(DC):
                mm = nc.tensor.matmul(out, block(k, c), rhs(c), start=first and c == 0, stop=last and c == DC - 1)
            mm.then_inc(tile_used, 1)

        def chunk_of(src):
            return lambda c: src[:, c, :]

        def linear(name, n, src, evict, queues):
            trips = n // RING
            base = STREAM[name]
            free(*range(RING))
            with nc.Fori(0, trips) as i:
                for q, per in queues:
                    q.enter(i, per)
                for k in range(RING):
                    j = base + i * RING + k
                    fetch(k, j, tiles_d[bass.ds(j, 1)])
                for k in range(RING):
                    j = base + i * RING + k
                    q, nth = evict.frees[k]
                    PE.after(q.before(nth))
                    product(banks[k][:, 0:T], k, j, chunk_of(src))
                    evict(k, i * RING + k, banks[k][:, 0:T], used(j))
            steps = [q.leave(trips) for q, _ in queues]
            for k in range(RING):
                freed[k] = evict.frees[k][0].last()
            return steps

        def values(name, v_sb):
            base = STREAM[name]
            for k in range(RING):
                fetch(k, base + k, tiles_d[base + k:base + k + 1])
            free(0, 1)
            for k in range(RING):
                PE.after(arrived(k, base + k))
                for c in (2 * k, 2 * k + 1):
                    for t in range(TT):
                        mm = nc.tensor.matmul(banks[t][:, :], hT[:, c, t * P:(t + 1) * P],
                                              ring[:, k, (c % 2) * HALF:(c % 2 + 1) * HALF],
                                              start=c == 0, stop=c == DC - 1)
                mm.then_inc(tile_used, 1)
            SE.after(used(base + RING - 1))
            for t in range(TT):
                freed[t] = SE.mark(nc.scalar.copy(v_sb[:, t, :], banks[t][:, :]))
            return freed[t]

        def inverse_rms(src, sq, n_chunks, width, bank, ready, selector=None):
            SE.after(*ready)
            half = n_chunks // 2
            b, bank = bank, banks[bank]
            free(b)
            for a in range(2):
                s = SE.mark(nc.scalar.activation(sq[:, a * half:(a + 1) * half, :],
                                                 src[:, a * half:(a + 1) * half, :], ACT.Square))
                PE.after(s)
                for c in range(a * half, (a + 1) * half):
                    mm = nc.tensor.matmul(bank[:, 0:T], ones, sq[:, c, :], start=c == 0, stop=c == n_chunks - 1)
            summed = PE.mark(mm)
            SE.after(summed)
            root = SE.mark(nc.scalar.activation(rstd[:, :], bank[:, 0:T], ACT.Sqrt, bias=eps_col,
                                                scale=1.0 / width))
            freed[b] = root
            VE.after(root)
            return VE.mark(nc.vector.reciprocal(rstd[:, :], rstd[:, :]))

        def normalise(dst, src, gains, ready, shift=None):
            VE.after(*ready)
            for c in range(DC):
                s = VE.mark(nc.vector.scalar_tensor_tensor(dst[:, c, :], src[:, c, :], gains(c), rstd[:, :],
                                                           ALU.mult, ALU.mult))
            if shift is not None:
                VE.after(s)
                for c in range(DC):
                    s = VE.mark(nc.vector.tensor_scalar(dst[:, c, :], dst[:, c, :], shift(c), None, ALU.add))
            return s

        loaded_cols = load(nc.scalar, "cols", cols[:, :], cols_d)
        loaded_x = load(nc.scalar, "x", xT[:, :, :], x_d)
        loaded_const = load(nc.scalar, "const", const[:, :], const_d)
        for q in (PE, VE, SE, GP):
            q.after(loaded_cols, loaded_const)
        SE.after(loaded_x)
        VE.after(loaded_x)

        with ExitStack() as one:
            c1 = sb("const1", [N_CONST1], one)
            cv = sb("cv", [20, T], one)
            v_sb = sb("v_sb", [TT, HALF], one)
            og = sb("og", [HC, T], one)
            mixT = sb("mixT", [DC, T], one)
            gate_w = sb("gate_w", [DC, 16], one)
            gates = sb("gates", [T], one)
            f1 = sb("f1", [FILTER_HIDDEN], one)
            f23 = sb("f23", [2, FILTER_HIDDEN], one)
            f4 = sb("f4", [4 * HALF], one)
            hid = sb("hid", [T], one)
            turns = sb("turns", [T], one)
            kb = sb("kb", [2, TT, HALF], one)
            kf = sb("kf", [2, TT, HALF], one)

            loaded_c1 = load(nc.scalar, "const1", c1[:, :], const1_d)
            loaded_f1 = load(nc.scalar, "filt_w1", f1[0:FILTER_EMB, :], f1_d)
            loaded_f23 = load(nc.scalar, "filt_w23", f23[0:FILTER_HIDDEN, :, :], f23_d)
            loaded_f4 = load(nc.scalar, "filt_w4", f4[0:FILTER_HIDDEN, :], f4_d)
            loaded_gw = load(nc.scalar, "gate_w", gate_w[:, :, :], gate_w_d)
            for q in (PE, VE):
                q.after(loaded_c1)
            PE.after(loaded_f1, loaded_f23, loaded_f4, loaded_gw)

            def c1v(name, n, rows=P):
                return c1[0:rows, CONST1[name]:CONST1[name] + n]

            window = c1v("window", TT * HALF).rearrange("p (a n) -> p a n", a=TT)
            fwd_cos = c1v("fwd_cos", TT * T).rearrange("p (a n) -> p a n", a=TT)
            fwd_sin = c1v("fwd_sin", TT * T).rearrange("p (a n) -> p a n", a=TT)
            fwd_cos_a = c1v("fwd_cos_a", TT * P).rearrange("p (a n) -> p a n", a=TT)
            fwd_sin_a = c1v("fwd_sin_a", TT * P).rearrange("p (a n) -> p a n", a=TT)
            inv_cos = c1v("inv_cos", TT * T).rearrange("p (a n) -> p a n", a=TT)
            inv_sin = c1v("inv_sin", TT * T).rearrange("p (a n) -> p a n", a=TT)
            dir_mask = c1v("dir_mask", TT * 2 * T).rearrange("p (a d n) -> p a (d n)", a=TT, d=2)

            scratch = sb("scratch", [DC, T], one)
            normed = inverse_rms(xT, scratch, DC, D, 4, [loaded_x])
            h_ready = normalise(hT, xT, lambda c: col("norm_mix_pre", c), [normed])
            PE.after(h_ready)

            def filter_layer(n, lhsT, rhs, ready):
                H = FILTER_HIDDEN
                PE.after(*ready)
                free(5)
                mm = PE.mark(nc.tensor.matmul(banks[5][0:H, 0:T], lhsT, rhs, start=True, stop=True))
                h, w = hid[0:H, :], turns[0:H, :]
                VE.after(mm)
                s = VE.mark(nc.vector.tensor_scalar(h, banks[5][0:H, 0:T], col("filt_b", n, rows=H),
                                                    col("filt_freq", n, rows=H), ALU.add, ALU.mult))
                freed[5] = s
                magic = 1.5 * 2.0**23
                VE.after(s)
                s = VE.mark(nc.vector.tensor_scalar(w, h, 1.0 / (2 * math.pi), magic, ALU.mult, ALU.add))
                VE.after(s)
                s = VE.mark(nc.vector.tensor_scalar(w, w, -magic, None, ALU.add))
                c_1, c_2 = 6.28125, 0.0019350051879882812
                for part in (c_1, c_2, 2 * math.pi - c_1 - c_2):
                    VE.after(s)
                    s = VE.mark(nc.vector.scalar_tensor_tensor(h, w, -part, h, ALU.mult, ALU.add))
                VE.after(s)
                s = VE.mark(nc.vector.tensor_scalar(h, h, 3.1415925, -3.1415925, ALU.min, ALU.max))
                SE.after(s)
                return SE.mark(nc.scalar.activation(h, h, ACT.Sin))

            filt = filter_layer(0, f1[0:FILTER_EMB, :], c1v("emb", T, FILTER_EMB), [])

            for c in range(DC):
                mm = nc.tensor.matmul(banks[6][0:16, 0:T], gate_w[:, c, :], hT[:, c, :], start=c == 0,
                                      stop=c == DC - 1)
            mm = PE.mark(mm)
            SE.after(mm)
            gates_ready = SE.mark(nc.scalar.activation(gates[0:16, :], banks[6][0:16, 0:T], ACT.Identity,
                                                       bias=col("b_gates", rows=16)))

            freed[6] = gates_ready

            class Conv:
                frees = [(VE, 2 * k + 2) for k in range(RING)]

                def __call__(self, k, chunk, psum, done):
                    dst = cv[:, bass.ds(chunk, 1), :]
                    SE.after(done)
                    s = SE.mark(nc.scalar.activation(dst, psum.unsqueeze(1), ACT.Identity,
                                                     bias=col_at("conv_b", chunk), scale=col_at("tap1", chunk)))
                    VE.after(s)
                    right, left = dst[:, :, 1:T], dst[:, :, 0:T - 1]
                    s = VE.mark(nc.vector.scalar_tensor_tensor(right, psum[:, 0:T - 1].unsqueeze(1),
                                                               col_at("tap0", chunk), right, ALU.mult, ALU.add))
                    VE.after(s)
                    return VE.mark(nc.vector.scalar_tensor_tensor(left, psum[:, 1:T].unsqueeze(1),
                                                                  col_at("tap2", chunk), left, ALU.mult, ALU.add))

            convolved = linear("conv", 20, hT, Conv(), [(SE, RING), (VE, 2 * RING)])
            PE.after(*convolved)
            SE.after(*convolved)

            filt = filter_layer(1, f23[0:FILTER_HIDDEN, 0, :], hid[0:FILTER_HIDDEN, :], [filt])

            base = STREAM["ogate"]
            for k in range(RING):
                fetch(k, base + k, tiles_d[base + k:base + k + 1])
                free(k)
                product(banks[k][:, 0:T], k, base + k, chunk_of(hT))
                SE.after(used(base + k))
                og_ready = SE.mark(nc.scalar.activation(og[:, k, :], banks[k][:, 0:T], ACT.Sigmoid))
                freed[k] = og_ready
            qk_ready = SE.mark(nc.scalar.activation(cv[:, 12:20, :], cv[:, 12:20, :], ACT.Silu))

            filt = filter_layer(2, f23[0:FILTER_HIDDEN, 1, :], hid[0:FILTER_HIDDEN, :], [filt])
            PE.after(og_ready)
            v_ready = values("value", v_sb)

            rows = {n: sb(n, [2, T], one) for n in ("lf", "row_a", "csum", "cgate", "peak", "negm")}

            def row(name):
                return rows[name][0:M_HEADS, :, :]

            PE.after(gates_ready)
            free(4, 5)
            for kind in range(4):
                bank = banks[4 + kind % 2]
                mm = nc.tensor.matmul(bank[0:M_HEADS, (kind // 2) * T:(kind // 2 + 1) * T],
                                      const[0:16, CONST["ident"] + 4 * kind:CONST["ident"] + 4 * kind + 4],
                                      gates[0:16, :], start=True, stop=True)
            gates_rows = PE.mark(mm)

            def bank_row(b):
                return banks[b][0:M_HEADS, :].rearrange("p (d t) -> p d t", d=2)

            SE.after(gates_rows)
            s = SE.mark(nc.scalar.activation(row("row_a"), bank_row(5), ACT.Abs))
            SE.after(s)
            s = SE.mark(nc.scalar.activation(row("row_a"), row("row_a"), ACT.Exp, scale=-1.0))
            SE.after(s)
            s = SE.mark(nc.scalar.activation(row("row_a"), row("row_a"), ACT.Ln, bias=1.0))
            VE.after(s)
            s = VE.mark(nc.vector.scalar_tensor_tensor(row("lf"), bank_row(5), 0.0, row("row_a"), ALU.min,
                                                       ALU.subtract))
            freed[5] = s
            VE.after(s)
            scan_ones = cst("scan_ones", T, M_HEADS)

            def along(name, d):
                return rows[name][0:M_HEADS, 0, :] if d == 0 else rows[name][0:M_HEADS, 1, ::-1]

            for d in range(2):
                s = VE.mark(nc.vector.tensor_tensor_scan(along("csum", d), scan_ones, along("lf", d), 0.0,
                                                         ALU.mult, ALU.add))
            VE.after(s)
            s = VE.mark(nc.vector.tensor_tensor(row("cgate"), bank_row(4), row("csum"), ALU.subtract))
            VE.after(s)
            cgate_ready = freed[4] = s
            for d in range(2):
                s = VE.mark(nc.vector.tensor_tensor_scan(along("peak", d), along("cgate", d), along("cgate", d),
                                                         0.0, ALU.max, ALU.max))
            VE.after(s)
            s = VE.mark(nc.vector.scalar_tensor_tensor(row("negm"), row("csum"), -1.0, row("peak"), ALU.mult,
                                                       ALU.subtract))
            VE.after(s)
            rows_ready = VE.mark(nc.vector.tensor_scalar(row("peak"), row("peak"), -1.0, None, ALU.mult))

            PE.after(cgate_ready)
            free(6)
            for d in range(2):
                for t in range(TT):
                    at = (d * TT + t) * M_HEADS
                    mm = nc.tensor.transpose(banks[6][:, at:at + M_HEADS],
                                             rows["cgate"][0:M_HEADS, d, t * P:(t + 1) * P],
                                             const[0:M_HEADS, CONST["ident"]:CONST["ident"] + M_HEADS])
            mm = PE.mark(mm)
            ccol = sb("ccol", [2 * TT * M_HEADS], one)
            VE.after(mm)
            ccol_ready = freed[6] = VE.mark(nc.vector.tensor_copy(ccol[:, :], banks[6][:, 0:2 * TT * M_HEADS]))

            fbias_s = sem("loaded_fbias")
            PE.after(filt)
            for order in range(2):
                for d, dst in ((0, kf), (1, kb)):
                    for t in range(TT):
                        b = 2 * d + t
                        free(b)
                        w = (d * 2 + order) * HALF
                        mm = PE.mark(nc.tensor.matmul(banks[b][:, :], hid[0:FILTER_HIDDEN, t * P:(t + 1) * P],
                                                      f4[0:FILTER_HIDDEN, w:w + HALF], start=True, stop=True))
                        VE.after(mm)
                        s = freed[b] = VE.mark(nc.vector.tensor_tensor(dst[:, order, t, :], banks[b][:, :],
                                                                       window[:, t, :], ALU.mult))
            nc.gpsimd.wait_ge(*s)
            nc.gpsimd.dma_start(kb[0:1, :, 0, :], fbias_d).then_inc(fbias_s, 16)
            VE.after((fbias_s, 16))
            ks = sb("ks", [2, TT, HALF], one)
            s1 = VE.mark(nc.vector.tensor_tensor(ks[:, :, :, :], kf[:, :, :, :], kb[:, :, :, :], ALU.add))
            s2 = VE.mark(nc.vector.tensor_tensor(kf[:, :, :, :], kf[:, :, :, :], kb[:, :, :, :], ALU.subtract))
            PE.after(s2)

            spec_r = [sb(f"spec_r{o}", [TT, HALF], one) for o in range(2)]
            spec_i = [sb(f"spec_i{o}", [TT, HALF], one) for o in range(2)]
            spec_n = [sb(f"spec_n{o}", [HALF], one) for o in range(2)]
            spectra = {}

            def spectrum(dst, matrix, src, b):
                free(b)
                for t in range(TT):
                    mm = nc.tensor.matmul(banks[b][:, :], matrix(t), src(t), start=t == 0, stop=t == TT - 1)
                mm = PE.mark(mm)
                SE.after(mm)
                freed[b] = SE.mark(nc.scalar.copy(dst, banks[b][:, :]))
                return freed[b]

            for o in range(2):
                for f in range(TT):
                    at = slice(f * P, (f + 1) * P)
                    spectrum(spec_r[o][:, f, :], lambda t: fwd_cos[:, t, at], lambda t: ks[:, o, t, :], 0)
                    m = (lambda t: fwd_sin_a[:, t, :]) if f == 0 else (lambda t: fwd_sin[:, t, at])
                    spectrum(spec_i[o][:, f, :], m, lambda t: kf[:, o, t, :], 1)
                spectra[o] = spectrum(spec_n[o][:, :], lambda t: fwd_cos_a[:, t, :], lambda t: ks[:, o, t, :], 2)

            zx = sb("zx", [2, TT, HALF], one)
            for n in range(2):
                for t in range(TT):
                    b = 4 + (2 * n + t) % 2
                    free(b)
                    for c in range(HC):
                        mm = nc.tensor.transpose(banks[b][:, c * P:(c + 1) * P], cv[:, 4 * n + c, t * P:(t + 1) * P],
                                                 ident)
                    mm = PE.mark(mm)
                    SE.after(mm)
                    s = freed[b] = SE.mark(nc.scalar.copy(zx[:, n, t, :], banks[b][:, :]))
            zx_ready = s

            yr = sb("yr", [TT, HALF], one)
            yi = sb("yi", [TT, HALF], one)
            prod = sb("prod", [TT, HALF], one)

            def multiply_spectra(z, order, ready):
                PE.after(*ready)
                free(0, 1, 2, 3)
                done = []
                for f in range(TT):
                    at = slice(f * P, (f + 1) * P)
                    for b, mat in ((2 * f, fwd_cos), (2 * f + 1, fwd_sin)):
                        for t in range(TT):
                            mm = nc.tensor.matmul(banks[b][:, :], mat[:, t, at], z[:, t, :], start=t == 0,
                                                  stop=t == TT - 1)
                    done.append(PE.mark(mm))
                VE.after(spectra[order])
                for f in range(TT):
                    re, im = banks[2 * f][:, :], banks[2 * f + 1][:, :]
                    k_r, k_i = spec_r[order][:, f, :], spec_i[order][:, f, :]
                    k_n = spec_n[order][:, :] if f == 0 else k_r
                    VE.after(done[f])
                    VE.mark(nc.vector.tensor_tensor(yr[:, f, :], re, k_r, ALU.mult))
                    s1 = VE.mark(nc.vector.tensor_tensor(prod[:, f, :], im, k_i, ALU.mult))
                    VE.mark(nc.vector.tensor_tensor(yi[:, f, :], re, k_i, ALU.mult))
                    VE.after(s1)
                    s2 = VE.mark(nc.vector.tensor_tensor(yr[:, f, :], yr[:, f, :], prod[:, f, :], ALU.subtract))
                    freed[2 * f] = s2
                    VE.after(s2)
                    s3 = freed[2 * f + 1] = VE.mark(nc.vector.tensor_tensor(prod[:, f, :], im, k_n, ALU.mult))
                    VE.after(s3)
                    s4 = VE.mark(nc.vector.tensor_tensor(yi[:, f, :], yi[:, f, :], prod[:, f, :], ALU.add))
                return s4

            k_tok = sb("wts", [TT, 2 * T], one)
            guard = sb("guard", [2 * T], one)
            parts = sb("parts", [2 * T], one)
            hm = mixT[:, 0:HC, :]

            def mlstm_head(h):
                scores, peaks, negms, den = banks[4], banks[5], banks[6], banks[7]
                PE.after(qk_ready, rows_ready)
                free(4, 5, 6, 7)
                for t in range(TT):
                    mm = nc.tensor.matmul(scores[:, t * T:(t + 1) * T], cv[:, 16 + h, t * P:(t + 1) * P],
                                          cv[:, 12 + h, :], start=True, stop=True)
                sel = const[0:M_HEADS, CONST["head_rows"] + h * P:CONST["head_rows"] + (h + 1) * P]
                nc.tensor.matmul(peaks[:, :], sel, rows["peak"][0:M_HEADS, :, :], start=True, stop=True)
                mm = PE.mark(nc.tensor.matmul(negms[:, :], sel, rows["negm"][0:M_HEADS, :, :], start=True,
                                              stop=True))
                VE.after(mm, ccol_ready)
                SE.after(mm)
                for t in range(TT):
                    s = freed[5] = VE.mark(nc.vector.tensor_tensor(k_tok[:, t, :], peaks[:, :], dir_mask[:, t, :],
                                                                   ALU.add))
                    SE.after(s)
                    for d in range(2):
                        at = (d * TT + t) * M_HEADS + h
                        e = SE.mark(nc.scalar.activation(k_tok[:, t, d * T:(d + 1) * T],
                                                         k_tok[:, t, d * T:(d + 1) * T], ACT.Exp,
                                                         bias=ccol[:, at:at + 1]))
                    VE.after(e)
                    s = VE.mark(nc.vector.scalar_tensor_tensor(
                        k_tok[:, t, :].rearrange("p (d n) -> p d n", d=2),
                        scores[:, t * T:(t + 1) * T].unsqueeze(1).to_broadcast([P, 2, T]), float(P) ** -0.5,
                        k_tok[:, t, :].rearrange("p (d n) -> p d n", d=2), ALU.mult, ALU.mult))
                g = freed[6] = SE.mark(nc.scalar.activation(guard[:, :], negms[:, :], ACT.Exp))
                PE.after(s)
                for t in range(TT):
                    mm = nc.tensor.matmul(den[:, :], ones, k_tok[:, t, :], start=t == 0, stop=t == TT - 1)
                summed = PE.mark(mm)
                for t in range(TT):
                    mm = nc.tensor.matmul(scores[:, :], v_sb[:, t, h * P:(h + 1) * P], k_tok[:, t, :],
                                          start=t == 0, stop=t == TT - 1)
                nums = PE.mark(mm)
                VE.after(summed, g)
                s = VE.mark(nc.vector.scalar_tensor_tensor(parts[:, :], den[:, :], -1.0, guard[:, :], ALU.mult,
                                                           ALU.max))
                VE.after(s)
                s = VE.mark(nc.vector.tensor_tensor(parts[:, :], den[:, :], parts[:, :], ALU.max))
                VE.after(s)
                freed[7] = s
                s = VE.mark(nc.vector.reciprocal(parts[:, :], parts[:, :]))
                VE.after(s, nums)
                s = freed[4] = VE.mark(nc.vector.tensor_tensor(parts[:, :], scores[:, :], parts[:, :], ALU.mult))
                VE.after(s)
                out = VE.mark(nc.vector.tensor_tensor(hm[:, h, :], parts[:, 0:T], parts[:, T:2 * T], ALU.add))
                return out

            s4 = multiply_spectra(zx[:, 0, :, :], 0, [zx_ready])
            mlstm_head(0)
            PE.after(s4)
            for t in range(TT):
                at = slice(t * P, (t + 1) * P)
                free(t)
                for n, (mat, y) in enumerate(((inv_cos, yr), (inv_sin, yi))):
                    for f in range(TT):
                        mm = nc.tensor.matmul(banks[t][:, :], mat[:, f, at], y[:, f, :], start=n + f == 0,
                                              stop=n + f == TT)
                mm = PE.mark(mm)
                VE.after(mm)
                z_ready = freed[t] = VE.mark(nc.vector.tensor_tensor(zx[:, 0, t, :], banks[t][:, :], zx[:, 1, t, :],
                                                                     ALU.mult))
            mlstm_head(1)
            s4 = multiply_spectra(zx[:, 0, :, :], 1, [z_ready])
            mlstm_head(2)
            PE.after(s4)
            zT = scratch[:, 4:8, :]
            for c in range(HC):
                dst = banks[c][:, 0:T]
                free(c)
                for n, (mat, y) in enumerate(((inv_cos, yr), (inv_sin, yi))):
                    for f in range(TT):
                        mm = nc.tensor.matmul(dst, y[:, f, c * P:(c + 1) * P], mat[:, f, :], start=n + f == 0,
                                              stop=n + f == TT)
                mm = PE.mark(mm)
                VE.after(mm)
                z_ready = freed[c] = VE.mark(nc.vector.tensor_tensor(zT[:, c, :], dst, cv[:, 8 + c, :], ALU.mult))
            mlstm_head(3)
            VE.after(VE.last(), og_ready)
            hm_ready = VE.mark(nc.vector.tensor_tensor(hm[:, :, :], hm[:, :, :], og[:, :, :], ALU.mult))

            sq4 = scratch[:, 0:4, :]

            def group_norm(src, sums, n_group, dst, gain_name, ready, before):
                SE.after(*ready, *before)
                s = SE.mark(nc.scalar.activation(sq4, src, ACT.Square))
                PE.after(s)
                free(0, 1)
                for c in range(HC):
                    mm = nc.tensor.matmul(banks[c // 2][:, (c % 2) * T:(c % 2 + 1) * T], sums, sq4[:, c, :],
                                          start=True, stop=True)
                mm = PE.mark(mm)
                SE.after(mm)
                for b in range(2):
                    s = freed[b] = SE.mark(nc.scalar.activation(sq4[:, 2 * b:2 * b + 2, :],
                                                     banks[b][:, :].rearrange("p (a n) -> p a n", a=2), ACT.Sqrt,
                                                     bias=eps_col, scale=1.0 / n_group))
                VE.after(s)
                s = VE.mark(nc.vector.reciprocal(sq4, sq4))
                VE.after(s)
                for c in range(HC):
                    s = VE.mark(nc.vector.scalar_tensor_tensor(dst(c), src[:, c, :], col(gain_name, c), sq4[:, c, :],
                                                               ALU.mult, ALU.mult))
                return s

            s = group_norm(zT, ones_half, HALF // 8, lambda c: mixT[:, HC + c, :], "hyena_norm", [z_ready], [])
            mix_ready = group_norm(hm, ones, HALF // M_HEADS, lambda c: mixT[:, c, :], "mlstm_norm",
                                   [hm_ready], [s])
            PE.after(mix_ready)

            yT = cv[:, 0:DC, :]

            class Copy:
                frees = [(SE, k + 1) for k in range(RING)]

                def __init__(self, dst):
                    self.dst = dst

                def __call__(self, k, chunk, psum, done):
                    SE.after(done)
                    return SE.mark(nc.scalar.copy(self.dst[:, bass.ds(chunk, 1), :], psum.unsqueeze(1)))

            def residual(y, gains, normed):
                s = normalise(y, y, gains, [normed])
                VE.after(s)
                return VE.mark(nc.vector.tensor_tensor(xT[:, :, :], xT[:, :, :], y[:, :, :], ALU.add))

            (y_ready,) = linear("out", DC, mixT, Copy(yT), [(SE, RING)])
            normed = inverse_rms(yT, scratch, DC, D, 4, [y_ready])
            x_ready = residual(yT, lambda c: col("norm_mix_post", c), normed)

            normed = inverse_rms(xT, scratch, DC, D, 4, [x_ready])
            h_ready = normalise(hT, xT, lambda c: col("norm_mlp_pre", c), [normed])
            PE.after(h_ready)
            mix_done = h_ready
        with ExitStack() as two:
            ff = sb("ff", [FF // P, T], two)
            yT = sb("yT2", [DC, T], two)
            scratch = sb("scratch2", [DC, T], two)
            NQ = N_MOD * D // 4
            ada_w = [sb(f"ada_w{b}", [NQ], two) for b in range(2)]
            acc = sb("acc", [N_MOD * D], two)
            sc = sb("silu_c", [DC], two)
            ada_loaded = [sem(f"ada_loaded{b}") for b in range(2)]
            SE.after(mix_done)
            VE.after(SE.mark(nc.scalar.activation(sc[:, :], col("c", 0, DC), ACT.Silu)))
            VE.after(VE.mark(nc.vector.memset(acc[:, :], 0.0)))
            GP.after(VE.last())

            def ada_step(half, i, nth):
                for b in range(2):
                    q = 2 * half + b
                    nc.gpsimd.wait_ge(*VE.before(nth + b))
                    nc.gpsimd.dma_start(ada_w[b][:, :], ada_d[bass.ds(i, 1), :, q * NQ:(q + 1) * NQ]
                                        .rearrange("a p n -> p (a n)")).then_inc(ada_loaded[b], 16)
                for b in range(2):
                    q = 2 * half + b
                    VE.after((ada_loaded[b], i * 16 + 16 + half * DC * 16))
                    dst = acc[:, q * NQ:(q + 1) * NQ]
                    VE.mark(nc.vector.scalar_tensor_tensor(dst, ada_w[b][:, :], sc[:, bass.ds(i, 1)], dst,
                                                           ALU.mult, ALU.add))

            relu = sb("relu", [RING, T], two)

            class Relu2:
                frees = [(SE, k + 1) for k in range(RING)]

                def __call__(self, k, chunk, psum, done):
                    SE.after(done, VE.before(k + 1))
                    s = SE.mark(nc.scalar.activation(relu[:, k, :], psum, ACT.Relu))
                    VE.after(s)
                    VE.mark(nc.vector.tensor_tensor(ff[:, bass.ds(chunk, 1), :], relu[:, k:k + 1, :],
                                                    relu[:, k:k + 1, :], ALU.mult))
                    if k == RING - 1:
                        i = VE.i
                        VE.after(VE.before(VE.per))
                        ada_step(0, i, RING + 1)
                    return s

            steps = linear("mlp_in", FF // P, hT, Relu2(), [(SE, RING), (VE, RING + 2)])
            PE.after(*steps)
            VE.after(VE.last())

            base = STREAM["mlp_out"]
            free(4)
            with nc.Fori(0, DC) as i:
                SE.enter(i, 1)
                VE.enter(i, 2)
                for k in range(RING):
                    fetch(k, base + i * RING + k, tiles_d[bass.ds(base + i * RING + k, 1)])
                PE.after(SE.before(SE.per))
                for k in range(RING):
                    product(banks[4][:, 0:T], k, base + i * RING + k, lambda c: ff[:, k * DC + c, :],
                            first=k == 0, last=k == RING - 1)
                SE.after(used(base + i * RING + RING - 1))
                SE.mark(nc.scalar.copy(yT[:, bass.ds(i, 1), :], banks[4][:, 0:T].unsqueeze(1)))
                VE.after(VE.before(VE.per))
                ada_step(1, i, 1)
            y_ready = freed[4] = SE.leave(DC)
            acc_ready = VE.leave(DC)
            normed = inverse_rms(yT, scratch, DC, D, 5, [y_ready])
            x_ready = residual(yT, lambda c: col("norm_mlp_post", c), normed)

            PE.after(acc_ready)
            free(6)
            for n in range(N_MOD * DC):
                mm = nc.tensor.matmul(banks[6][:, n:n + 1], acc[:, n * P:(n + 1) * P], ones[:, 0:1], start=True,
                                      stop=True)
            mm = PE.mark(mm)
            VE.after(mm)
            mod_ready = freed[6] = VE.mark(nc.vector.tensor_tensor(mod[:, :], banks[6][:, 0:N_MOD * DC],
                                                        col("b_ada", 0, N_MOD * DC), ALU.add))

            def modulation(n, c):
                return mod[:, n * DC + c:n * DC + c + 1]

            def adaptive(name, scale, shift, ready, sq):
                VE.after(*ready)
                s = VE.mark(nc.vector.scalar_tensor_tensor(gain[:, :], mod[:, scale * DC:(scale + 1) * DC], 1.0,
                                                           col(name, 0, DC), ALU.add, ALU.mult))
                normed = inverse_rms(xT, sq, DC, D, 5, ready)
                return normalise(hT, xT, lambda c: gain[:, c:c + 1], [normed, s], lambda c: modulation(shift, c))

            h_ready = adaptive("norm1", 1, 0, [x_ready, mod_ready], scratch)
            PE.after(h_ready)
            SE.after(h_ready)

        with ExitStack() as three:
            qk = sb("qk", [DC, T], three)
            v_sb = sb("v2_sb", [TT, HALF], three)
            up = sb("up", [HC, PAD + T], three)
            sums = [sb(f"sums{b}", [PAD + T], three) for b in range(2)]
            mixed = sb("mixed", [HC, T], three)
            mixT = sb("mixT2", [DC, T], three)
            scratch = sb("scratch3", [DC, T], three)
            att = sb("att", [ATT_COLS], three)
            poolw = sb("poolw", [HC, P], three)
            probs = sb("probs", [A_HEADS, T], three)
            pT = sb("pT", [TT, A_HEADS, P], three)
            stats = sb("stats", [3, A_HEADS], three)
            GP.after(h_ready, SE.last(), PE.last())
            loaded_att = load(nc.gpsimd, "att", att[:, :], att_d)
            loaded_poolw = load(nc.gpsimd, "poolw", poolw[:, :, :], poolw_d)
            padded = GP.mark(nc.gpsimd.memset(up[:, :, 0:PAD], 0.0))
            for b in range(2):
                padded = GP.mark(nc.gpsimd.memset(sums[b][:, 0:PAD], 0.0))

            class Copy2(object):
                frees = [(SE, k + 1) for k in range(RING)]

                def __init__(self, dst):
                    self.dst = dst

                def __call__(self, k, chunk, psum, done):
                    SE.after(done)
                    return SE.mark(nc.scalar.copy(self.dst[:, bass.ds(chunk, 1), :], psum.unsqueeze(1)))

            (qk_ready,) = linear("qk", DC, hT, Copy2(qk), [(SE, RING)])
            PE.after(qk_ready)
            base = STREAM["pool_in"]
            for k in range(RING):
                free(k)
                fetch(k, base + k, tiles_d[base + k:base + k + 1])
                product(banks[k][:, 0:T], k, base + k, chunk_of(hT))
                SE.after(used(base + k))
                up_ready = freed[k] = SE.mark(nc.scalar.copy(up[:, k, PAD:PAD + T], banks[k][:, 0:T]))
            PE.after(up_ready)
            v_ready = values("value2", v_sb)

            VE.after(up_ready, padded, loaded_att)
            for g in range(HC):
                src = up[:, g, :]
                for n in range(g + 1):
                    dst, w = sums[n % 2], 2**n
                    s = VE.mark(nc.vector.tensor_tensor(dst[:, PAD:PAD + T], src[:, PAD:PAD + T],
                                                        src[:, PAD - w:PAD + T - w], ALU.add))
                    VE.after(s)
                    src = dst[:, :]
                at = COUNT_AT + g * T
                s = VE.mark(nc.vector.tensor_tensor(mixed[:, g, :], src[:, PAD:PAD + T], att[:, at:at + T],
                                                    ALU.mult))
                VE.after(s)
                mixed_ready = VE.mark(nc.vector.tensor_tensor(mixed[:, g, :], mixed[:, g, :],
                                                              up[:, g, PAD:PAD + T], ALU.subtract))
            PE.after(mixed_ready, loaded_poolw)
            for g in range(HC):
                free(g)
                mm = PE.mark(nc.tensor.matmul(banks[g][:, 0:T], poolw[:, g, :], mixed[:, g, :], start=True,
                                              stop=True))
                VE.after(mm)
                pool_ready = freed[g] = VE.mark(nc.vector.tensor_scalar(mixT[:, HC + g, :], banks[g][:, 0:T],
                                                                        col("pool_scale", g), None, ALU.mult))

            PE.after(pool_ready)
            out_banks = (banks[6], banks[7])
            free(6, 7)
            for t in range(TT):
                S = (t + 1) * P
                per_bank = 512 // S
                p = probs[:, :, 0:S]
                bias = att[:, (A_HEADS * P if t else 0):(A_HEADS * P if t else 0) + A_HEADS * S].rearrange(
                    "p (h s) -> p h s", h=A_HEADS)
                for b in range(A_HEADS // per_bank):
                    free(b)
                    for n in range(per_bank):
                        h = HEAD_ORDER[b * per_bank + n]
                        lo = A_DIM * (h % 2)
                        mm = nc.tensor.matmul(banks[b][:, n * S:(n + 1) * S],
                                              qk[lo:lo + A_DIM, h // 2, t * P:(t + 1) * P],
                                              qk[lo:lo + A_DIM, HC + h // 2, 0:S], start=True, stop=True)
                    mm = PE.mark(mm)
                    VE.after(mm)
                    hs = slice(b * per_bank, (b + 1) * per_bank)
                    s = VE.mark(nc.vector.scalar_tensor_tensor(
                        p[:, hs, :], banks[b][:, :].rearrange("p (h s) -> p h s", s=S), A_DIM ** -0.5,
                        bias[:, hs, :], ALU.mult, ALU.add))
                    freed[b] = s
                VE.after(s)
                s = VE.mark(nc.vector.tensor_reduce(stats[:, 0, :], p, AX.X, ALU.max))
                VE.after(s)
                s = VE.mark(nc.vector.tensor_scalar(stats[:, 0, :], stats[:, 0, :], -1.0, None, ALU.mult))
                SE.after(s)
                for h in range(A_HEADS):
                    s = SE.mark(nc.scalar.activation(p[:, h, :], p[:, h, :], ACT.Exp, bias=stats[:, 0, h:h + 1],
                                                     accum_out=stats[:, 1, h:h + 1]))
                VE.after(s)
                s = VE.mark(nc.vector.reciprocal(stats[:, 2, :], stats[:, 1, :]))
                VE.after(s)
                norm = VE.mark(nc.vector.tensor_tensor(p, p, stats[:, 2, :].unsqueeze(2).to_broadcast(
                    [P, A_HEADS, S]), ALU.mult))
                PE.after(norm)
                for k in range(t + 1):
                    for g in range(2):
                        b = 2 * k + g
                        free(b)
                        for n in range(4):
                            mm = nc.tensor.transpose(banks[b][:, n * P:(n + 1) * P],
                                                     p[:, 4 * g + n, k * P:(k + 1) * P], ident)
                        mm = PE.mark(mm)
                        SE.after(mm)
                        freed[b] = SE.mark(nc.scalar.copy(pT[:, k, 4 * g:4 * g + 4, :],
                                                              banks[b][:, :].rearrange("p (h s) -> p h s", h=4)))
                PE.after(freed[2 * t + 1])
                for n, h in enumerate(HEAD_ORDER):
                    lo = A_DIM * (h % 2)
                    bank, at = out_banks[h // 4], (h // 2 % 2) * T + t * P
                    for k in range(t + 1):
                        mm = nc.tensor.matmul(bank[lo:lo + A_DIM, at:at + P],
                                              v_sb[:, k, h * A_DIM:(h + 1) * A_DIM], pT[:, k, n, :],
                                              start=k == 0, stop=k == t)
                att_done = PE.mark(mm)
                SE.after(att_done)
            for b in range(2):
                att_ready = freed[6 + b] = SE.mark(nc.scalar.copy(mixT[:, 2 * b:2 * b + 2, :],
                                                   out_banks[b][:, :].rearrange("p (a n) -> p a n", a=2)))
            PE.after(att_ready)

            class AddGated:
                frees = [(VE, k + 1) for k in range(RING)]

                def __call__(self, k, chunk, psum, done):
                    VE.after(done)
                    dst = xT[:, bass.ds(chunk, 1), :]
                    return VE.mark(nc.vector.scalar_tensor_tensor(dst, psum.unsqueeze(1),
                                                                  mod[:, bass.ds(chunk + 2 * DC, 1)], dst,
                                                                  ALU.mult, ALU.add))

            (x_ready,) = linear("out2", DC, mixT, AddGated(), [(VE, RING)])
            h_ready = adaptive("norm2", 4, 3, [x_ready], scratch)
            PE.after(h_ready)
            SE.after(h_ready)

        acts = sb("acts", [NKEYS, T])
        pq = acts[:, 0:2 * PEER_HEADS, :]
        keys = sb("keys", [2, P])
        slotT = sb("slotT", [3, T + GROUP])
        GP.after(h_ready, SE.last(), PE.last())
        loaded_keys = load(nc.gpsimd, "keys", keys[:, :, :], keys_d)

        class Copy3(object):
            frees = [(SE, k + 1) for k in range(RING)]

            def __call__(self, k, chunk, psum, done):
                SE.after(done)
                return SE.mark(nc.scalar.copy(pq[:, bass.ds(chunk, 1), :], psum.unsqueeze(1)))

        (pq_ready,) = linear("peer_q", 2 * PEER_HEADS, hT, Copy3(), [(SE, RING)])
        PE.after(pq_ready, loaded_keys)

        with ExitStack() as four:
            score = sb("score", [2 * PEER_HEADS, NKEYS], four)
            left = sb("left", [2 * PEER_HEADS, NKEYS], four)
            cand, pairs = score, left
            top_v = sb("top_v", [2 * PEER_HEADS, TOPK], four)
            top_i = sb("top_i", [2 * PEER_HEADS, TOPK], four, U32)
            best2 = sb("best2", [TT, PEER_HEADS, TOPK], four)
            best_i = sb("best_i", [PEER_HEADS, TOPK], four, U32)
            pos_i = sb("pos_i", [PEER_HEADS, TOPK], four, U32)
            key_f = sb("key_f", [2 * PEER_HEADS, TOPK], four)
            pos_f = sb("pos_f", [2, PEER_HEADS, TOPK], four)
            peak = sb("best_peak", [PEER_HEADS], four)
            zsum = sb("zsum", [TT, PEER_HEADS], four)
            slot2 = sb("slot2", [TT, 3, SLOTS], four)

            free(*range(8))
            for t in range(TT):
                for g in range(4):
                    for n in range(4):
                        hp = 4 * g + n
                        mm = nc.tensor.matmul(banks[4 * t + g][:, n * P:(n + 1) * P], pq[:, hp, t * P:(t + 1) * P],
                                              keys[:, hp % 2, :], start=True, stop=True)
                scored = PE.mark(mm)
            second = sb("second", [2 * PEER_HEADS, NKEYS], four)
            SE.after(scored)
            for t, dst in ((0, score), (1, second)):
                for g in range(4):
                    s = freed[4 * t + g] = SE.mark(nc.scalar.copy(
                        dst[:, 4 * g:4 * g + 4, :], banks[4 * t + g][:, :].rearrange("p (h s) -> p h s", h=4)))
            scores_ready = s
            PE.after(scores_ready)

            def activate(first, n):
                base = N_TILES + first
                with nc.Fori(0, n // RING) as i:
                    SE.enter(i, RING)
                    for k in range(RING):
                        fetch(k, base + i * RING + k, u_d[bass.ds(i * RING + first + k, 1)])
                    for k in range(RING):
                        j = base + i * RING + k
                        PE.after(SE.before(k + 1))
                        product(banks[k][:, 0:T], k, j, chunk_of(hT))
                        SE.after(used(j))
                        SE.mark(nc.scalar.activation(acts[:, bass.ds(i * RING + first + k, 1), :],
                                                     banks[k][:, 0:T].unsqueeze(1), ACT.Gelu))
                return SE.leave(n // RING)

            activate(0, BESIDE)

            def top16(n, src, rest, values, indices, ready):
                VE.after(*ready)
                for r in range(n):
                    s = VE.mark(nc.vector.max(values(r, 0), src(r)))
                VE.after(s)
                for r in range(n):
                    VE.mark(nc.vector.max_index(indices(r, 0), values(r, 0), src(r)))
                    s = VE.mark(nc.vector.match_replace(rest(r), values(r, 0), src(r), LOWEST))
                VE.after(s)
                for r in range(n):
                    s = VE.mark(nc.vector.max(values(r, 1), rest(r)))
                VE.after(s)
                for r in range(n):
                    s = VE.mark(nc.vector.max_index(indices(r, 1), values(r, 1), rest(r)))
                return s

            def eight(a):
                return lambda r, half: a[:, r, 8 * half:8 * half + 8]

            for t in range(TT):
                src = score if t == 0 else second
                best_v, slot = best2[:, t, :, :], slot2[:, t, :, :]
                s = top16(2 * PEER_HEADS, lambda r: src[:, r, :], lambda r: left[:, r, :], eight(top_v),
                          eight(top_i), [scores_ready])
                VE.after(s)
                v4 = top_v[:, :, :].rearrange("p (h c) k -> p h c k", c=2)
                cand4 = cand[:, :, :].rearrange("p r k -> p (r k)").rearrange("p (h a b) -> p h a b", a=TOPK, b=TOPK)
                first = v4[:, :, 0, :].unsqueeze(3).to_broadcast([P, PEER_HEADS, TOPK, TOPK])
                other = v4[:, :, 1, :].unsqueeze(2).to_broadcast([P, PEER_HEADS, TOPK, TOPK])
                s = VE.mark(nc.vector.tensor_tensor(cand4, first, other, ALU.add))
                kf_ready = VE.mark(nc.vector.tensor_copy(key_f[:, :, :], top_i[:, :, :]))
                cand_r = cand[:, :, :].rearrange("p r k -> p (r k)").rearrange("p (h n) -> p h n", h=PEER_HEADS)
                left_r = left[:, :, :].rearrange("p r k -> p (r k)").rearrange("p (h n) -> p h n", h=PEER_HEADS)
                s = top16(PEER_HEADS, lambda r: cand_r[:, r, :], lambda r: left_r[:, r, :], eight(best_v),
                          eight(best_i), [s])
                VE.after(s)
                s = VE.mark(nc.vector.tensor_copy(peak[:, :].unsqueeze(2), best_v[:, :, 0:1]))
                VE.after(s)
                s = VE.mark(nc.vector.tensor_tensor(best_v, best_v,
                                                    peak[:, :].unsqueeze(2).to_broadcast([P, PEER_HEADS, TOPK]),
                                                    ALU.subtract))
                for c, (op, n) in enumerate(((ALU.logical_shift_right, 4), (ALU.bitwise_and, TOPK - 1))):
                    s = VE.mark(nc.vector.tensor_single_scalar(pos_i[:, :, :], best_i[:, :, :], n, op))
                    VE.after(s)
                    s = VE.mark(nc.vector.tensor_copy(pos_f[:, c, :, :], pos_i[:, :, :]))
                    VE.after(s)
                VE.after(kf_ready)
                k4 = key_f[:, :, :].rearrange("p (h c) k -> p h c k", c=2)
                pairs4 = left[:, :, :].rearrange("p r k -> p (r k)").rearrange("p (h a b) -> p h a b", a=TOPK,
                                                                              b=TOPK)
                count = iota[:, 0:TOPK].unsqueeze(1).unsqueeze(1).to_broadcast([P, PEER_HEADS, TOPK, TOPK])
                for c in range(2):
                    place = pos_f[:, c, :, :].unsqueeze(3).to_broadcast([P, PEER_HEADS, TOPK, TOPK])
                    table = k4[:, :, c, :].unsqueeze(2).to_broadcast([P, PEER_HEADS, TOPK, TOPK])
                    s = VE.mark(nc.vector.tensor_tensor(pairs4, place, count, ALU.is_equal))
                    VE.after(s)
                    s = VE.mark(nc.vector.tensor_tensor(pairs4, pairs4, table, ALU.mult))
                    VE.after(s)
                    s = VE.mark(nc.vector.tensor_reduce(
                        slot[:, 2 * c, :].rearrange("p (h k) -> p h k", h=PEER_HEADS), pairs4, AX.X, ALU.add))
                    VE.after(s)
            SE.after(s)
            flat = best2[:, :, :, :].rearrange("p t h k -> p (t h) k")
            s = SE.mark(nc.scalar.activation(flat, flat, ACT.Exp))
            VE.after(s)
            zs = zsum[:, :, :].rearrange("p t h -> p (t h)")
            s = VE.mark(nc.vector.tensor_reduce(zs, flat, AX.X, ALU.add))
            VE.after(s)
            s = VE.mark(nc.vector.reciprocal(zs, zs))
            VE.after(s)
            for t in range(TT):
                s = VE.mark(nc.vector.tensor_tensor(
                    slot2[:, t, 1, :].rearrange("p (h k) -> p h k", h=PEER_HEADS), best2[:, t, :, :],
                    zsum[:, t, :].unsqueeze(2).to_broadcast([P, PEER_HEADS, TOPK]), ALU.mult))

            acts_ready = activate(BESIDE, NKEYS - BESIDE)

            PE.after(s)
            for t in range(TT):
                free(4 + t)
                for n in range(3):
                    mm = nc.tensor.transpose(banks[4 + t][:, n * P:(n + 1) * P], slot2[:, t, n, :], ident)
                mm = PE.mark(mm)
                VE.after(mm)
                slots_ready = freed[4 + t] = VE.mark(nc.vector.tensor_copy(
                    slotT[:, :, t * P:(t + 1) * P], banks[4 + t][:, 0:3 * P].rearrange("p (n k) -> p n k", n=3)))

        BODY = 4
        hot1 = [sb(f"hot1_{b}", [GROUP, NKEYS]) for b in range(2)]
        hot2 = [sb(f"hot2_{b}", [GROUP, NKEYS]) for b in range(BODY)]
        now = [sb(f"now{b}", [2, GROUP]) for b in range(2)]

        def gated_rows(b, at, wait_for):
            s = VE.mark(nc.vector.tensor_copy(now[b][:, :, :], slotT[:, 0:2, bass.ds(at, GROUP)]))
            VE.after(s, *wait_for)
            for n in range(GROUP):
                VE.mark(nc.vector.tensor_scalar(hot1[b][:, n, :], iota, now[b][:, 0, n:n + 1],
                                                now[b][:, 1, n:n + 1], ALU.is_equal, ALU.mult))

        GP.after(slots_ready)
        VE.after(slots_ready, acts_ready)
        PE.after(acts_ready)
        free(*range(BODY))
        gated_rows(0, 0, [])
        VE.mark(nc.vector.memset(slotT[:, :, T:T + GROUP], 0.0))
        VE.after(VE.last())
        per = GROUP + 2
        trips = T // (BODY * GROUP)
        with nc.Fori(0, trips) as i:
            PE.enter(i, BODY)
            VE.enter(i, BODY * per)
            GP.enter(i, BODY)
            SE.enter(i, 2 * BODY)
            for b in range(BODY):
                at = i * (BODY * GROUP) + b * GROUP
                made1 = VE.before(BODY * per - 1) if b == 0 else VE.last_at(-1)
                GP.after(PE.before(b + 1))
                diff = GP.mark(nc.gpsimd.tensor_tensor(
                    hot2[b][:, :, :], iota.unsqueeze(1).to_broadcast([P, GROUP, NKEYS]),
                    slotT[:, 2, bass.ds(at, GROUP)].unsqueeze(2).to_broadcast([P, GROUP, NKEYS]), ALU.subtract))
                SE.after(diff)
                SE.after(SE.mark(nc.scalar.activation(hot2[b][:, :, :], hot2[b][:, :, :], ACT.Square)))
                made2 = SE.mark(nc.scalar.activation(hot2[b][:, :, :], hot2[b][:, :, :], ACT.Relu, scale=-1.0,
                                                     bias=1.0))
                PE.after(made1, made2, VE.before((b + 1) * per))
                for n in range(GROUP):
                    mm = nc.tensor.matmul(banks[b][:, n * P:(n + 1) * P], hot2[b][:, n, :], hot1[b % 2][:, n, :],
                                          start=True, stop=True)
                ahead = PE.before(BODY) if b == 0 else PE.last_at()
                multiplied = PE.mark(mm)
                gated_rows((b + 1) % 2, at + GROUP, [ahead])
                VE.after(multiplied)
                dst = acts[:, :, bass.ds(at, GROUP)]
                VE.mark(nc.vector.tensor_tensor(dst, banks[b][:, :].rearrange("p (n e) -> p e n", n=GROUP), dst,
                                                ALU.mult))
        PE.leave(trips)
        gated = VE.leave(trips)
        GP.leave(trips)
        SE.leave(trips)

        PE.after(gated)
        zeros = cst("zeros", HALF)
        for b in range(4):
            nc.tensor.matmul(banks[b][:, :], zeros[:, 0:P], zeros, start=True, stop=False, skip_group_check=True)
        base = N_TILES + NKEYS
        with nc.Fori(0, NKEYS // RING) as i:
            for k in range(RING):
                fetch(k, base + i * RING + k, v_d[bass.ds(i * RING + k, 1)])
            for k in range(RING):
                j = base + i * RING + k
                PE.after(arrived(k, j))
                for c in range(DC):
                    mm = nc.tensor.matmul(banks[c // 2][:, (c % 2) * T:(c % 2 + 1) * T].unsqueeze(1), block(k, c),
                                          acts[:, bass.ds(i * RING + k, 1), :], start=False, stop=False,
                                          skip_group_check=True)
                mm.then_inc(tile_used, 1)
        for b in range(4):
            mm = nc.tensor.matmul(banks[b][:, :], zeros[:, 0:P], zeros, start=False, stop=True,
                                  skip_group_check=True)
        y_done = PE.mark(mm)
        VE.after(y_done)
        for c in range(DC):
            x_ready = VE.mark(nc.vector.scalar_tensor_tensor(
                xT[:, c, :], banks[c // 2][:, (c % 2) * T:(c % 2 + 1) * T], mod[:, 5 * DC + c:5 * DC + c + 1],
                xT[:, c, :], ALU.mult, ALU.add))
        sq = acts[:, 0:DC, :]
        normed = inverse_rms(xT, sq, DC, D, 4, [x_ready])
        out_ready = normalise(hT, xT, lambda c: col("final", c), [normed])
        stored = sem("stored")
        nc.sync.wait_ge(*out_ready)
        nc.sync.dma_start(out_d, hT[:, :, :]).then_inc(stored, 16)
        nc.sync.wait_ge(stored, 16)


def constants():
    def pack(table, n_cols, parts):
        out = np.zeros((P, n_cols), np.float32)
        for name, a in parts.items():
            a = np.asarray(a, np.float64).astype(np.float32)
            out[:a.shape[0], table[name]:table[name] + a.shape[1]] = a
        return out

    lanes = np.arange(P)
    tok = np.arange(T)
    rows = np.zeros((M_HEADS, M_HEADS, P))
    for h in range(M_HEADS):
        rows[h, h] = 1
    const = pack(CONST, N_CONST, {
        "ident": np.eye(P), "ones": np.ones((P, P)), "ones_half": (lanes[:, None] // 64 == lanes // 64) * 1.0,
        "iota": np.tile(lanes, (P, 1)), "eps": np.full((P, 1), EPS), "head_rows": rows.reshape(M_HEADS, -1),
        "scan_ones": np.ones((P, T)),
        "zeros": np.zeros((P, HALF)),
    })

    f32 = np.float32
    bands = (FILTER_EMB - 1) // 2
    t = np.linspace(0.0, 1.0, T, dtype=f32)
    ang = (f32(2.0 * math.pi) * tok.astype(f32) / f32(T))[:, None]
    f = np.linspace(1e-4, bands - 1, bands, dtype=f32)[None, :]
    phase = (f * ang).astype(np.float64)
    emb = np.concatenate([t[:, None], np.cos(phase), -np.sin(phase)], axis=1).T
    deltas = np.linspace(math.log(1e-2) / 1.5, math.log(1e-2) / 0.3, HALF, dtype=f32)
    window = np.exp(-t[:, None].astype(np.float64) * np.abs(deltas))

    def by_tile(a):
        return a.reshape(TT, P, -1).transpose(1, 0, 2).reshape(P, -1)

    theta = 2 * math.pi * ((tok[:, None] * tok[None, :]) % (2 * T)) / (2 * T)
    alt = (-1.0) ** tok
    cos, sin = np.cos(theta), -np.sin(theta)
    sin_nyq, cos_nyq, sin_a = sin.copy(), cos[:, :P].copy(), sin[:, :P].copy()
    sin_nyq[:, 0] = alt
    cos_nyq[:, 0] = alt
    sin_a[:, 0] = 0
    inv_cos, inv_sin = 2 * cos.T / (2 * T), 2 * sin.T / (2 * T)
    inv_cos[0] = 1.0 / (2 * T)
    inv_sin[0] = alt / (2 * T)
    mask = np.zeros((TT, P, 2, T))
    for n in range(TT):
        key = n * P + lanes[:, None]
        mask[n, :, 0] = np.where(key <= tok, 0, NEG)
        mask[n, :, 1] = np.where(key >= tok, 0, NEG)
    const1 = pack(CONST1, N_CONST1, {
        "emb": emb, "window": by_tile(window), "fwd_cos": by_tile(cos), "fwd_sin": by_tile(sin_nyq),
        "fwd_cos_a": by_tile(cos_nyq), "fwd_sin_a": by_tile(sin_a), "inv_cos": by_tile(inv_cos),
        "inv_sin": by_tile(inv_sin), "dir_mask": mask.transpose(1, 0, 2, 3).reshape(P, -1),
    })

    att = []
    for n in range(TT):
        S = (n + 1) * P
        dist = (n * P + lanes[:, None]) - np.arange(S)[None, :]
        times = sum(((dist >= 0) & (dist <= w) & (dist % d == 0)).astype(np.float64) for w, d in BRANCHES)
        kept = np.log(np.maximum(times, 1))
        for h in HEAD_ORDER:
            slope = 2.0 ** (-8.0 * (h + 1) / A_HEADS)
            att.append(np.where(times > 0, kept - slope * dist, NEG))
    counts = np.stack([1.0 / np.minimum(tok + 1, w) for w in WINDOWS])
    att.append(np.tile(counts.reshape(1, -1), (P, 1)))
    return const, const1, np.concatenate(att, axis=1).astype(np.float32)


def kernel(**inputs):
    import concourse.bacc as bacc
    from concourse.bass_utils import run_bass_kernel_spmd

    a = {k: np.asarray(v) for k, v in inputs.items()}

    def by_chunk(w):
        return w.reshape(DC, P, -1, P).transpose(2, 1, 0, 3).reshape(-1, P, TILE)

    def by_rows(w):
        return w.reshape(RING, 2, P, HALF).transpose(0, 2, 1, 3).reshape(RING, P, TILE)

    w = a["w_in"]
    conv = np.r_[1024:1536, 1536:2048, 2048:2560, 0:512, 512:1024]
    w2 = a["w_in_2"][0]
    mlp_out = a["w_mlp_out"].reshape(4, DC, P, DC, P).transpose(3, 0, 2, 1, 4).reshape(-1, P, TILE)
    tiles = np.concatenate([
        by_chunk(w[:, conv]), by_chunk(w[:, 3072:3584]), by_rows(w[:, 2560:3072]), by_chunk(a["w_out"]),
        by_chunk(a["w_mlp_in"]), mlp_out, by_chunk(w2[:, 0:1024]), by_chunk(w2[:, 1536:2048]),
        by_rows(w2[:, 1024:1536]), by_chunk(a["w_out_2"][0]), by_chunk(a["peer_wq_2"][0])])

    cols = np.zeros((P, N_COLS), np.float32)

    def put(name, v, rows=P):
        v = v.reshape(-1, rows).T
        cols[:rows, COLS[name]:COLS[name] + v.shape[1]] = v

    for name, key in (("norm_mix_pre", "norm_mix_pre"), ("norm_mix_post", "norm_mix_post"),
                      ("norm_mlp_pre", "norm_mlp_pre"), ("norm_mlp_post", "norm_mlp_post"),
                      ("mlstm_norm", "mlstm_norm_w"), ("hyena_norm", "hyena_norm_w"), ("norm1", "norm1_g_2"),
                      ("pool_scale", "pool_scale_2"), ("norm2", "norm2_g_2"), ("final", "final_g_2"),
                      ("b_ada", "b_ada_2"), ("c", "c_2")):
        put(name, a[key])
    for n in range(3):
        put(f"tap{n}", a["conv_w"][n, conv])
    put("conv_b", a["conv_b"][conv])
    put("b_gates", a["b_gates"], 16)
    put("filt_b", np.stack([a["filt_b1"], a["filt_b2"], a["filt_b3"]]), FILTER_HIDDEN)
    put("filt_freq", a["filt_freq"], FILTER_HIDDEN)

    const, const1, att = constants()
    arrays = {
        "x": a["x"][0].T.reshape(DC, P, T).transpose(1, 0, 2),
        "tiles": tiles,
        "experts_u": a["peer_u_2"][0].reshape(NKEYS, P, DC, P).transpose(0, 3, 2, 1).reshape(NKEYS, P, TILE),
        "experts_v": a["peer_v_2"][0].reshape(NKEYS, P, TILE),
        "w_ada": a["w_ada_2"][0].reshape(DC, P, N_MOD * D),
        "cols": cols, "const": const, "const1": const1, "att": att,
        "gate_w": w[:, 3584:3600].reshape(DC, P, 16).transpose(1, 0, 2),
        "filt_w1": a["filt_w1"],
        "filt_w23": np.stack([a["filt_w2"], a["filt_w3"]], axis=1),
        "filt_w4": a["filt_w4"],
        "filt_bias": a["filt_bias"].reshape(1, 2, HALF),
        "pool_w": a["pool_w_2"][0].transpose(1, 0, 2),
        "keys": a["peer_subkeys_2"][0].transpose(2, 0, 1),
    }
    arrays = {f"in_{k}": np.ascontiguousarray(v) for k, v in arrays.items()}
    nc = bacc.Bacc("TRN2", target_bir_lowering=False, num_devices=1)
    args = [nc.dram_tensor(k, v.shape, F32, kind="ExternalInput").ap() for k, v in arrays.items()]
    args.append(nc.dram_tensor("out", (P, DC, T), F32, kind="ExternalOutput").ap())
    build(nc, *args)
    result = run_bass_kernel_spmd(nc, [arrays], core_ids=[0]).results[0]["out"]
    return result.transpose(1, 0, 2).reshape(D, T).T.reshape(1, T, D)
```

```python
import math
from contextlib import ExitStack

import numpy as np

import concourse.bass as bass
import concourse.mybir as mybir

P = 128
T = 256
TT = T // P
D = 1024
DC = D // P
FF = 4 * D
HALF = 512
HC = HALF // P
M_HEADS = 4
FILTER_EMB, FILTER_HIDDEN = 33, 64
A_HEADS, A_DIM = 8, 64
HEAD_ORDER = (0, 2, 4, 6, 1, 3, 5, 7)
BRANCHES = ((128, 1), (512, 4), (2048, 16))
WINDOWS = (2, 4, 8, 16)
PAD = 16
PEER_HEADS, NKEYS, TOPK = 8, 128, 16
SLOTS = PEER_HEADS * TOPK
N_MOD = 6
EPS = 1e-6
NEG = -1e30
LOWEST = -3.0e38
BESIDE = 48
GROUP = 4
RING = 4
TILE = D

F32 = mybir.dt.float32
F32R = mybir.dt.float32r
U32 = mybir.dt.uint32
ALU = mybir.AluOpType
ACT = mybir.ActivationFunctionType
AX = mybir.AxisListType

STREAM = {}
_at = 0
for _name, _n in (("conv", 20), ("ogate", 4), ("value", 4), ("out", 8), ("mlp_in", 32), ("mlp_out", 32),
                  ("qk", 8), ("pool_in", 4), ("value2", 4), ("out2", 8), ("peer_q", 16)):
    STREAM[_name] = _at
    _at += _n
N_TILES = _at

COLS = {}
_at = 0
for _name, _n in (("norm_mix_pre", DC), ("norm_mix_post", DC), ("norm_mlp_pre", DC), ("norm_mlp_post", DC),
                  ("tap0", 20), ("tap1", 20), ("tap2", 20), ("conv_b", 20), ("mlstm_norm", HC),
                  ("hyena_norm", HC), ("norm1", DC), ("pool_scale", HC), ("norm2", DC), ("final", DC),
                  ("b_ada", N_MOD * DC), ("c", DC), ("b_gates", 1), ("filt_b", 3), ("filt_freq", 3)):
    COLS[_name] = _at
    _at += _n
N_COLS = _at

CONST = {}
_at = 0
for _name, _n in (("ident", P), ("ones", P), ("ones_half", P), ("iota", P), ("eps", 1), ("zeros", HALF)):
    CONST[_name] = _at
    _at += _n
N_CONST = _at
CONST1 = {}
_at = 0
for _name, _n in (("emb", T), ("window", TT * HALF), ("fwd_cos", TT * T), ("fwd_sin", TT * T),
                  ("fwd_cos_a", TT * P), ("fwd_sin_a", TT * P), ("inv_cos", TT * T), ("inv_sin", TT * T),
                  ("dir_mask", TT * 2 * T), ("head_rows", M_HEADS * P), ("scan_ones", T)):
    CONST1[_name] = _at
    _at += _n
N_CONST1 = _at
COUNT_AT = A_HEADS * P + A_HEADS * T
ATT_COLS = COUNT_AT + HC * T


class Queue:

    def __init__(self, engine, sem):
        self.engine, self.sem, self.n, self.i, self.per = engine, sem, 32, None, 0
        engine.sem_inc(sem, self.n)

    def after(self, *steps):
        for sem, value in steps:
            self.engine.wait_ge(sem, value)

    def mark(self, instruction):
        instruction.then_inc(self.sem, 1)
        self.n += 1
        return (self.sem, self.n if self.i is None else self.n + self.i * self.per)

    def enter(self, i, per):
        self.i, self.per, self.first = i, per, self.n

    def again(self, i):
        self.i, self.n = i, self.first

    def leave(self, trips):
        assert self.n == self.first + self.per, (self.n - self.first, self.per)
        self.n = self.first + trips * self.per
        self.i = None
        return (self.sem, self.n)

    def before(self, nth):
        assert self.first + nth > self.per
        return (self.sem, self.i * self.per + (self.first + nth - self.per))

    def last(self):
        return (self.sem, self.n)

    def last_at(self, back=0):
        return (self.sem, self.i * self.per + (self.n + back))


def build(nc, x_d, tiles_d, u_d, v_d, ada_d, cols_d, const_d, const1_d, att_d, gate_w_d, f1_d, f23_d, f4_d,
          fbias_d, poolw_d, keys_d, out_d):
    ctx = ExitStack()
    with ctx:
        def sem(name):
            return ctx.enter_context(nc.semaphore(name))

        def sb(name, shape, stack=ctx, dt=F32):
            return stack.enter_context(nc.sbuf_tensor(name, [P, *shape], dt))

        PE = Queue(nc.tensor, sem("pe_steps"))
        VE = Queue(nc.vector, sem("vector_steps"))
        SE = Queue(nc.scalar, sem("scalar_steps"))
        GP = Queue(nc.gpsimd, sem("gpsimd_steps"))

        banks = [ctx.enter_context(nc.psum_tensor(f"bank{n}", [P, 512], F32)) for n in range(8)]

        freed = {}

        def free(*numbers):
            PE.after(*(freed[b] for b in numbers if b in freed))

        ring = sb("ring", [RING, TILE])
        cols = sb("cols", [N_COLS])
        const = sb("const", [N_CONST])
        xT = sb("xT", [DC, T])
        h_hi, h_lo = sb("h_hi", [DC, T], dt=F32R), sb("h_lo", [DC, T], dt=F32R)
        w_hi, w_lo = sb("w_hi", [2, TILE], dt=F32R), sb("w_lo", [2, TILE], dt=F32R)
        rstd = sb("rstd", [T])
        mod = sb("mod", [N_MOD * DC])
        gain = sb("gain", [DC])

        def col(name, c=0, n=1, rows=P):
            return cols[0:rows, COLS[name] + c:COLS[name] + c + n]

        def col_at(name, c):
            return cols[:, bass.ds(c + COLS[name], 1)]

        def cst(name, n, rows=P):
            return const[0:rows, CONST[name]:CONST[name] + n]

        ident, ones = cst("ident", P), cst("ones", P)
        ones_half, iota = cst("ones_half", P), cst("iota", P)
        eps_col = cst("eps", 1)

        def load(engine, name, out, in_):
            s = sem("loaded_" + name)
            engine.dma_start(out, in_).then_inc(s, 16)
            return (s, 16)

        tile_loaded = [sem(f"tile_loaded{k}") for k in range(RING)]
        half_used = sem("half_used")
        nc.tensor.sem_inc(half_used, 2 * RING)

        def fetch(k, j, source):
            nc.sync.wait_ge(half_used, 2 * j + 2)
            nc.sync.dma_start(ring[:, k, :], source.rearrange("a p n -> p (a n)")).then_inc(tile_loaded[k], 16)

        def arrived(k, j):
            return (tile_loaded[k], (j - k) * (16 // RING) + 16)

        def used(j, half=1):
            return (half_used, j * 2 + (half + 1 + 2 * RING))

        half_rounded, half_split = sem("half_rounded"), sem("half_split")
        whole = [0]

        def split(k, j, beside=None):
            nc.scalar.wait_ge(*arrived(k, j))
            rest = None
            if beside is not None:
                nc.scalar.wait_ge(*used(j - 2))
                rest = beside()
            for half in range(2):
                at = slice(half * HALF, (half + 1) * HALF)
                nc.scalar.wait_ge(*used(j - 2, half))
                nc.scalar.copy(w_hi[:, k % 2, at], ring[:, k, at]).then_inc(half_rounded, 1)
                nc.vector.wait_ge(half_rounded, (j - whole[0]) * 2 + (half + 1))
                if half == 0 and rest is not None:
                    rest()
                nc.vector.tensor_tensor(w_lo[:, k % 2, at], ring[:, k, at], w_hi[:, k % 2, at],
                                        ALU.subtract).then_inc(half_split, 1)

        def parts_of(j, half):
            return (half_split, (j - whole[0]) * 2 + (half + 1))

        def add_parts(out, weight, moving, start, stop):
            nc.tensor.matmul(out, weight[0], moving[0], start=start, stop=False)
            nc.tensor.matmul(out, weight[0], moving[1], start=False, stop=False)
            return nc.tensor.matmul(out, weight[1], moving[0], start=False, stop=stop)

        def product3(out, k, j, rhs, first=True, last=True):
            for half in range(2):
                PE.after(parts_of(j, half))
                for c in range(half * DC // 2, (half + 1) * DC // 2):
                    at = slice(c * P, (c + 1) * P)
                    mm = add_parts(out, (w_hi[:, k % 2, at], w_lo[:, k % 2, at]), rhs(c), first and c == 0,
                                   last and c == DC - 1)
                mm.then_inc(half_used, 1)

        def block(k, c):
            return ring[:, k, c * P:(c + 1) * P]

        def product(out, k, j, rhs, first=True, last=True):
            PE.after(arrived(k, j))
            for c in range(DC):
                mm = nc.tensor.matmul(out, block(k, c), rhs(c), start=first and c == 0, stop=last and c == DC - 1)
                if c % (DC // 2) == DC // 2 - 1:
                    mm.then_inc(half_used, 1)

        def h_parts(c):
            return h_hi[:, c, :], h_lo[:, c, :]

        def into_parts(src, at, ready):
            SE.after(*ready)
            s = SE.mark(nc.scalar.copy(h_hi[:, at:at + 2, :], src))
            VE.after(s)
            return VE.mark(nc.vector.tensor_tensor(h_lo[:, at:at + 2, :], src, h_hi[:, at:at + 2, :],
                                                   ALU.subtract))

        def linear(name, n, evict, queues, begin=None, last=False):
            trips = n // RING
            base = STREAM[name]
            free(*range(RING))

            def trip(i, follow=True):
                if begin is not None:
                    begin(i)
                for k in range(RING):
                    j = base + i * RING + k
                    fetch(k, j, tiles_d[bass.ds(j, 1)])
                for k in range(RING):
                    j = base + i * RING + k
                    q, nth = evict.frees[k]
                    PE.after(q.before(nth))
                    if follow or k < RING - 1:
                        split((k + 1) % RING, j + 1)
                    product3(banks[k][:, 0:T], k, j, h_parts)
                    evict(k, i * RING + k, banks[k][:, 0:T], used(j))

            with nc.Fori(0, trips - last) as i:
                for q, per in queues:
                    q.enter(i, per)
                trip(i)
            if last:
                for q, per in queues:
                    q.again(trips - 1)
                trip(trips - 1, False)
            steps = [q.leave(trips) for q, _ in queues]
            for k in range(RING):
                freed[k] = evict.frees[k][0].last()
            return steps

        def values(name, v_sb):
            base = STREAM[name]
            for k in range(RING):
                fetch(k, base + k, tiles_d[base + k:base + k + 1])
            free(0, 1)
            for k in range(RING):
                split((k + 1) % RING, base + k + 1)
                for c in (2 * k, 2 * k + 1):
                    PE.after(parts_of(base + k, c % 2))
                    at = slice((c % 2) * HALF, (c % 2 + 1) * HALF)
                    for t in range(TT):
                        tokens = slice(t * P, (t + 1) * P)
                        mm = add_parts(banks[t][:, :], (h_hi[:, c, tokens], h_lo[:, c, tokens]),
                                       (w_hi[:, k % 2, at], w_lo[:, k % 2, at]), c == 0, c == DC - 1)
                    mm.then_inc(half_used, 1)
            SE.after(used(base + RING - 1))
            for t in range(TT):
                freed[t] = SE.mark(nc.scalar.copy(v_sb[:, t, :], banks[t][:, :]))
            return freed[t]

        def inverse_rms(src, sq, n_chunks, width, bank, ready, selector=None):
            SE.after(*ready)
            half = n_chunks // 2
            b, bank = bank, banks[bank]
            free(b)
            for a in range(2):
                s = SE.mark(nc.scalar.activation(sq[:, a * half:(a + 1) * half, :],
                                                 src[:, a * half:(a + 1) * half, :], ACT.Square))
                PE.after(s)
                for c in range(a * half, (a + 1) * half):
                    mm = nc.tensor.matmul(bank[:, 0:T], ones, sq[:, c, :], start=c == 0, stop=c == n_chunks - 1)
            summed = PE.mark(mm)
            SE.after(summed)
            root = SE.mark(nc.scalar.activation(rstd[:, :], bank[:, 0:T], ACT.Sqrt, bias=eps_col,
                                                scale=1.0 / width))
            freed[b] = root
            VE.after(root)
            return VE.mark(nc.vector.reciprocal(rstd[:, :], rstd[:, :]))

        def normalise(dst, src, gains, ready, shift=None):
            VE.after(*ready)
            for c in range(DC):
                s = VE.mark(nc.vector.scalar_tensor_tensor(dst[:, c, :], src[:, c, :], gains(c), rstd[:, :],
                                                           ALU.mult, ALU.mult))
            if shift is not None:
                VE.after(s)
                for c in range(DC):
                    s = VE.mark(nc.vector.tensor_scalar(dst[:, c, :], dst[:, c, :], shift(c), None, ALU.add))
            return s

        def normalise_into_parts(tmp, src, gains, ready, shift=None):
            VE.after(*ready)
            s = rounded = None
            for c in range(0, DC, 2):
                for n in (c, c + 1):
                    s = VE.mark(nc.vector.scalar_tensor_tensor(tmp[:, n, :], src[:, n, :], gains(n), rstd[:, :],
                                                               ALU.mult, ALU.mult))
                if shift is not None:
                    VE.after(s)
                    for n in (c, c + 1):
                        s = VE.mark(nc.vector.tensor_scalar(tmp[:, n, :], tmp[:, n, :], shift(n), None, ALU.add))
                SE.after(s)
                done, rounded = rounded, SE.mark(nc.scalar.copy(h_hi[:, c:c + 2, :], tmp[:, c:c + 2, :]))
                for step, at in ((done, c - 2), (rounded, c) if c == DC - 2 else (None, 0)):
                    if step:
                        VE.after(step)
                        s = VE.mark(nc.vector.tensor_tensor(h_lo[:, at:at + 2, :], tmp[:, at:at + 2, :],
                                                            h_hi[:, at:at + 2, :], ALU.subtract))
            return s

        loaded_cols = load(nc.scalar, "cols", cols[:, :], cols_d)
        loaded_x = load(nc.scalar, "x", xT[:, :, :], x_d)
        loaded_const = load(nc.scalar, "const", const[:, :], const_d)
        for q in (PE, VE, SE, GP):
            q.after(loaded_cols, loaded_const)
        SE.after(loaded_x)
        VE.after(loaded_x)

        with ExitStack() as one:
            c1 = sb("const1", [N_CONST1], one)
            cv = sb("cv", [20, T], one)
            v_sb = sb("v_sb", [TT, HALF], one)
            og = sb("og", [HC, T], one)
            mixT = sb("mixT", [DC, T], one)
            gate_w = sb("gate_w", [DC, 16], one)
            gates = sb("gates", [T], one)
            f1 = sb("f1", [FILTER_HIDDEN], one)
            f23 = sb("f23", [2, FILTER_HIDDEN], one)
            hid = sb("hid", [T], one)
            turns = sb("turns", [T], one)
            kb = sb("kb", [2, TT, HALF], one)
            kf = sb("kf", [2, TT, HALF], one)
            ks = sb("ks", [2, TT, HALF], one)
            f4 = ks[:, :, :, :].rearrange("p a b n -> p (a b n)")

            loaded_c1 = load(nc.scalar, "const1", c1[:, :], const1_d)
            loaded_f1 = load(nc.scalar, "filt_w1", f1[0:FILTER_EMB, :], f1_d)
            loaded_f23 = load(nc.scalar, "filt_w23", f23[0:FILTER_HIDDEN, :, :], f23_d)
            loaded_f4 = load(nc.scalar, "filt_w4", f4[0:FILTER_HIDDEN, :], f4_d)
            loaded_gw = load(nc.scalar, "gate_w", gate_w[:, :, :], gate_w_d)
            for q in (PE, VE):
                q.after(loaded_c1)
            PE.after(loaded_f1, loaded_f23, loaded_f4, loaded_gw)

            def c1v(name, n, rows=P):
                return c1[0:rows, CONST1[name]:CONST1[name] + n]

            window = c1v("window", TT * HALF).rearrange("p (a n) -> p a n", a=TT)
            fwd_cos = c1v("fwd_cos", TT * T).rearrange("p (a n) -> p a n", a=TT)
            fwd_sin = c1v("fwd_sin", TT * T).rearrange("p (a n) -> p a n", a=TT)
            fwd_cos_a = c1v("fwd_cos_a", TT * P).rearrange("p (a n) -> p a n", a=TT)
            fwd_sin_a = c1v("fwd_sin_a", TT * P).rearrange("p (a n) -> p a n", a=TT)
            inv_cos = c1v("inv_cos", TT * T).rearrange("p (a n) -> p a n", a=TT)
            inv_sin = c1v("inv_sin", TT * T).rearrange("p (a n) -> p a n", a=TT)
            dir_mask = c1v("dir_mask", TT * 2 * T).rearrange("p (a d n) -> p a (d n)", a=TT, d=2)

            scratch = sb("scratch", [DC, T], one)
            normed = inverse_rms(xT, scratch, DC, D, 4, [loaded_x])
            split(0, 0)
            h_ready = normalise_into_parts(scratch, xT, lambda c: col("norm_mix_pre", c), [normed])
            PE.after(h_ready)

            def filter_layer(n, lhsT, rhs, ready):
                H = FILTER_HIDDEN
                PE.after(*ready)
                free(5)
                mm = PE.mark(nc.tensor.matmul(banks[5][0:H, 0:T], lhsT, rhs, start=True, stop=True))
                h, w = hid[0:H, :], turns[0:H, :]
                VE.after(mm)
                s = VE.mark(nc.vector.tensor_scalar(h, banks[5][0:H, 0:T], col("filt_b", n, rows=H),
                                                    col("filt_freq", n, rows=H), ALU.add, ALU.mult))
                freed[5] = s
                magic = 1.5 * 2.0**23
                VE.after(s)
                s = VE.mark(nc.vector.tensor_scalar(w, h, 1.0 / (2 * math.pi), magic, ALU.mult, ALU.add))
                VE.after(s)
                s = VE.mark(nc.vector.tensor_scalar(w, w, -magic, None, ALU.add))
                c_1, c_2 = 6.28125, 0.0019350051879882812
                for part in (c_1, c_2, 2 * math.pi - c_1 - c_2):
                    VE.after(s)
                    s = VE.mark(nc.vector.scalar_tensor_tensor(h, w, -part, h, ALU.mult, ALU.add))
                VE.after(s)
                s = VE.mark(nc.vector.tensor_scalar(h, h, 3.1415925, -3.1415925, ALU.min, ALU.max))
                SE.after(s)
                return SE.mark(nc.scalar.activation(h, h, ACT.Sin))

            filt = filter_layer(0, f1[0:FILTER_EMB, :], c1v("emb", T, FILTER_EMB), [])

            for c in range(DC):
                mm = nc.tensor.matmul(banks[6][0:16, 0:T], gate_w[:, c, :], scratch[:, c, :], start=c == 0,
                                      stop=c == DC - 1)
            mm = PE.mark(mm)
            SE.after(mm)
            gates_ready = SE.mark(nc.scalar.activation(gates[0:16, :], banks[6][0:16, 0:T], ACT.Identity,
                                                       bias=col("b_gates", rows=16)))

            freed[6] = gates_ready

            class Conv:
                frees = [(VE, 2 * k + 2) for k in range(RING)]

                def __call__(self, k, chunk, psum, done):
                    dst = cv[:, bass.ds(chunk, 1), :]
                    SE.after(done)
                    s = SE.mark(nc.scalar.activation(dst, psum.unsqueeze(1), ACT.Identity,
                                                     bias=col_at("conv_b", chunk), scale=col_at("tap1", chunk)))
                    VE.after(s)
                    right, left = dst[:, :, 1:T], dst[:, :, 0:T - 1]
                    s = VE.mark(nc.vector.scalar_tensor_tensor(right, psum[:, 0:T - 1].unsqueeze(1),
                                                               col_at("tap0", chunk), right, ALU.mult, ALU.add))
                    VE.after(s)
                    return VE.mark(nc.vector.scalar_tensor_tensor(left, psum[:, 1:T].unsqueeze(1),
                                                                  col_at("tap2", chunk), left, ALU.mult, ALU.add))

            convolved = linear("conv", 20, Conv(), [(SE, RING), (VE, 2 * RING)])
            PE.after(*convolved)
            SE.after(*convolved)

            filt = filter_layer(1, f23[0:FILTER_HIDDEN, 0, :], hid[0:FILTER_HIDDEN, :], [filt])

            base = STREAM["ogate"]
            for k in range(RING):
                fetch(k, base + k, tiles_d[base + k:base + k + 1])
                free(k)
                split((k + 1) % RING, base + k + 1)
                product3(banks[k][:, 0:T], k, base + k, h_parts)
                SE.after(used(base + k))
                og_ready = SE.mark(nc.scalar.activation(og[:, k, :], banks[k][:, 0:T], ACT.Sigmoid))
                freed[k] = og_ready
            qk_ready = SE.mark(nc.scalar.activation(cv[:, 12:20, :], cv[:, 12:20, :], ACT.Silu))

            filt = filter_layer(2, f23[0:FILTER_HIDDEN, 1, :], hid[0:FILTER_HIDDEN, :], [filt])
            PE.after(og_ready)
            v_ready = values("value", v_sb)

            rows = {n: sb(n, [2, T], one) for n in ("lf", "row_a", "csum", "cgate", "peak", "negm")}

            def row(name):
                return rows[name][0:M_HEADS, :, :]

            PE.after(gates_ready)
            free(4, 5)
            for kind in range(4):
                bank = banks[4 + kind % 2]
                mm = nc.tensor.matmul(bank[0:M_HEADS, (kind // 2) * T:(kind // 2 + 1) * T],
                                      const[0:16, CONST["ident"] + 4 * kind:CONST["ident"] + 4 * kind + 4],
                                      gates[0:16, :], start=True, stop=True)
            gates_rows = PE.mark(mm)

            def bank_row(b):
                return banks[b][0:M_HEADS, :].rearrange("p (d t) -> p d t", d=2)

            SE.after(gates_rows)
            s = SE.mark(nc.scalar.activation(row("row_a"), bank_row(5), ACT.Abs))
            SE.after(s)
            s = SE.mark(nc.scalar.activation(row("row_a"), row("row_a"), ACT.Exp, scale=-1.0))
            SE.after(s)
            s = SE.mark(nc.scalar.activation(row("row_a"), row("row_a"), ACT.Ln, bias=1.0))
            VE.after(s)
            s = VE.mark(nc.vector.scalar_tensor_tensor(row("lf"), bank_row(5), 0.0, row("row_a"), ALU.min,
                                                       ALU.subtract))
            freed[5] = s
            VE.after(s)
            scan_ones = c1v("scan_ones", T, M_HEADS)

            def along(name, d):
                return rows[name][0:M_HEADS, 0, :] if d == 0 else rows[name][0:M_HEADS, 1, ::-1]

            for d in range(2):
                s = VE.mark(nc.vector.tensor_tensor_scan(along("csum", d), scan_ones, along("lf", d), 0.0,
                                                         ALU.mult, ALU.add))
            VE.after(s)
            s = VE.mark(nc.vector.tensor_tensor(row("cgate"), bank_row(4), row("csum"), ALU.subtract))
            VE.after(s)
            cgate_ready = freed[4] = s
            for d in range(2):
                s = VE.mark(nc.vector.tensor_tensor_scan(along("peak", d), along("cgate", d), along("cgate", d),
                                                         0.0, ALU.max, ALU.max))
            VE.after(s)
            s = VE.mark(nc.vector.scalar_tensor_tensor(row("negm"), row("csum"), -1.0, row("peak"), ALU.mult,
                                                       ALU.subtract))
            VE.after(s)
            rows_ready = VE.mark(nc.vector.tensor_scalar(row("peak"), row("peak"), -1.0, None, ALU.mult))

            PE.after(cgate_ready)
            free(6)
            for d in range(2):
                for t in range(TT):
                    at = (d * TT + t) * M_HEADS
                    mm = nc.tensor.transpose(banks[6][:, at:at + M_HEADS],
                                             rows["cgate"][0:M_HEADS, d, t * P:(t + 1) * P],
                                             const[0:M_HEADS, CONST["ident"]:CONST["ident"] + M_HEADS])
            mm = PE.mark(mm)
            ccol = sb("ccol", [2 * TT * M_HEADS], one)
            VE.after(mm)
            ccol_ready = freed[6] = VE.mark(nc.vector.tensor_copy(ccol[:, :], banks[6][:, 0:2 * TT * M_HEADS]))

            fbias_s = sem("loaded_fbias")
            PE.after(filt)
            for order in range(2):
                for d, dst in ((0, kf), (1, kb)):
                    for t in range(TT):
                        b = 2 * d + t
                        free(b)
                        w = (d * 2 + order) * HALF
                        mm = PE.mark(nc.tensor.matmul(banks[b][:, :], hid[0:FILTER_HIDDEN, t * P:(t + 1) * P],
                                                      f4[0:FILTER_HIDDEN, w:w + HALF], start=True, stop=True))
                        VE.after(mm)
                        s = freed[b] = VE.mark(nc.vector.tensor_tensor(dst[:, order, t, :], banks[b][:, :],
                                                                       window[:, t, :], ALU.mult))
            nc.gpsimd.wait_ge(*s)
            nc.gpsimd.dma_start(kb[0:1, :, 0, :], fbias_d).then_inc(fbias_s, 16)
            VE.after((fbias_s, 16))
            s1 = VE.mark(nc.vector.tensor_tensor(ks[:, :, :, :], kf[:, :, :, :], kb[:, :, :, :], ALU.add))
            s2 = VE.mark(nc.vector.tensor_tensor(kf[:, :, :, :], kf[:, :, :, :], kb[:, :, :, :], ALU.subtract))
            PE.after(s2)

            spec_r = [sb(f"spec_r{o}", [TT, HALF], one) for o in range(2)]
            spec_i = [sb(f"spec_i{o}", [TT, HALF], one) for o in range(2)]
            spec_n = [sb(f"spec_n{o}", [HALF], one) for o in range(2)]
            spectra = {}

            def spectrum(dst, matrix, src, b):
                free(b)
                for t in range(TT):
                    mm = nc.tensor.matmul(banks[b][:, :], matrix(t), src(t), start=t == 0, stop=t == TT - 1)
                mm = PE.mark(mm)
                SE.after(mm)
                freed[b] = SE.mark(nc.scalar.copy(dst, banks[b][:, :]))
                return freed[b]

            for o in range(2):
                for f in range(TT):
                    at = slice(f * P, (f + 1) * P)
                    spectrum(spec_r[o][:, f, :], lambda t: fwd_cos[:, t, at], lambda t: ks[:, o, t, :], 0)
                    m = (lambda t: fwd_sin_a[:, t, :]) if f == 0 else (lambda t: fwd_sin[:, t, at])
                    spectrum(spec_i[o][:, f, :], m, lambda t: kf[:, o, t, :], 1)
                spectra[o] = spectrum(spec_n[o][:, :], lambda t: fwd_cos_a[:, t, :], lambda t: ks[:, o, t, :], 2)

            zx = kb
            for n in range(2):
                for t in range(TT):
                    b = 4 + (2 * n + t) % 2
                    free(b)
                    for c in range(HC):
                        mm = nc.tensor.transpose(banks[b][:, c * P:(c + 1) * P], cv[:, 4 * n + c, t * P:(t + 1) * P],
                                                 ident)
                    mm = PE.mark(mm)
                    SE.after(mm)
                    s = freed[b] = SE.mark(nc.scalar.copy(zx[:, n, t, :], banks[b][:, :]))
            zx_ready = s

            yr = cv[:, 0:HC, :].rearrange("p (a b) n -> p a (b n)", a=TT)
            yi = cv[:, HC:DC, :].rearrange("p (a b) n -> p a (b n)", a=TT)
            prod = sb("prod", [TT, HALF], one)

            def multiply_spectra(z, order, ready):
                PE.after(*ready)
                free(0, 1, 2, 3)
                done = []
                for f in range(TT):
                    at = slice(f * P, (f + 1) * P)
                    for b, mat in ((2 * f, fwd_cos), (2 * f + 1, fwd_sin)):
                        for t in range(TT):
                            mm = nc.tensor.matmul(banks[b][:, :], mat[:, t, at], z[:, t, :], start=t == 0,
                                                  stop=t == TT - 1)
                    done.append(PE.mark(mm))
                VE.after(spectra[order])
                for f in range(TT):
                    re, im = banks[2 * f][:, :], banks[2 * f + 1][:, :]
                    k_r, k_i = spec_r[order][:, f, :], spec_i[order][:, f, :]
                    k_n = spec_n[order][:, :] if f == 0 else k_r
                    VE.after(done[f])
                    VE.mark(nc.vector.tensor_tensor(yr[:, f, :], re, k_r, ALU.mult))
                    s1 = VE.mark(nc.vector.tensor_tensor(prod[:, f, :], im, k_i, ALU.mult))
                    VE.mark(nc.vector.tensor_tensor(yi[:, f, :], re, k_i, ALU.mult))
                    VE.after(s1)
                    s2 = VE.mark(nc.vector.tensor_tensor(yr[:, f, :], yr[:, f, :], prod[:, f, :], ALU.subtract))
                    freed[2 * f] = s2
                    VE.after(s2)
                    s3 = freed[2 * f + 1] = VE.mark(nc.vector.tensor_tensor(prod[:, f, :], im, k_n, ALU.mult))
                    VE.after(s3)
                    s4 = VE.mark(nc.vector.tensor_tensor(yi[:, f, :], yi[:, f, :], prod[:, f, :], ALU.add))
                return s4

            k_tok = sb("wts", [TT, 2 * T], one)
            guard = sb("guard", [2 * T], one)
            parts = sb("parts", [2 * T], one)
            hm = mixT[:, 0:HC, :]

            def mlstm_head(h):
                scores, peaks, negms, den = banks[4], banks[5], banks[6], banks[7]
                PE.after(qk_ready, rows_ready)
                free(4, 5, 6, 7)
                for t in range(TT):
                    mm = nc.tensor.matmul(scores[:, t * T:(t + 1) * T], cv[:, 16 + h, t * P:(t + 1) * P],
                                          cv[:, 12 + h, :], start=True, stop=True)
                sel = c1v("head_rows", M_HEADS * P, M_HEADS)[:, h * P:(h + 1) * P]
                nc.tensor.matmul(peaks[:, :], sel, rows["peak"][0:M_HEADS, :, :], start=True, stop=True)
                mm = PE.mark(nc.tensor.matmul(negms[:, :], sel, rows["negm"][0:M_HEADS, :, :], start=True,
                                              stop=True))
                VE.after(mm, ccol_ready)
                SE.after(mm)
                for t in range(TT):
                    s = freed[5] = VE.mark(nc.vector.tensor_tensor(k_tok[:, t, :], peaks[:, :], dir_mask[:, t, :],
                                                                   ALU.add))
                    SE.after(s)
                    for d in range(2):
                        at = (d * TT + t) * M_HEADS + h
                        e = SE.mark(nc.scalar.activation(k_tok[:, t, d * T:(d + 1) * T],
                                                         k_tok[:, t, d * T:(d + 1) * T], ACT.Exp,
                                                         bias=ccol[:, at:at + 1]))
                    VE.after(e)
                    s = VE.mark(nc.vector.scalar_tensor_tensor(
                        k_tok[:, t, :].rearrange("p (d n) -> p d n", d=2),
                        scores[:, t * T:(t + 1) * T].unsqueeze(1).to_broadcast([P, 2, T]), float(P) ** -0.5,
                        k_tok[:, t, :].rearrange("p (d n) -> p d n", d=2), ALU.mult, ALU.mult))
                g = freed[6] = SE.mark(nc.scalar.activation(guard[:, :], negms[:, :], ACT.Exp))
                PE.after(s)
                for t in range(TT):
                    mm = nc.tensor.matmul(den[:, :], ones, k_tok[:, t, :], start=t == 0, stop=t == TT - 1)
                summed = PE.mark(mm)
                for t in range(TT):
                    mm = nc.tensor.matmul(scores[:, :], v_sb[:, t, h * P:(h + 1) * P], k_tok[:, t, :],
                                          start=t == 0, stop=t == TT - 1)
                nums = PE.mark(mm)
                VE.after(summed, g)
                s = VE.mark(nc.vector.scalar_tensor_tensor(parts[:, :], den[:, :], -1.0, guard[:, :], ALU.mult,
                                                           ALU.max))
                VE.after(s)
                s = VE.mark(nc.vector.tensor_tensor(parts[:, :], den[:, :], parts[:, :], ALU.max))
                VE.after(s)
                freed[7] = s
                s = VE.mark(nc.vector.reciprocal(parts[:, :], parts[:, :]))
                VE.after(s, nums)
                s = freed[4] = VE.mark(nc.vector.tensor_tensor(parts[:, :], scores[:, :], parts[:, :], ALU.mult))
                VE.after(s)
                out = VE.mark(nc.vector.tensor_tensor(hm[:, h, :], parts[:, 0:T], parts[:, T:2 * T], ALU.add))
                return out

            s4 = multiply_spectra(zx[:, 0, :, :], 0, [zx_ready])
            mlstm_head(0)
            PE.after(s4)
            for t in range(TT):
                at = slice(t * P, (t + 1) * P)
                free(t)
                for n, (mat, y) in enumerate(((inv_cos, yr), (inv_sin, yi))):
                    for f in range(TT):
                        mm = nc.tensor.matmul(banks[t][:, :], mat[:, f, at], y[:, f, :], start=n + f == 0,
                                              stop=n + f == TT)
                mm = PE.mark(mm)
                VE.after(mm)
                z_ready = freed[t] = VE.mark(nc.vector.tensor_tensor(zx[:, 0, t, :], banks[t][:, :], zx[:, 1, t, :],
                                                                     ALU.mult))
            mlstm_head(1)
            s4 = multiply_spectra(zx[:, 0, :, :], 1, [z_ready])
            mlstm_head(2)
            PE.after(s4)
            zT = scratch[:, 4:8, :]
            for c in range(HC):
                dst = banks[c][:, 0:T]
                free(c)
                for n, (mat, y) in enumerate(((inv_cos, yr), (inv_sin, yi))):
                    for f in range(TT):
                        mm = nc.tensor.matmul(dst, y[:, f, c * P:(c + 1) * P], mat[:, f, :], start=n + f == 0,
                                              stop=n + f == TT)
                mm = PE.mark(mm)
                VE.after(mm)
                z_ready = freed[c] = VE.mark(nc.vector.tensor_tensor(zT[:, c, :], dst, cv[:, 8 + c, :], ALU.mult))
            mlstm_head(3)
            VE.after(VE.last(), og_ready)
            hm_ready = VE.mark(nc.vector.tensor_tensor(hm[:, :, :], hm[:, :, :], og[:, :, :], ALU.mult))

            sq4 = scratch[:, 0:4, :]

            def group_norm(src, sums, n_group, dst, gain_name, ready, before):
                SE.after(*ready, *before)
                s = SE.mark(nc.scalar.activation(sq4, src, ACT.Square))
                PE.after(s)
                free(0, 1)
                for c in range(HC):
                    mm = nc.tensor.matmul(banks[c // 2][:, (c % 2) * T:(c % 2 + 1) * T], sums, sq4[:, c, :],
                                          start=True, stop=True)
                mm = PE.mark(mm)
                SE.after(mm)
                for b in range(2):
                    s = freed[b] = SE.mark(nc.scalar.activation(sq4[:, 2 * b:2 * b + 2, :],
                                                     banks[b][:, :].rearrange("p (a n) -> p a n", a=2), ACT.Sqrt,
                                                     bias=eps_col, scale=1.0 / n_group))
                VE.after(s)
                s = VE.mark(nc.vector.reciprocal(sq4, sq4))
                VE.after(s)
                for c in range(HC):
                    s = VE.mark(nc.vector.scalar_tensor_tensor(dst(c), src[:, c, :], col(gain_name, c), sq4[:, c, :],
                                                               ALU.mult, ALU.mult))
                return s

            s = group_norm(zT, ones_half, HALF // 8, lambda c: mixT[:, HC + c, :], "hyena_norm", [z_ready], [])
            for c in (0, 2):
                into_parts(mixT[:, HC + c:HC + c + 2, :], HC + c, [s])
            mix_ready = group_norm(hm, ones, HALF // M_HEADS, lambda c: mixT[:, c, :], "mlstm_norm",
                                   [hm_ready], [s])
            for c in (0, 2):
                mix_ready = into_parts(mixT[:, c:c + 2, :], c, [mix_ready])
            PE.after(mix_ready)

            yT = cv[:, 0:DC, :]

            class Copy:
                frees = [(SE, k + 1) for k in range(RING)]

                def __init__(self, dst):
                    self.dst = dst

                def __call__(self, k, chunk, psum, done):
                    SE.after(done)
                    return SE.mark(nc.scalar.copy(self.dst[:, bass.ds(chunk, 1), :], psum.unsqueeze(1)))

            def residual(y, gains, normed):
                s = normalise(y, y, gains, [normed])
                VE.after(s)
                return VE.mark(nc.vector.tensor_tensor(xT[:, :, :], xT[:, :, :], y[:, :, :], ALU.add))

            (y_ready,) = linear("out", DC, Copy(yT), [(SE, RING)])
            normed = inverse_rms(yT, scratch, DC, D, 4, [y_ready])
            x_ready = residual(yT, lambda c: col("norm_mix_post", c), normed)

            normed = inverse_rms(xT, scratch, DC, D, 4, [x_ready])
            h_ready = normalise_into_parts(scratch, xT, lambda c: col("norm_mlp_pre", c), [normed])
            PE.after(h_ready)
            mix_done = h_ready
        with ExitStack() as two:
            ff_hi, ff_lo = (sb(n, [FF // P, T], two, F32R) for n in ("ff_hi", "ff_lo"))
            yT = sb("yT2", [DC, T], two)
            scratch = sb("scratch2", [DC, T], two)
            NQ = N_MOD * D // 4
            ada_w = [sb(f"ada_w{b}", [NQ], two) for b in range(2)]
            acc = sb("acc", [N_MOD * D], two)
            sc = sb("silu_c", [DC], two)
            ada_loaded = [sem(f"ada_loaded{b}") for b in range(2)]
            SE.after(mix_done)
            VE.after(SE.mark(nc.scalar.activation(sc[:, :], col("c", 0, DC), ACT.Silu)))
            VE.after(VE.mark(nc.vector.memset(acc[:, :], 0.0)))
            GP.after(VE.last())

            def ada_load(half, i):
                for b in range(2):
                    q = 2 * half + b
                    nc.gpsimd.wait_ge(*VE.before(b + 1))
                    nc.gpsimd.dma_start(ada_w[b][:, :], ada_d[bass.ds(i, 1), :, q * NQ:(q + 1) * NQ]
                                        .rearrange("a p n -> p (a n)")).then_inc(ada_loaded[b], 16)

            def ada_add(half, i, b):
                q = 2 * half + b
                VE.after((ada_loaded[b], i * 16 + 16 + half * DC * 16))
                dst = acc[:, q * NQ:(q + 1) * NQ]
                VE.mark(nc.vector.scalar_tensor_tensor(dst, ada_w[b][:, :], sc[:, bass.ds(i, 1)], dst,
                                                       ALU.mult, ALU.add))

            relu = sb("relu", [RING, T], two)
            square = sb("square", [RING, T], two)

            class Relu2:
                frees = [(SE, 2 * k + 1) for k in range(RING)]

                def __call__(self, k, chunk, psum, done):
                    SE.after(done, GP.before(2 * k + 2))
                    s = SE.mark(nc.scalar.activation(relu[:, k, :], psum, ACT.Relu))
                    GP.after(s)
                    squared = GP.mark(nc.gpsimd.tensor_tensor(square[:, k, :], relu[:, k, :], relu[:, k, :],
                                                              ALU.mult))
                    SE.after(s)
                    rounded = SE.mark(nc.scalar.activation(ff_hi[:, bass.ds(chunk, 1), :], relu[:, k:k + 1, :],
                                                           ACT.Square))
                    GP.after(squared, rounded)
                    GP.mark(nc.gpsimd.tensor_tensor(ff_lo[:, bass.ds(chunk, 1), :], square[:, k:k + 1, :],
                                                    ff_hi[:, bass.ds(chunk, 1), :], ALU.subtract))
                    if k % 2:
                        VE.after(VE.before(k // 2 + 1))
                        ada_add(0, VE.i, k // 2)

            steps = linear("mlp_in", FF // P, Relu2(), [(SE, 2 * RING), (VE, 2), (GP, 2 * RING)],
                           lambda i: ada_load(0, i))
            PE.after(*steps)
            VE.after(VE.last())

            base = STREAM["mlp_out"]
            free(4)
            with nc.Fori(0, DC) as i:
                SE.enter(i, 1)
                VE.enter(i, 2)
                for k in range(RING):
                    fetch(k, base + i * RING + k, tiles_d[bass.ds(base + i * RING + k, 1)])
                PE.after(SE.before(SE.per))
                ada_load(1, i)
                for k in range(RING):
                    j = base + i * RING + k
                    split((k + 1) % RING, j + 1)
                    product3(banks[4][:, 0:T], k, j, lambda c: (ff_hi[:, k * DC + c, :], ff_lo[:, k * DC + c, :]),
                             first=k == 0, last=k == RING - 1)
                    if k % 2:
                        VE.after(VE.before(k // 2 + 1))
                        ada_add(1, i, k // 2)
                SE.after(used(base + i * RING + RING - 1))
                SE.mark(nc.scalar.copy(yT[:, bass.ds(i, 1), :], banks[4][:, 0:T].unsqueeze(1)))
            y_ready = freed[4] = SE.leave(DC)
            acc_ready = VE.leave(DC)
            normed = inverse_rms(yT, scratch, DC, D, 5, [y_ready])
            x_ready = residual(yT, lambda c: col("norm_mlp_post", c), normed)

            PE.after(acc_ready)
            free(6)
            for n in range(N_MOD * DC):
                mm = nc.tensor.matmul(banks[6][:, n:n + 1], acc[:, n * P:(n + 1) * P], ones[:, 0:1], start=True,
                                      stop=True)
            mm = PE.mark(mm)
            VE.after(mm)
            mod_ready = freed[6] = VE.mark(nc.vector.tensor_tensor(mod[:, :], banks[6][:, 0:N_MOD * DC],
                                                        col("b_ada", 0, N_MOD * DC), ALU.add))

            def modulation(n, c):
                return mod[:, n * DC + c:n * DC + c + 1]

            def adaptive(name, scale, shift, ready, sq):
                VE.after(*ready)
                s = VE.mark(nc.vector.scalar_tensor_tensor(gain[:, :], mod[:, scale * DC:(scale + 1) * DC], 1.0,
                                                           col(name, 0, DC), ALU.add, ALU.mult))
                normed = inverse_rms(xT, sq, DC, D, 5, ready)
                return normalise_into_parts(sq, xT, lambda c: gain[:, c:c + 1], [normed, s],
                                            lambda c: modulation(shift, c))

            h_ready = adaptive("norm1", 1, 0, [x_ready, mod_ready], scratch)
            PE.after(h_ready)
            SE.after(h_ready)

        with ExitStack() as three:
            qk = sb("qk", [DC, T], three)
            v_sb = sb("v2_sb", [TT, HALF], three)
            up = sb("up", [HC, PAD + T], three)
            sums = [sb(f"sums{b}", [PAD + T], three) for b in range(2)]
            mixed = sb("mixed", [HC, T], three)
            mixT = sb("mixT2", [DC, T], three)
            scratch = sb("scratch3", [DC, T], three)
            att = sb("att", [ATT_COLS], three)
            poolw = sb("poolw", [HC, P], three)
            probs = sb("probs", [A_HEADS, T], three)
            pT = sb("pT", [TT, A_HEADS, P], three)
            stats = sb("stats", [3, A_HEADS], three)
            GP.after(h_ready, SE.last(), PE.last())
            loaded_att = load(nc.gpsimd, "att", att[:, :], att_d)
            loaded_poolw = load(nc.gpsimd, "poolw", poolw[:, :, :], poolw_d)
            padded = GP.mark(nc.gpsimd.memset(up[:, :, 0:PAD], 0.0))
            for b in range(2):
                padded = GP.mark(nc.gpsimd.memset(sums[b][:, 0:PAD], 0.0))

            class Copy2(object):
                frees = [(SE, k + 1) for k in range(RING)]

                def __init__(self, dst):
                    self.dst = dst

                def __call__(self, k, chunk, psum, done):
                    SE.after(done)
                    return SE.mark(nc.scalar.copy(self.dst[:, bass.ds(chunk, 1), :], psum.unsqueeze(1)))

            (qk_ready,) = linear("qk", DC, Copy2(qk), [(SE, RING)])
            PE.after(qk_ready)
            base = STREAM["pool_in"]
            for k in range(RING):
                free(k)
                fetch(k, base + k, tiles_d[base + k:base + k + 1])
                split((k + 1) % RING, base + k + 1)
                product3(banks[k][:, 0:T], k, base + k, h_parts)
                SE.after(used(base + k))
                up_ready = freed[k] = SE.mark(nc.scalar.copy(up[:, k, PAD:PAD + T], banks[k][:, 0:T]))
            PE.after(up_ready)
            v_ready = values("value2", v_sb)

            VE.after(up_ready, padded, loaded_att)
            for g in range(HC):
                src = up[:, g, :]
                for n in range(g + 1):
                    dst, w = sums[n % 2], 2**n
                    s = VE.mark(nc.vector.tensor_tensor(dst[:, PAD:PAD + T], src[:, PAD:PAD + T],
                                                        src[:, PAD - w:PAD + T - w], ALU.add))
                    VE.after(s)
                    src = dst[:, :]
                at = COUNT_AT + g * T
                s = VE.mark(nc.vector.tensor_tensor(mixed[:, g, :], src[:, PAD:PAD + T], att[:, at:at + T],
                                                    ALU.mult))
                VE.after(s)
                mixed_ready = VE.mark(nc.vector.tensor_tensor(mixed[:, g, :], mixed[:, g, :],
                                                              up[:, g, PAD:PAD + T], ALU.subtract))
            PE.after(mixed_ready, loaded_poolw)
            for g in range(HC):
                free(g)
                mm = PE.mark(nc.tensor.matmul(banks[g][:, 0:T], poolw[:, g, :], mixed[:, g, :], start=True,
                                              stop=True))
                VE.after(mm)
                pool_ready = freed[g] = VE.mark(nc.vector.tensor_scalar(mixT[:, HC + g, :], banks[g][:, 0:T],
                                                                        col("pool_scale", g), None, ALU.mult))

            for c in (HC, HC + 2):
                pool_ready = into_parts(mixT[:, c:c + 2, :], c, [pool_ready, v_ready])

            PE.after(pool_ready)
            out_banks = (banks[6], banks[7])
            free(6, 7)
            for t in range(TT):
                S = (t + 1) * P
                per_bank = 512 // S
                p = probs[:, :, 0:S]
                bias = att[:, (A_HEADS * P if t else 0):(A_HEADS * P if t else 0) + A_HEADS * S].rearrange(
                    "p (h s) -> p h s", h=A_HEADS)
                for b in range(A_HEADS // per_bank):
                    free(b)
                    for n in range(per_bank):
                        h = HEAD_ORDER[b * per_bank + n]
                        lo = A_DIM * (h % 2)
                        mm = nc.tensor.matmul(banks[b][:, n * S:(n + 1) * S],
                                              qk[lo:lo + A_DIM, h // 2, t * P:(t + 1) * P],
                                              qk[lo:lo + A_DIM, HC + h // 2, 0:S], start=True, stop=True)
                    mm = PE.mark(mm)
                    VE.after(mm)
                    hs = slice(b * per_bank, (b + 1) * per_bank)
                    s = VE.mark(nc.vector.scalar_tensor_tensor(
                        p[:, hs, :], banks[b][:, :].rearrange("p (h s) -> p h s", s=S), A_DIM ** -0.5,
                        bias[:, hs, :], ALU.mult, ALU.add))
                    freed[b] = s
                VE.after(s)
                s = VE.mark(nc.vector.tensor_reduce(stats[:, 0, :], p, AX.X, ALU.max))
                VE.after(s)
                s = VE.mark(nc.vector.tensor_scalar(stats[:, 0, :], stats[:, 0, :], -1.0, None, ALU.mult))
                SE.after(s)
                for h in range(A_HEADS):
                    s = SE.mark(nc.scalar.activation(p[:, h, :], p[:, h, :], ACT.Exp, bias=stats[:, 0, h:h + 1],
                                                     accum_out=stats[:, 1, h:h + 1]))
                VE.after(s)
                s = VE.mark(nc.vector.reciprocal(stats[:, 2, :], stats[:, 1, :]))
                VE.after(s)
                norm = VE.mark(nc.vector.tensor_tensor(p, p, stats[:, 2, :].unsqueeze(2).to_broadcast(
                    [P, A_HEADS, S]), ALU.mult))
                PE.after(norm)
                for k in range(t + 1):
                    for g in range(2):
                        b = 2 * k + g
                        free(b)
                        for n in range(4):
                            mm = nc.tensor.transpose(banks[b][:, n * P:(n + 1) * P],
                                                     p[:, 4 * g + n, k * P:(k + 1) * P], ident)
                        mm = PE.mark(mm)
                        SE.after(mm)
                        freed[b] = SE.mark(nc.scalar.copy(pT[:, k, 4 * g:4 * g + 4, :],
                                                              banks[b][:, :].rearrange("p (h s) -> p h s", h=4)))
                PE.after(freed[2 * t + 1])
                for n, h in enumerate(HEAD_ORDER):
                    lo = A_DIM * (h % 2)
                    bank, at = out_banks[h // 4], (h // 2 % 2) * T + t * P
                    for k in range(t + 1):
                        mm = nc.tensor.matmul(bank[lo:lo + A_DIM, at:at + P],
                                              v_sb[:, k, h * A_DIM:(h + 1) * A_DIM], pT[:, k, n, :],
                                              start=k == 0, stop=k == t)
                att_done = PE.mark(mm)
                SE.after(att_done)
            for b in range(2):
                att_ready = freed[6 + b] = SE.mark(nc.scalar.copy(mixT[:, 2 * b:2 * b + 2, :],
                                                   out_banks[b][:, :].rearrange("p (a n) -> p a n", a=2)))
                att_ready = into_parts(mixT[:, 2 * b:2 * b + 2, :], 2 * b, [att_ready])
            PE.after(att_ready)

            class AddGated:
                frees = [(VE, k + 1) for k in range(RING)]

                def __call__(self, k, chunk, psum, done):
                    VE.after(done)
                    dst = xT[:, bass.ds(chunk, 1), :]
                    return VE.mark(nc.vector.scalar_tensor_tensor(dst, psum.unsqueeze(1),
                                                                  mod[:, bass.ds(chunk + 2 * DC, 1)], dst,
                                                                  ALU.mult, ALU.add))

            (x_ready,) = linear("out2", DC, AddGated(), [(VE, RING)])
            h_ready = adaptive("norm2", 4, 3, [x_ready], scratch)
            PE.after(h_ready)
            SE.after(h_ready)

        acts = sb("acts", [NKEYS, T])
        pq = acts[:, 0:2 * PEER_HEADS, :]
        keys = sb("keys", [2, P])
        slotT = sb("slotT", [3, T + GROUP])

        def view(at, a, b):
            return acts[:, at:at + DC, :].rearrange("p n t -> p (n t)").rearrange("p (a b) -> p a b", a=a)

        score, second = view(96, 2 * PEER_HEADS, NKEYS), view(104, 2 * PEER_HEADS, NKEYS)
        left = view(112, 2 * PEER_HEADS, NKEYS)
        h_whole = view(120, DC, T)
        GP.after(h_ready, SE.last(), PE.last())
        loaded_keys = load(nc.gpsimd, "keys", keys[:, :, :], keys_d)

        class Copy3(object):
            frees = [(SE, k + 1) for k in range(RING)]

            def __call__(self, k, chunk, psum, done):
                SE.after(done)
                return SE.mark(nc.scalar.copy(pq[:, bass.ds(chunk, 1), :], psum.unsqueeze(1)))

        (pq_ready,) = linear("peer_q", 2 * PEER_HEADS, Copy3(), [(SE, RING)], last=True)
        PE.after(pq_ready, loaded_keys)

        with ExitStack() as four:
            cand, pairs = score, left
            top_v = sb("top_v", [2 * PEER_HEADS, TOPK], four)
            top_i = sb("top_i", [2 * PEER_HEADS, TOPK], four, U32)
            best2 = sb("best2", [TT, PEER_HEADS, TOPK], four)
            best_i = sb("best_i", [PEER_HEADS, TOPK], four, U32)
            pos_i = sb("pos_i", [PEER_HEADS, TOPK], four, U32)
            key_f = sb("key_f", [2 * PEER_HEADS, TOPK], four)
            pos_f = sb("pos_f", [2, PEER_HEADS, TOPK], four)
            peak = sb("best_peak", [PEER_HEADS], four)
            zsum = sb("zsum", [TT, PEER_HEADS], four)
            slot2 = sb("slot2", [TT, 3, SLOTS], four)

            VE.after(pq_ready)
            whole_ready = VE.mark(nc.vector.tensor_tensor(h_whole, h_hi[:, :, :], h_lo[:, :, :], ALU.add))

            free(*range(8))
            for t in range(TT):
                for g in range(4):
                    for n in range(4):
                        hp = 4 * g + n
                        mm = nc.tensor.matmul(banks[4 * t + g][:, n * P:(n + 1) * P], pq[:, hp, t * P:(t + 1) * P],
                                              keys[:, hp % 2, :], start=True, stop=True)
                scored = PE.mark(mm)
            SE.after(scored)
            for t, dst in ((0, score), (1, second)):
                for g in range(4):
                    s = freed[4 * t + g] = SE.mark(nc.scalar.copy(
                        dst[:, 4 * g:4 * g + 4, :], banks[4 * t + g][:, :].rearrange("p (h s) -> p h s", h=4)))
            scores_ready = s
            PE.after(scores_ready, whole_ready)

            def activate(first, n, in_parts):
                base = N_TILES + first
                with nc.Fori(0, n // RING) as i:
                    SE.enter(i, RING)
                    for k in range(RING):
                        fetch(k, base + i * RING + k, u_d[bass.ds(i * RING + first + k, 1)])
                    for k in range(RING):
                        j = base + i * RING + k
                        PE.after(SE.before(k + 1))
                        if in_parts:
                            split((k + 1) % RING, j + 1)
                            product3(banks[k][:, 0:T], k, j, h_parts)
                        else:
                            product(banks[k][:, 0:T], k, j, lambda c: h_whole[:, c, :])
                        SE.after(used(j))
                        SE.mark(nc.scalar.activation(acts[:, bass.ds(i * RING + first + k, 1), :],
                                                     banks[k][:, 0:T].unsqueeze(1), ACT.Gelu))
                return SE.leave(n // RING)

            activate(0, BESIDE, False)
            whole[0] += BESIDE

            def top16(n, src, rest, values, indices, ready):
                VE.after(*ready)
                for r in range(n):
                    s = VE.mark(nc.vector.max(values(r, 0), src(r)))
                VE.after(s)
                for r in range(n):
                    VE.mark(nc.vector.max_index(indices(r, 0), values(r, 0), src(r)))
                    s = VE.mark(nc.vector.match_replace(rest(r), values(r, 0), src(r), LOWEST))
                VE.after(s)
                for r in range(n):
                    s = VE.mark(nc.vector.max(values(r, 1), rest(r)))
                VE.after(s)
                for r in range(n):
                    s = VE.mark(nc.vector.max_index(indices(r, 1), values(r, 1), rest(r)))
                return s

            def eight(a):
                return lambda r, half: a[:, r, 8 * half:8 * half + 8]

            for t in range(TT):
                src = score if t == 0 else second
                best_v, slot = best2[:, t, :, :], slot2[:, t, :, :]
                s = top16(2 * PEER_HEADS, lambda r: src[:, r, :], lambda r: left[:, r, :], eight(top_v),
                          eight(top_i), [scores_ready])
                VE.after(s)
                v4 = top_v[:, :, :].rearrange("p (h c) k -> p h c k", c=2)
                cand4 = cand[:, :, :].rearrange("p r k -> p (r k)").rearrange("p (h a b) -> p h a b", a=TOPK, b=TOPK)
                first = v4[:, :, 0, :].unsqueeze(3).to_broadcast([P, PEER_HEADS, TOPK, TOPK])
                other = v4[:, :, 1, :].unsqueeze(2).to_broadcast([P, PEER_HEADS, TOPK, TOPK])
                s = VE.mark(nc.vector.tensor_tensor(cand4, first, other, ALU.add))
                kf_ready = VE.mark(nc.vector.tensor_copy(key_f[:, :, :], top_i[:, :, :]))
                cand_r = cand[:, :, :].rearrange("p r k -> p (r k)").rearrange("p (h n) -> p h n", h=PEER_HEADS)
                left_r = left[:, :, :].rearrange("p r k -> p (r k)").rearrange("p (h n) -> p h n", h=PEER_HEADS)
                s = top16(PEER_HEADS, lambda r: cand_r[:, r, :], lambda r: left_r[:, r, :], eight(best_v),
                          eight(best_i), [s])
                VE.after(s)
                s = VE.mark(nc.vector.tensor_copy(peak[:, :].unsqueeze(2), best_v[:, :, 0:1]))
                VE.after(s)
                s = VE.mark(nc.vector.tensor_tensor(best_v, best_v,
                                                    peak[:, :].unsqueeze(2).to_broadcast([P, PEER_HEADS, TOPK]),
                                                    ALU.subtract))
                for c, (op, n) in enumerate(((ALU.logical_shift_right, 4), (ALU.bitwise_and, TOPK - 1))):
                    s = VE.mark(nc.vector.tensor_single_scalar(pos_i[:, :, :], best_i[:, :, :], n, op))
                    VE.after(s)
                    s = VE.mark(nc.vector.tensor_copy(pos_f[:, c, :, :], pos_i[:, :, :]))
                    VE.after(s)
                VE.after(kf_ready)
                k4 = key_f[:, :, :].rearrange("p (h c) k -> p h c k", c=2)
                pairs4 = left[:, :, :].rearrange("p r k -> p (r k)").rearrange("p (h a b) -> p h a b", a=TOPK,
                                                                              b=TOPK)
                count = iota[:, 0:TOPK].unsqueeze(1).unsqueeze(1).to_broadcast([P, PEER_HEADS, TOPK, TOPK])
                for c in range(2):
                    place = pos_f[:, c, :, :].unsqueeze(3).to_broadcast([P, PEER_HEADS, TOPK, TOPK])
                    table = k4[:, :, c, :].unsqueeze(2).to_broadcast([P, PEER_HEADS, TOPK, TOPK])
                    s = VE.mark(nc.vector.tensor_tensor(pairs4, place, count, ALU.is_equal))
                    VE.after(s)
                    s = VE.mark(nc.vector.tensor_tensor(pairs4, pairs4, table, ALU.mult))
                    VE.after(s)
                    s = VE.mark(nc.vector.tensor_reduce(
                        slot[:, 2 * c, :].rearrange("p (h k) -> p h k", h=PEER_HEADS), pairs4, AX.X, ALU.add))
                    VE.after(s)
            SE.after(s)
            flat = best2[:, :, :, :].rearrange("p t h k -> p (t h) k")
            s = SE.mark(nc.scalar.activation(flat, flat, ACT.Exp))
            VE.after(s)
            zs = zsum[:, :, :].rearrange("p t h -> p (t h)")
            s = VE.mark(nc.vector.tensor_reduce(zs, flat, AX.X, ALU.add))
            VE.after(s)
            s = VE.mark(nc.vector.reciprocal(zs, zs))
            VE.after(s)
            for t in range(TT):
                s = VE.mark(nc.vector.tensor_tensor(
                    slot2[:, t, 1, :].rearrange("p (h k) -> p h k", h=PEER_HEADS), best2[:, t, :, :],
                    zsum[:, t, :].unsqueeze(2).to_broadcast([P, PEER_HEADS, TOPK]), ALU.mult))

            split(0, N_TILES + BESIDE)
            acts_ready = activate(BESIDE, NKEYS - BESIDE, True)

            PE.after(s)
            for t in range(TT):
                free(4 + t)
                for n in range(3):
                    mm = nc.tensor.transpose(banks[4 + t][:, n * P:(n + 1) * P], slot2[:, t, n, :], ident)
                mm = PE.mark(mm)
                VE.after(mm)
                slots_ready = freed[4 + t] = VE.mark(nc.vector.tensor_copy(
                    slotT[:, :, t * P:(t + 1) * P], banks[4 + t][:, 0:3 * P].rearrange("p (n k) -> p n k", n=3)))

        BODY = 4
        five = ctx.enter_context(ExitStack())
        hot1 = [sb(f"hot1_{b}", [GROUP, NKEYS], five) for b in range(2)]
        hot2 = [sb(f"hot2_{b}", [GROUP, NKEYS], five) for b in range(BODY)]
        now = [sb(f"now{b}", [2, GROUP], five) for b in range(2)]

        def gated_rows(b, at, wait_for):
            s = VE.mark(nc.vector.tensor_copy(now[b][:, :, :], slotT[:, 0:2, bass.ds(at, GROUP)]))
            VE.after(s, *wait_for)
            for n in range(GROUP):
                VE.mark(nc.vector.tensor_scalar(hot1[b][:, n, :], iota, now[b][:, 0, n:n + 1],
                                                now[b][:, 1, n:n + 1], ALU.is_equal, ALU.mult))

        GP.after(slots_ready)
        VE.after(slots_ready, acts_ready)
        PE.after(acts_ready)
        free(*range(BODY))
        gated_rows(0, 0, [])
        VE.mark(nc.vector.memset(slotT[:, :, T:T + GROUP], 0.0))
        VE.after(VE.last())
        per = GROUP + 2
        trips = T // (BODY * GROUP)
        with nc.Fori(0, trips) as i:
            PE.enter(i, BODY)
            VE.enter(i, BODY * per)
            GP.enter(i, BODY)
            SE.enter(i, 2 * BODY)
            for b in range(BODY):
                at = i * (BODY * GROUP) + b * GROUP
                made1 = VE.before(BODY * per - 1) if b == 0 else VE.last_at(-1)
                GP.after(PE.before(b + 1))
                diff = GP.mark(nc.gpsimd.tensor_tensor(
                    hot2[b][:, :, :], iota.unsqueeze(1).to_broadcast([P, GROUP, NKEYS]),
                    slotT[:, 2, bass.ds(at, GROUP)].unsqueeze(2).to_broadcast([P, GROUP, NKEYS]), ALU.subtract))
                SE.after(diff)
                SE.after(SE.mark(nc.scalar.activation(hot2[b][:, :, :], hot2[b][:, :, :], ACT.Square)))
                made2 = SE.mark(nc.scalar.activation(hot2[b][:, :, :], hot2[b][:, :, :], ACT.Relu, scale=-1.0,
                                                     bias=1.0))
                PE.after(made1, made2, VE.before((b + 1) * per))
                for n in range(GROUP):
                    mm = nc.tensor.matmul(banks[b][:, n * P:(n + 1) * P], hot2[b][:, n, :], hot1[b % 2][:, n, :],
                                          start=True, stop=True)
                ahead = PE.before(BODY) if b == 0 else PE.last_at()
                multiplied = PE.mark(mm)
                gated_rows((b + 1) % 2, at + GROUP, [ahead])
                VE.after(multiplied)
                dst = acts[:, :, bass.ds(at, GROUP)]
                VE.mark(nc.vector.tensor_tensor(dst, banks[b][:, :].rearrange("p (n e) -> p e n", n=GROUP), dst,
                                                ALU.mult))
        PE.leave(trips)
        gated = VE.leave(trips)
        GP.leave(trips)
        SE.leave(trips)

        PE.after(gated)
        zeros = cst("zeros", HALF)
        for b in range(4):
            nc.tensor.matmul(banks[b][:, :], zeros[:, 0:P], zeros, start=True, stop=False, skip_group_check=True)
        base = N_TILES + NKEYS
        five.close()
        g_hi, g_lo = sb("g_hi", [2, T], dt=F32R), sb("g_lo", [2, T], dt=F32R)

        def split_acts(k, n):
            src = acts[:, bass.ds(n, 1), :]
            b = slice(k % 2, k % 2 + 1)
            nc.scalar.copy(g_hi[:, b, :], src)
            return lambda: nc.vector.tensor_tensor(g_lo[:, b, :], src, g_hi[:, b, :], ALU.subtract)

        SE.after(gated)
        VE.after(SE.mark(nc.scalar.copy(g_hi[:, 0:1, :], acts[:, 0:1, :])))
        PE.after(VE.mark(nc.vector.tensor_tensor(g_lo[:, 0:1, :], acts[:, 0:1, :], g_hi[:, 0:1, :], ALU.subtract)))

        def add_experts(i, follow=True):
            for k in range(RING):
                fetch(k, base + i * RING + k, v_d[bass.ds(i * RING + k, 1)])
            for k in range(RING):
                j = base + i * RING + k
                if follow or k < RING - 1:
                    split((k + 1) % RING, j + 1, lambda: split_acts(k + 1, i * RING + k + 1))
                product_of_half_banks(k, j, (g_hi[:, k % 2, :], g_lo[:, k % 2, :]))

        def product_of_half_banks(k, j, gates):
            for half in range(2):
                PE.after(parts_of(j, half))
                for c in range(half * DC // 2, (half + 1) * DC // 2):
                    at = slice(c * P, (c + 1) * P)
                    out = banks[c // 2][:, (c % 2) * T:(c % 2 + 1) * T]
                    for w, g in ((w_hi, gates[0]), (w_hi, gates[1]), (w_lo, gates[0])):
                        mm = nc.tensor.matmul(out, w[:, k % 2, at], g, start=False, stop=False,
                                              skip_group_check=True)
                mm.then_inc(half_used, 1)

        with nc.Fori(0, NKEYS // RING - 1) as i:
            add_experts(i)
        add_experts(NKEYS // RING - 1, False)
        for b in range(4):
            mm = nc.tensor.matmul(banks[b][:, :], zeros[:, 0:P], zeros, start=False, stop=True,
                                  skip_group_check=True)
        y_done = PE.mark(mm)
        VE.after(y_done)
        for c in range(DC):
            x_ready = VE.mark(nc.vector.scalar_tensor_tensor(
                xT[:, c, :], banks[c // 2][:, (c % 2) * T:(c % 2 + 1) * T], mod[:, 5 * DC + c:5 * DC + c + 1],
                xT[:, c, :], ALU.mult, ALU.add))
        sq = acts[:, 0:DC, :]
        normed = inverse_rms(xT, sq, DC, D, 4, [x_ready])
        outT = acts[:, DC:2 * DC, :]
        out_ready = normalise(outT, xT, lambda c: col("final", c), [normed])
        stored = sem("stored")
        nc.sync.wait_ge(*out_ready)
        nc.sync.dma_start(out_d, outT).then_inc(stored, 16)
        nc.sync.wait_ge(stored, 16)


def constants():
    def pack(table, n_cols, parts):
        out = np.zeros((P, n_cols), np.float32)
        for name, a in parts.items():
            a = np.asarray(a, np.float64).astype(np.float32)
            out[:a.shape[0], table[name]:table[name] + a.shape[1]] = a
        return out

    lanes = np.arange(P)
    tok = np.arange(T)
    rows = np.zeros((M_HEADS, M_HEADS, P))
    for h in range(M_HEADS):
        rows[h, h] = 1
    const = pack(CONST, N_CONST, {
        "ident": np.eye(P), "ones": np.ones((P, P)), "ones_half": (lanes[:, None] // 64 == lanes // 64) * 1.0,
        "iota": np.tile(lanes, (P, 1)), "eps": np.full((P, 1), EPS),
        "zeros": np.zeros((P, HALF)),
    })

    f32 = np.float32
    bands = (FILTER_EMB - 1) // 2
    t = np.linspace(0.0, 1.0, T, dtype=f32)
    ang = (f32(2.0 * math.pi) * tok.astype(f32) / f32(T))[:, None]
    f = np.linspace(1e-4, bands - 1, bands, dtype=f32)[None, :]
    phase = (f * ang).astype(np.float64)
    emb = np.concatenate([t[:, None], np.cos(phase), -np.sin(phase)], axis=1).T
    deltas = np.linspace(math.log(1e-2) / 1.5, math.log(1e-2) / 0.3, HALF, dtype=f32)
    window = np.exp(-t[:, None].astype(np.float64) * np.abs(deltas))

    def by_tile(a):
        return a.reshape(TT, P, -1).transpose(1, 0, 2).reshape(P, -1)

    theta = 2 * math.pi * ((tok[:, None] * tok[None, :]) % (2 * T)) / (2 * T)
    alt = (-1.0) ** tok
    cos, sin = np.cos(theta), -np.sin(theta)
    sin_nyq, cos_nyq, sin_a = sin.copy(), cos[:, :P].copy(), sin[:, :P].copy()
    sin_nyq[:, 0] = alt
    cos_nyq[:, 0] = alt
    sin_a[:, 0] = 0
    inv_cos, inv_sin = 2 * cos.T / (2 * T), 2 * sin.T / (2 * T)
    inv_cos[0] = 1.0 / (2 * T)
    inv_sin[0] = alt / (2 * T)
    mask = np.zeros((TT, P, 2, T))
    for n in range(TT):
        key = n * P + lanes[:, None]
        mask[n, :, 0] = np.where(key <= tok, 0, NEG)
        mask[n, :, 1] = np.where(key >= tok, 0, NEG)
    const1 = pack(CONST1, N_CONST1, {
        "emb": emb, "window": by_tile(window), "fwd_cos": by_tile(cos), "fwd_sin": by_tile(sin_nyq),
        "fwd_cos_a": by_tile(cos_nyq), "fwd_sin_a": by_tile(sin_a), "inv_cos": by_tile(inv_cos),
        "inv_sin": by_tile(inv_sin), "dir_mask": mask.transpose(1, 0, 2, 3).reshape(P, -1),
        "head_rows": rows.reshape(M_HEADS, -1), "scan_ones": np.ones((P, T)),
    })

    att = []
    for n in range(TT):
        S = (n + 1) * P
        dist = (n * P + lanes[:, None]) - np.arange(S)[None, :]
        times = sum(((dist >= 0) & (dist <= w) & (dist % d == 0)).astype(np.float64) for w, d in BRANCHES)
        kept = np.log(np.maximum(times, 1))
        for h in HEAD_ORDER:
            slope = 2.0 ** (-8.0 * (h + 1) / A_HEADS)
            att.append(np.where(times > 0, kept - slope * dist, NEG))
    counts = np.stack([1.0 / np.minimum(tok + 1, w) for w in WINDOWS])
    att.append(np.tile(counts.reshape(1, -1), (P, 1)))
    return const, const1, np.concatenate(att, axis=1).astype(np.float32)


def kernel(**inputs):
    import concourse.bacc as bacc
    from concourse.bass_utils import run_bass_kernel_spmd

    a = {k: np.asarray(v) for k, v in inputs.items()}

    def by_chunk(w):
        return w.reshape(DC, P, -1, P).transpose(2, 1, 0, 3).reshape(-1, P, TILE)

    def by_rows(w):
        return w.reshape(RING, 2, P, HALF).transpose(0, 2, 1, 3).reshape(RING, P, TILE)

    w = a["w_in"]
    conv = np.r_[1024:1536, 1536:2048, 2048:2560, 0:512, 512:1024]
    w2 = a["w_in_2"][0]
    mlp_out = a["w_mlp_out"].reshape(4, DC, P, DC, P).transpose(3, 0, 2, 1, 4).reshape(-1, P, TILE)
    tiles = np.concatenate([
        by_chunk(w[:, conv]), by_chunk(w[:, 3072:3584]), by_rows(w[:, 2560:3072]), by_chunk(a["w_out"]),
        by_chunk(a["w_mlp_in"]), mlp_out, by_chunk(w2[:, 0:1024]), by_chunk(w2[:, 1536:2048]),
        by_rows(w2[:, 1024:1536]), by_chunk(a["w_out_2"][0]), by_chunk(a["peer_wq_2"][0])])

    cols = np.zeros((P, N_COLS), np.float32)

    def put(name, v, rows=P):
        v = v.reshape(-1, rows).T
        cols[:rows, COLS[name]:COLS[name] + v.shape[1]] = v

    for name, key in (("norm_mix_pre", "norm_mix_pre"), ("norm_mix_post", "norm_mix_post"),
                      ("norm_mlp_pre", "norm_mlp_pre"), ("norm_mlp_post", "norm_mlp_post"),
                      ("mlstm_norm", "mlstm_norm_w"), ("hyena_norm", "hyena_norm_w"), ("norm1", "norm1_g_2"),
                      ("pool_scale", "pool_scale_2"), ("norm2", "norm2_g_2"), ("final", "final_g_2"),
                      ("b_ada", "b_ada_2"), ("c", "c_2")):
        put(name, a[key])
    for n in range(3):
        put(f"tap{n}", a["conv_w"][n, conv])
    put("conv_b", a["conv_b"][conv])
    put("b_gates", a["b_gates"], 16)
    put("filt_b", np.stack([a["filt_b1"], a["filt_b2"], a["filt_b3"]]), FILTER_HIDDEN)
    put("filt_freq", a["filt_freq"], FILTER_HIDDEN)

    const, const1, att = constants()
    arrays = {
        "x": a["x"][0].T.reshape(DC, P, T).transpose(1, 0, 2),
        "tiles": tiles,
        "experts_u": a["peer_u_2"][0].reshape(NKEYS, P, DC, P).transpose(0, 3, 2, 1).reshape(NKEYS, P, TILE),
        "experts_v": a["peer_v_2"][0].reshape(NKEYS, P, TILE),
        "w_ada": a["w_ada_2"][0].reshape(DC, P, N_MOD * D),
        "cols": cols, "const": const, "const1": const1, "att": att,
        "gate_w": w[:, 3584:3600].reshape(DC, P, 16).transpose(1, 0, 2),
        "filt_w1": a["filt_w1"],
        "filt_w23": np.stack([a["filt_w2"], a["filt_w3"]], axis=1),
        "filt_w4": a["filt_w4"],
        "filt_bias": a["filt_bias"].reshape(1, 2, HALF),
        "pool_w": a["pool_w_2"][0].transpose(1, 0, 2),
        "keys": a["peer_subkeys_2"][0].transpose(2, 0, 1),
    }
    arrays = {f"in_{k}": np.ascontiguousarray(v) for k, v in arrays.items()}
    nc = bacc.Bacc("TRN2", target_bir_lowering=False, num_devices=1)
    args = [nc.dram_tensor(k, v.shape, F32, kind="ExternalInput").ap() for k, v in arrays.items()]
    args.append(nc.dram_tensor("out", (P, DC, T), F32, kind="ExternalOutput").ap())
    build(nc, *args)
    result = run_bass_kernel_spmd(nc, [arrays], core_ids=[0]).results[0]["out"]
    return result.transpose(1, 0, 2).reshape(D, T).T.reshape(1, T, D)
```

```python
import math
from contextlib import ExitStack

import numpy as np

import concourse.bass as bass
import concourse.mybir as mybir

P = 128
T = 256
TT = T // P
D = 1024
DC = D // P
FF = 4 * D
HALF = 512
HC = HALF // P
M_HEADS = 4
FILTER_EMB, FILTER_HIDDEN = 33, 64
A_HEADS, A_DIM = 8, 64
HEAD_ORDER = (0, 2, 4, 6, 1, 3, 5, 7)
BRANCHES = ((128, 1), (512, 4), (2048, 16))
WINDOWS = (2, 4, 8, 16)
PAD = 16
PEER_HEADS, NKEYS, TOPK = 8, 128, 16
SLOTS = PEER_HEADS * TOPK
GROUPS = 8
N_MOD = 6
EPS = 1e-6
NEG = -1e30
LOWEST = -3.0e38
BESIDE = 28
GROUP = 4
RING = 4
TILE = D

F32 = mybir.dt.float32
F32R = mybir.dt.float32r
U32 = mybir.dt.uint32
ALU = mybir.AluOpType
ACT = mybir.ActivationFunctionType
AX = mybir.AxisListType

STREAM = {}
_at = 0
for _name, _n in (("conv", 20), ("value", 4), ("ogate", 4), ("out", 8), ("mlp_in", 32), ("mlp_out", 32),
                  ("qk", 8), ("pool_in", 4), ("value2", 4), ("out2", 8), ("peer_q", 16)):
    STREAM[_name] = _at
    _at += _n
N_TILES = _at

COLS = {}
_at = 0
for _name, _n in (("norm_mix_pre", DC), ("norm_mix_post", DC), ("norm_mlp_pre", DC), ("norm_mlp_post", DC),
                  ("tap0", 20), ("tap1", 20), ("tap2", 20), ("conv_b", 20), ("mlstm_norm", HC),
                  ("hyena_norm", HC), ("norm1", DC), ("pool_scale", HC), ("norm2", DC), ("final", DC),
                  ("b_ada", N_MOD * DC), ("c", DC), ("b_gates", 1), ("filt_b", 3), ("filt_freq", 3)):
    COLS[_name] = _at
    _at += _n
N_COLS = _at

CONST = {}
_at = 0
for _name, _n in (("ident", P), ("ones", P), ("iota", P), ("eps", 1), ("zeros", HALF)):
    CONST[_name] = _at
    _at += _n
N_CONST = _at
CONST1 = {}
_at = 0
for _name, _n in (("emb", T), ("window", TT * HALF), ("fwd_cos", TT * T), ("fwd_sin", TT * T),
                  ("fwd_cos_a", TT * P), ("fwd_sin_a", TT * P), ("inv_cos", TT * T), ("inv_sin", TT * T),
                  ("dir_mask", TT * 2 * T), ("head_rows", M_HEADS * P),
                  ("head_sums", HC * GROUPS), ("group_sums", HC * GROUPS), ("group_rows", HC * P)):
    CONST1[_name] = _at
    _at += _n
N_CONST1 = _at
COUNT_AT = A_HEADS * P + A_HEADS * T
ATT_COLS = COUNT_AT + HC * T


class Queue:

    def __init__(self, engine, sem):
        self.engine, self.sem, self.n, self.i, self.per = engine, sem, 32, None, 0
        engine.sem_inc(sem, self.n)

    def after(self, *steps):
        for sem, value in steps:
            self.engine.wait_ge(sem, value)

    def mark(self, instruction):
        instruction.then_inc(self.sem, 1)
        self.n += 1
        return (self.sem, self.n if self.i is None else self.n + self.i * self.per)

    def enter(self, i, per):
        self.i, self.per, self.first = i, per, self.n

    def again(self, i):
        self.i, self.n = i, self.first

    def leave(self, trips):
        assert self.n == self.first + self.per, (self.n - self.first, self.per)
        self.n = self.first + trips * self.per
        self.i = None
        return (self.sem, self.n)

    def before(self, nth):
        assert self.first + nth > self.per
        return (self.sem, self.i * self.per + (self.first + nth - self.per))

    def last(self):
        return (self.sem, self.n)

    def here(self, nth):
        return (self.sem, self.i * self.per + (self.first + nth))

    def last_at(self, back=0):
        return (self.sem, self.i * self.per + (self.n + back))


def build(nc, x_d, tiles_d, u_d, v_d, ada_d, cols_d, const_d, const1_d, att_d, gate_w_d, f1_d, f23_d, f4_d,
          fbias_d, poolw_d, keys_d, out_d):
    ctx = ExitStack()
    with ctx:
        def sem(name):
            return ctx.enter_context(nc.semaphore(name))

        def sb(name, shape, stack=ctx, dt=F32):
            return stack.enter_context(nc.sbuf_tensor(name, [P, *shape], dt))

        PE = Queue(nc.tensor, sem("pe_steps"))
        VE = Queue(nc.vector, sem("vector_steps"))
        SE = Queue(nc.scalar, sem("scalar_steps"))
        GP = Queue(nc.gpsimd, sem("gpsimd_steps"))

        banks = [ctx.enter_context(nc.psum_tensor(f"bank{n}", [P, 512], F32)) for n in range(8)]

        freed = {}

        def free(*numbers):
            PE.after(*(freed[b] for b in numbers if b in freed))

        ring = sb("ring", [RING, TILE])
        cols = sb("cols", [N_COLS])
        const = sb("const", [N_CONST])
        xT = sb("xT", [DC, T])
        h_hi, h_lo = sb("h_hi", [DC, T], dt=F32R), sb("h_lo", [DC, T], dt=F32R)
        w_hi, w_lo = sb("w_hi", [2, TILE], dt=F32R), sb("w_lo", [2, TILE], dt=F32R)
        rstd = sb("rstd", [T])
        mod = sb("mod", [N_MOD * DC])
        gain = sb("gain", [DC])
        table_out = sb("table_out", [8])
        before_peer = ctx.enter_context(ExitStack())
        sumsq = sb("sumsq", [T], before_peer)
        square = sb("square", [RING, T], before_peer)

        def col(name, c=0, n=1, rows=P):
            return cols[0:rows, COLS[name] + c:COLS[name] + c + n]

        def col_at(name, c):
            return cols[:, bass.ds(c + COLS[name], 1)]

        def cst(name, n, rows=P):
            return const[0:rows, CONST[name]:CONST[name] + n]

        ident, ones = cst("ident", P), cst("ones", P)
        iota = cst("iota", P)
        eps_col = cst("eps", 1)

        def load(engine, name, out, in_):
            s = sem("loaded_" + name)
            engine.dma_start(out, in_).then_inc(s, 16)
            return (s, 16)

        tables = [0]

        def load_table(function):
            n = tables[0]
            tables[0] += 1
            SE.mark(nc.scalar.activation(table_out[:, n:n + 1], eps_col, function))

        tile_loaded = [sem(f"tile_loaded{k}") for k in range(RING)]
        half_used = sem("half_used")
        nc.tensor.sem_inc(half_used, 2 * RING)

        def fetch(k, j, source):
            nc.sync.wait_ge(half_used, 2 * j + 2)
            nc.sync.dma_start(ring[:, k, :], source.rearrange("a p n -> p (a n)")).then_inc(tile_loaded[k], 16)

        def arrived(k, j):
            return (tile_loaded[k], (j - k) * (16 // RING) + 16)

        def used(j, half=1):
            return (half_used, j * 2 + (half + 1 + 2 * RING))

        half_rounded, half_split = sem("half_rounded"), sem("half_split")
        whole = [0]

        def split(k, j, beside=None):
            nc.scalar.wait_ge(*arrived(k, j))
            rest = None
            if beside is not None:
                nc.scalar.wait_ge(*used(j - 2))
                rest = beside()
            for half in range(2):
                at = slice(half * HALF, (half + 1) * HALF)
                nc.scalar.wait_ge(*used(j - 2, half))
                nc.scalar.copy(w_hi[:, k % 2, at], ring[:, k, at]).then_inc(half_rounded, 1)
                nc.vector.wait_ge(half_rounded, (j - whole[0]) * 2 + (half + 1))
                if half == 0 and rest is not None:
                    rest()
                nc.vector.tensor_tensor(w_lo[:, k % 2, at], ring[:, k, at], w_hi[:, k % 2, at],
                                        ALU.subtract).then_inc(half_split, 1)

        def parts_of(j, half):
            return (half_split, (j - whole[0]) * 2 + (half + 1))

        def add_parts(out, weight, moving, start, stop):
            nc.tensor.matmul(out, weight[0], moving[0], start=start, stop=False)
            nc.tensor.matmul(out, weight[0], moving[1], start=False, stop=False)
            return nc.tensor.matmul(out, weight[1], moving[0], start=False, stop=stop)

        def product3(out, k, j, rhs, first=True, last=True, inputs=None):
            for half in range(2):
                PE.after(parts_of(j, half), *(inputs[half:half + 1] if inputs else ()))
                for c in range(half * DC // 2, (half + 1) * DC // 2):
                    at = slice(c * P, (c + 1) * P)
                    mm = add_parts(out, (w_hi[:, k % 2, at], w_lo[:, k % 2, at]), rhs(c), first and c == 0,
                                   last and c == DC - 1)
                mm.then_inc(half_used, 1)

        def block(k, c):
            return ring[:, k, c * P:(c + 1) * P]

        def product(out, k, j, rhs, first=True, last=True):
            PE.after(arrived(k, j))
            for c in range(DC):
                mm = nc.tensor.matmul(out, block(k, c), rhs(c), start=first and c == 0, stop=last and c == DC - 1)
                if c % (DC // 2) == DC // 2 - 1:
                    mm.then_inc(half_used, 1)

        def h_parts(c):
            return h_hi[:, c, :], h_lo[:, c, :]

        def into_parts(src, at, ready):
            SE.after(*ready)
            s = SE.mark(nc.scalar.copy(h_hi[:, at:at + 2, :], src))
            VE.after(s)
            return VE.mark(nc.vector.tensor_tensor(h_lo[:, at:at + 2, :], src, h_hi[:, at:at + 2, :],
                                                   ALU.subtract))

        def linear(name, n, evict, queues, beside=None, last=False, inputs=None):
            trips = n // RING
            base = STREAM[name]
            free(*range(RING))

            def trip(i, follow=True):
                for k in range(RING):
                    j = base + i * RING + k
                    fetch(k, j, tiles_d[bass.ds(j, 1)])
                    if beside is not None and k:
                        beside(i, k - 1)
                if beside is not None:
                    beside(i, RING - 1)
                for k in range(RING):
                    j = base + i * RING + k
                    q, nth = evict.frees[k]
                    PE.after(q.before(nth))
                    if follow or k < RING - 1:
                        split((k + 1) % RING, j + 1)
                    product3(banks[k][:, 0:T], k, j, h_parts, inputs=inputs)
                    evict(k, i * RING + k, banks[k][:, 0:T], used(j))

            with nc.Fori(0, trips - last) as i:
                for q, per in queues:
                    q.enter(i, per)
                trip(i)
            if last:
                for q, per in queues:
                    q.again(trips - 1)
                trip(trips - 1, False)
            steps = [q.leave(trips) for q, _ in queues]
            for k in range(RING):
                freed[k] = evict.frees[k][0].last()
            return steps

        class Evict:

            def __init__(self, dst, squares):
                self.dst, self.squares, self.steps = dst, squares, 2 if squares else 1
                self.frees = [(SE, self.steps * (k + 1)) for k in range(RING)]

            def __call__(self, k, chunk, psum, done):
                SE.after(done)
                SE.mark(nc.scalar.copy(self.dst[:, bass.ds(chunk, 1), :], psum.unsqueeze(1)))
                if self.squares:
                    add_square(k, psum)

        def copied_layer(name, n, dst, squares=False, last=False, inputs=None):
            evict = Evict(dst, squares)
            queues = [(SE, evict.steps * RING)] + ([(GP, RING)] if squares else [])
            return linear(name, n, evict, queues, last=last, inputs=inputs)

        def values(name, v_sb, scale=None):
            base = STREAM[name]
            for k in range(RING):
                fetch(k, base + k, tiles_d[base + k:base + k + 1])
            free(0, 1)
            for k in range(RING):
                split((k + 1) % RING, base + k + 1)
                for c in (2 * k, 2 * k + 1):
                    PE.after(parts_of(base + k, c % 2))
                    at = slice((c % 2) * HALF, (c % 2 + 1) * HALF)
                    for t in range(TT):
                        tokens = slice(t * P, (t + 1) * P)
                        mm = add_parts(banks[t][:, :], (h_hi[:, c, tokens], h_lo[:, c, tokens]),
                                       (w_hi[:, k % 2, at], w_lo[:, k % 2, at]), c == 0, c == DC - 1)
                    mm.then_inc(half_used, 1)
                if k < RING - 1:
                    yield None
            SE.after(used(base + RING - 1))
            for t in range(TT):
                factor = 1.0 if scale is None else scale[:, t:t + 1]
                freed[t] = SE.mark(nc.scalar.activation(v_sb[:, t, :], banks[t][:, :], ACT.Copy, scale=factor))
            yield freed[t]

        def inverse_root(summed, bank):
            SE.after(summed)
            root = freed[bank] = SE.mark(nc.scalar.activation(rstd[:, :], banks[bank][:, 0:T], ACT.Sqrt,
                                                              bias=eps_col, scale=1.0 / D))
            VE.after(root)
            return VE.mark(nc.vector.reciprocal(rstd[:, :], rstd[:, :]))

        def inverse_rms(bank, ready):
            PE.after(ready)
            free(bank)
            return inverse_root(PE.mark(nc.tensor.matmul(banks[bank][:, 0:T], ones, sumsq[:, :], start=True,
                                                         stop=True)), bank)

        def add_square(k, chunk):
            SE.after(GP.before(k + 1))
            s = SE.mark(nc.scalar.activation(square[:, k, :], chunk, ACT.Square))
            GP.after(s, GP.last_at() if k else GP.before(GP.per))
            GP.mark(nc.gpsimd.tensor_tensor(sumsq[:, :], sumsq[:, :], square[:, k, :], ALU.add))

        def clear_sumsq():
            GP.after(GP.mark(nc.gpsimd.memset(sumsq[:, :], 0.0)))

        squared = {}

        def chunk_square(src, c, bank, ready, square=square):
            SE.after(ready)
            if c >= RING:
                SE.after(squared[c - RING])
            if c == 0:
                free(bank)
            PE.after(SE.mark(nc.scalar.activation(square[:, c % RING, :], src[:, c, :], ACT.Square)))
            squared[c] = PE.mark(nc.tensor.matmul(banks[bank][:, 0:T], ones, square[:, c % RING, :],
                                                  start=c == 0, stop=c == DC - 1))
            return squared[c]

        def part_chunk(src, c, gain, ready, shift=None):
            SE.after(ready)
            rounded = SE.mark(nc.scalar.activation(h_hi[:, c, :], src[:, c, :], ACT.Identity,
                                                   scale=gain, bias=0.0 if shift is None else shift))
            VE.after(rounded)
            if shift is None:
                rest = nc.vector.scalar_tensor_tensor(h_lo[:, c, :], src[:, c, :], gain, h_hi[:, c, :], ALU.mult,
                                                      ALU.subtract)
            else:
                rest = nc.vector.scalar_tensor_tensor(h_lo[:, c, :], src[:, c, :], shift, h_hi[:, c, :], ALU.add,
                                                      ALU.subtract)
            return VE.mark(rest)

        def residual_chunk(y, c, gain):
            GP.after(VE.mark(nc.vector.scalar_tensor_tensor(y[:, c, :], y[:, c, :], gain, rstd[:, :], ALU.mult,
                                                            ALU.mult)))
            return GP.mark(nc.gpsimd.tensor_tensor(xT[:, c, :], xT[:, c, :], y[:, c, :], ALU.add))

        def adaptive_parts(tmp, normed, shift):
            VE.after(normed)
            products, steps = [], []
            for c in range(DC + 1):
                if c < DC:
                    products.append(VE.mark(nc.vector.scalar_tensor_tensor(
                        tmp[:, c, :], xT[:, c, :], gain[:, c:c + 1], rstd[:, :], ALU.mult, ALU.mult)))
                if c:
                    steps.append(part_chunk(tmp, c - 1, 1.0, products[c - 1], modulation(shift, c - 1)))
            return [steps[DC // 2 - 1], steps[DC - 1]]

        def modulation(n, c):
            return mod[:, n * DC + c:n * DC + c + 1]

        def adaptive_gain(name, scale):
            return VE.mark(nc.vector.scalar_tensor_tensor(gain[:, :], mod[:, scale * DC:(scale + 1) * DC], 1.0,
                                                          col(name, 0, DC), ALU.add, ALU.mult))

        loaded_x = load(nc.sync, "x", xT[:, :, :], x_d)
        loaded_const = load(nc.scalar, "const", const[:, :], const_d)
        loaded_cols = load(nc.scalar, "cols", cols[:, :], cols_d)
        nc.sync.wait_ge(*loaded_x)
        for q in (SE, PE, VE, GP):
            q.after(loaded_cols, loaded_const, loaded_x)
        load_table(ACT.Sqrt)

        with ExitStack() as one:
            c1 = sb("const1", [N_CONST1], one)
            cv_room = sb("cv", [1 + 20, T], one)
            cv = cv_room[:, 1:1 + 20, :]
            v_sb = sb("v_sb", [TT, HALF], one)
            og = sb("og", [HC, T], one)
            mixT = sb("mixT", [DC, T], one)
            gate_w = sb("gate_w", [DC, 16], one)
            gates = sb("gates", [T], one)
            f1 = sb("f1", [FILTER_HIDDEN], one)
            f23 = sb("f23", [2, FILTER_HIDDEN], one)
            hid = sb("hid", [T], one)
            turns = sb("turns", [T], one)
            kb = sb("kb", [2, TT, HALF], one)
            kf = sb("kf", [2, TT, HALF], one)
            ks = sb("ks", [2, TT, HALF], one)
            f4 = ks[:, :, :, :].rearrange("p a b n -> p (a b n)")

            loaded_c1 = load(nc.scalar, "const1", c1[:, :], const1_d)
            loaded_f1 = load(nc.scalar, "filt_w1", f1[0:FILTER_EMB, :], f1_d)
            loaded_f23 = load(nc.scalar, "filt_w23", f23[0:FILTER_HIDDEN, :, :], f23_d)
            loaded_f4 = load(nc.scalar, "filt_w4", f4[0:FILTER_HIDDEN, :], f4_d)
            loaded_gw = load(nc.scalar, "gate_w", gate_w[:, :, :], gate_w_d)

            def c1v(name, n, rows=P):
                return c1[0:rows, CONST1[name]:CONST1[name] + n]

            window = c1v("window", TT * HALF).rearrange("p (a n) -> p a n", a=TT)
            fwd_cos = c1v("fwd_cos", TT * T).rearrange("p (a n) -> p a n", a=TT)
            fwd_sin = c1v("fwd_sin", TT * T).rearrange("p (a n) -> p a n", a=TT)
            fwd_cos_a = c1v("fwd_cos_a", TT * P).rearrange("p (a n) -> p a n", a=TT)
            fwd_sin_a = c1v("fwd_sin_a", TT * P).rearrange("p (a n) -> p a n", a=TT)
            inv_cos = c1v("inv_cos", TT * T).rearrange("p (a n) -> p a n", a=TT)
            inv_sin = c1v("inv_sin", TT * T).rearrange("p (a n) -> p a n", a=TT)
            dir_mask = c1v("dir_mask", TT * 2 * T).rearrange("p (a d n) -> p a (d n)", a=TT, d=2)

            scratch = sb("scratch", [DC, T], one)
            for n in range(2):
                at = slice(n * RING, (n + 1) * RING)
                s = SE.mark(nc.scalar.activation(scratch[:, at, :], xT[:, at, :], ACT.Square))
            VE.after(s)
            for n in (4, 2):
                VE.after(VE.mark(nc.vector.tensor_tensor(scratch[:, 0:n, :], scratch[:, 0:n, :],
                                                         scratch[:, n:2 * n, :], ALU.add)))
            s = VE.mark(nc.vector.tensor_tensor(sumsq[:, :], scratch[:, 0, :], scratch[:, 1, :], ALU.add))
            steps = [part_chunk(xT, c, col("norm_mix_pre", c), loaded_x) for c in range(DC)]
            h_ready = [steps[DC // 2 - 1], steps[DC - 1]]
            split(0, 0)
            GP.after(h_ready[1])
            whole_ready = GP.mark(nc.gpsimd.tensor_tensor(scratch[:, :, :], h_hi[:, :, :], h_lo[:, :, :], ALU.add))
            normed = inverse_rms(4, s)
            VE.after(normed)

            def filter_layer(n, lhsT, rhs, ready):
                H = FILTER_HIDDEN
                PE.after(*ready)
                free(5)
                mm = PE.mark(nc.tensor.matmul(banks[5][0:H, 0:T], lhsT, rhs, start=True, stop=True))
                h, w = hid[0:H, :], turns[0:H, :]
                VE.after(mm)
                s = VE.mark(nc.vector.tensor_scalar(h, banks[5][0:H, 0:T], col("filt_b", n, rows=H),
                                                    col("filt_freq", n, rows=H), ALU.add, ALU.mult))
                freed[5] = s
                magic = 1.5 * 2.0**23
                VE.after(s)
                s = VE.mark(nc.vector.tensor_scalar(w, h, 1.0 / (2 * math.pi), magic, ALU.mult, ALU.add))
                VE.after(s)
                s = VE.mark(nc.vector.tensor_scalar(w, w, -magic, None, ALU.add))
                c_1, c_2 = 6.28125, 0.0019350051879882812
                for part in (c_1, c_2, 2 * math.pi - c_1 - c_2):
                    VE.after(s)
                    s = VE.mark(nc.vector.scalar_tensor_tensor(h, w, -part, h, ALU.mult, ALU.add))
                VE.after(s)
                s = VE.mark(nc.vector.tensor_scalar(h, h, 3.1415925, -3.1415925, ALU.min, ALU.max))
                SE.after(s)
                return SE.mark(nc.scalar.activation(h, h, ACT.Sin))

            def input_gates():
                PE.after(whole_ready, loaded_gw)
                free(6)
                for c in range(DC):
                    mm = nc.tensor.matmul(banks[6][0:16, 0:T], gate_w[:, c, :], scratch[:, c, :], start=c == 0,
                                        stop=c == DC - 1)
                VE.after(PE.mark(mm))
                s = freed[6] = VE.mark(nc.vector.tensor_tensor(gates[0:16, :], banks[6][0:16, 0:T], rstd[0:16, :],
                                                               ALU.mult))
                SE.after(s)
                return SE.mark(nc.scalar.activation(gates[0:16, :], gates[0:16, :], ACT.Identity,
                                                    bias=col("b_gates", rows=16)))

            scaled = square

            def taps(k, at, ready):
                dst, z = cv_room[:, bass.ds(at, 1), :], scaled[:, k:k + 1, :]
                SE.after(ready)
                s = SE.mark(nc.scalar.activation(dst, z, ACT.Identity, bias=col_at("conv_b", at - 1),
                                                 scale=col_at("tap1", at - 1)))
                VE.after(s)
                right, left = dst[:, :, 1:T], dst[:, :, 0:T - 1]
                s = VE.mark(nc.vector.scalar_tensor_tensor(right, z[:, :, 0:T - 1], col_at("tap0", at - 1), right,
                                                           ALU.mult, ALU.add))
                VE.after(s)
                return VE.mark(nc.vector.scalar_tensor_tensor(left, z[:, :, 1:T], col_at("tap2", at - 1), left,
                                                              ALU.mult, ALU.add))

            class Conv:
                frees = [(VE, 3 * k + 1) for k in range(RING)]

                def __call__(self, k, chunk, psum, done):
                    VE.after(done, VE.before(3 * k + 6) if k < RING - 1 else VE.here(3))
                    VE.mark(nc.vector.tensor_tensor(scaled[:, k, :], psum, rstd[:, :], ALU.mult))
                    taps((k - 1) % RING, chunk, VE.here(3 * k - 2) if k else VE.before(3 * RING - 2))

            cleared = VE.mark(nc.vector.memset(scaled[:, RING - 1, :], 0.0))
            VE.after(cleared)
            SE.after(cleared)
            convolved = linear("conv", 20, Conv(), [(SE, RING), (VE, 3 * RING)], inputs=h_ready)
            VE.after(VE.last())
            convolved = taps(RING - 1, 20, VE.last())
            PE.after(convolved)
            SE.after(convolved)

            VE.after(loaded_c1)
            PE.after(loaded_c1, loaded_f1, loaded_f23, loaded_f4)
            filt = filter_layer(0, f1[0:FILTER_EMB, :], c1v("emb", T, FILTER_EMB), [])
            free(5)
            for t in range(TT):
                mm = nc.tensor.matmul(banks[5][:, t:t + 1], rstd[0:1, t * P:(t + 1) * P], ones[0:1, 0:1],
                                      start=True, stop=True)
            rstd_col = sb("rstd_col", [TT], one)
            VE.after(PE.mark(mm))
            rstd_col_ready = freed[5] = VE.mark(nc.vector.tensor_copy(rstd_col[:, :], banks[5][:, 0:TT]))
            SE.after(rstd_col_ready)
            value_tiles = values("value", v_sb, rstd_col)
            next(value_tiles)
            gates_ready = input_gates()
            filt = filter_layer(1, f23[0:FILTER_HIDDEN, 0, :], hid[0:FILTER_HIDDEN, :], [filt])

            qk_ready = SE.mark(nc.scalar.activation(cv[:, 12:20, :], cv[:, 12:20, :], ACT.Silu))

            next(value_tiles)
            filt = filter_layer(2, f23[0:FILTER_HIDDEN, 1, :], hid[0:FILTER_HIDDEN, :], [filt])
            next(value_tiles)

            rows = {n: sb(n, [2, T], one) for n in ("lf", "row_a", "csum", "cgate", "peak", "negm")}

            def row(name):
                return rows[name][0:M_HEADS, :, :]

            PE.after(gates_ready)
            free(4, 5)
            for kind in range(4):
                bank = banks[4 + kind % 2]
                mm = nc.tensor.matmul(bank[0:M_HEADS, (kind // 2) * T:(kind // 2 + 1) * T],
                                      const[0:16, CONST["ident"] + 4 * kind:CONST["ident"] + 4 * kind + 4],
                                      gates[0:16, :], start=True, stop=True)
            gates_rows = PE.mark(mm)
            v_ready = next(value_tiles)
            base = STREAM["ogate"]
            for k in range(RING):
                fetch(k, base + k, tiles_d[base + k:base + k + 1])

            def bank_row(b):
                return banks[b][0:M_HEADS, :].rearrange("p (d t) -> p d t", d=2)

            SE.after(gates_rows)
            s = SE.mark(nc.scalar.activation(row("row_a"), bank_row(5), ACT.Abs))
            SE.after(s)
            s = SE.mark(nc.scalar.activation(row("row_a"), row("row_a"), ACT.Exp, scale=-1.0))
            SE.after(s)
            s = SE.mark(nc.scalar.activation(row("row_a"), row("row_a"), ACT.Ln, bias=1.0))
            VE.after(s)
            s = VE.mark(nc.vector.scalar_tensor_tensor(row("lf"), bank_row(5), 0.0, row("row_a"), ALU.min,
                                                       ALU.subtract))
            freed[5] = s
            VE.after(s)
            scan_ones = ones[0:M_HEADS, 0:1].to_broadcast([M_HEADS, T])

            def along(name, d):
                return rows[name][0:M_HEADS, 0, :] if d == 0 else rows[name][0:M_HEADS, 1, ::-1]

            for d in range(2):
                s = VE.mark(nc.vector.tensor_tensor_scan(along("csum", d), scan_ones, along("lf", d), 0.0,
                                                         ALU.mult, ALU.add))
            VE.after(s)
            s = VE.mark(nc.vector.tensor_tensor(row("cgate"), bank_row(4), row("csum"), ALU.subtract))
            VE.after(s)
            cgate_ready = freed[4] = s
            for d in range(2):
                s = VE.mark(nc.vector.tensor_tensor_scan(along("peak", d), along("cgate", d), along("cgate", d),
                                                         0.0, ALU.max, ALU.max))
            VE.after(s)
            s = VE.mark(nc.vector.scalar_tensor_tensor(row("negm"), row("csum"), -1.0, row("peak"), ALU.mult,
                                                       ALU.subtract))
            VE.after(s)
            rows_ready = VE.mark(nc.vector.tensor_scalar(row("peak"), row("peak"), -1.0, None, ALU.mult))

            PE.after(cgate_ready)
            free(6)
            for d in range(2):
                for t in range(TT):
                    at = (d * TT + t) * M_HEADS
                    mm = nc.tensor.transpose(banks[6][:, at:at + M_HEADS],
                                             rows["cgate"][0:M_HEADS, d, t * P:(t + 1) * P],
                                             const[0:M_HEADS, CONST["ident"]:CONST["ident"] + M_HEADS])
            mm = PE.mark(mm)
            ccol = sb("ccol", [2 * TT * M_HEADS], one)
            VE.after(mm)
            ccol_ready = freed[6] = VE.mark(nc.vector.tensor_copy(ccol[:, :], banks[6][:, 0:2 * TT * M_HEADS]))

            fbias_s = sem("loaded_fbias")
            PE.after(filt)
            for order in range(2):
                for d, dst in ((0, kf), (1, kb)):
                    for t in range(TT):
                        b = 2 * d + t
                        free(b)
                        w = (d * 2 + order) * HALF
                        mm = PE.mark(nc.tensor.matmul(banks[b][:, :], hid[0:FILTER_HIDDEN, t * P:(t + 1) * P],
                                                      f4[0:FILTER_HIDDEN, w:w + HALF], start=True, stop=True))
                        VE.after(mm)
                        s = freed[b] = VE.mark(nc.vector.tensor_tensor(dst[:, order, t, :], banks[b][:, :],
                                                                       window[:, t, :], ALU.mult))
            nc.gpsimd.wait_ge(*s)
            nc.gpsimd.dma_start(kb[0:1, :, 0, :], fbias_d).then_inc(fbias_s, 16)
            zx = scratch[:, :, :].rearrange("p (a b c) n -> p a b (c n)", a=2, b=TT)
            for n in range(2):
                for t in range(TT):
                    b = 4 + (2 * n + t) % 2
                    free(b)
                    for c in range(HC):
                        mm = nc.tensor.transpose(banks[b][:, c * P:(c + 1) * P], cv[:, 4 * n + c, t * P:(t + 1) * P],
                                                 ident)
                    mm = PE.mark(mm)
                    SE.after(mm)
                    s = freed[b] = SE.mark(nc.scalar.copy(zx[:, n, t, :], banks[b][:, :]))
            zx_ready = s

            def forward(z, ready):
                PE.after(ready)
                free(0, 1, 2, 3)
                done = []
                for f in range(TT):
                    at = slice(f * P, (f + 1) * P)
                    for b, mat in ((2 * f, fwd_cos), (2 * f + 1, fwd_sin)):
                        for t in range(TT):
                            mm = nc.tensor.matmul(banks[b][:, :], mat[:, t, at], z[:, t, :], start=t == 0,
                                                  stop=t == TT - 1)
                    done.append(PE.mark(mm))
                return done

            transformed = forward(zx[:, 0, :, :], zx_ready)

            VE.after((fbias_s, 16))
            VE.mark(nc.vector.tensor_tensor(ks[:, :, :, :], kf[:, :, :, :], kb[:, :, :, :], ALU.add))
            s2 = VE.mark(nc.vector.tensor_tensor(kf[:, :, :, :], kf[:, :, :, :], kb[:, :, :, :], ALU.subtract))
            PE.after(s2)

            spec_r = [sb(f"spec_r{o}", [TT, HALF], one) for o in range(2)]
            spec_i = [sb(f"spec_i{o}", [TT, HALF], one) for o in range(2)]
            spec_n = [sb(f"spec_n{o}", [HALF], one) for o in range(2)]
            spectra = {}

            def spectrum(dst, matrix, src, b):
                free(b)
                for t in range(TT):
                    mm = nc.tensor.matmul(banks[b][:, :], matrix(t), src(t), start=t == 0, stop=t == TT - 1)
                mm = PE.mark(mm)
                SE.after(mm)
                freed[b] = SE.mark(nc.scalar.copy(dst, banks[b][:, :]))
                return freed[b]

            def filter_spectra(o):
                for f in range(TT):
                    at = slice(f * P, (f + 1) * P)
                    spectrum(spec_r[o][:, f, :], lambda t: fwd_cos[:, t, at], lambda t: ks[:, o, t, :], 4)
                    m = (lambda t: fwd_sin_a[:, t, :]) if f == 0 else (lambda t: fwd_sin[:, t, at])
                    spectrum(spec_i[o][:, f, :], m, lambda t: kf[:, o, t, :], 5)
                spectra[o] = spectrum(spec_n[o][:, :], lambda t: fwd_cos_a[:, t, :], lambda t: ks[:, o, t, :], 6)

            yr = cv[:, 0:HC, :].rearrange("p (a b) n -> p a (b n)", a=TT)
            yi = cv[:, HC:DC, :].rearrange("p (a b) n -> p a (b n)", a=TT)
            prod = sb("prod", [TT, HALF], one)

            def multiply_spectra(order, done):
                VE.after(spectra[order])
                for f in range(TT):
                    re, im = banks[2 * f][:, :], banks[2 * f + 1][:, :]
                    k_r, k_i = spec_r[order][:, f, :], spec_i[order][:, f, :]
                    k_n = spec_n[order][:, :] if f == 0 else k_r
                    VE.after(done[f])
                    VE.mark(nc.vector.tensor_tensor(yr[:, f, :], re, k_r, ALU.mult))
                    s1 = VE.mark(nc.vector.tensor_tensor(prod[:, f, :], im, k_i, ALU.mult))
                    VE.mark(nc.vector.tensor_tensor(yi[:, f, :], re, k_i, ALU.mult))
                    VE.after(s1)
                    s2 = VE.mark(nc.vector.tensor_tensor(yr[:, f, :], yr[:, f, :], prod[:, f, :], ALU.subtract))
                    freed[2 * f] = s2
                    VE.after(s2)
                    s3 = freed[2 * f + 1] = VE.mark(nc.vector.tensor_tensor(prod[:, f, :], im, k_n, ALU.mult))
                    VE.after(s3)
                    s4 = VE.mark(nc.vector.tensor_tensor(yi[:, f, :], yi[:, f, :], prod[:, f, :], ALU.add))
                return s4

            filter_spectra(0)
            s4 = multiply_spectra(0, transformed)
            filter_spectra(1)

            weights = sb("wts", [TT, 2 * T], one)
            guard = sb("guard", [2 * T], one)
            parts = sb("parts", [2 * T], one)
            hm = mixT[:, 0:HC, :]

            def mlstm_head(h):
                scores, peaks, negms, gate = banks[4], banks[5], banks[6], banks[7]
                den = peaks
                PE.after(qk_ready, rows_ready)
                free(4, 5, 6, 7)
                for t in range(TT):
                    mm = nc.tensor.matmul(scores[:, t * T:(t + 1) * T], cv[:, 16 + h, t * P:(t + 1) * P],
                                          cv[:, 12 + h, :], start=True, stop=True)
                sel = c1v("head_rows", M_HEADS * P, M_HEADS)[:, h * P:(h + 1) * P]
                nc.tensor.matmul(peaks[:, :], sel, rows["peak"][0:M_HEADS, :, :], start=True, stop=True)
                mm = PE.mark(nc.tensor.matmul(negms[:, :], sel, rows["negm"][0:M_HEADS, :, :], start=True,
                                              stop=True))
                split((h + 1) % RING, STREAM["ogate"] + h + 1)
                product3(gate[:, 0:T], h, STREAM["ogate"] + h, h_parts)
                VE.after(mm, ccol_ready)
                SE.after(mm)
                for t in range(TT):
                    s = freed[5] = VE.mark(nc.vector.tensor_tensor(weights[:, t, :], peaks[:, :], dir_mask[:, t, :],
                                                                   ALU.add))
                    SE.after(s)
                    for d in range(2):
                        at = (d * TT + t) * M_HEADS + h
                        e = SE.mark(nc.scalar.activation(weights[:, t, d * T:(d + 1) * T],
                                                         weights[:, t, d * T:(d + 1) * T], ACT.Exp,
                                                         bias=ccol[:, at:at + 1]))
                    VE.after(e)
                    s = VE.mark(nc.vector.scalar_tensor_tensor(
                        weights[:, t, :].rearrange("p (d n) -> p d n", d=2),
                        scores[:, t * T:(t + 1) * T].unsqueeze(1).to_broadcast([P, 2, T]), float(P) ** -0.5,
                        weights[:, t, :].rearrange("p (d n) -> p d n", d=2), ALU.mult, ALU.mult))
                g = freed[6] = SE.mark(nc.scalar.activation(guard[:, :], negms[:, :], ACT.Exp))
                VE.after(used(STREAM["ogate"] + h))
                freed[7] = VE.mark(nc.vector.tensor_tensor(og[:, h, :], gate[:, 0:T], rstd[:, :], ALU.mult))
                PE.after(s)
                for t in range(TT):
                    mm = nc.tensor.matmul(den[:, :], ones, weights[:, t, :], start=t == 0, stop=t == TT - 1)
                summed = PE.mark(mm)
                for t in range(TT):
                    mm = nc.tensor.matmul(scores[:, :], v_sb[:, t, h * P:(h + 1) * P], weights[:, t, :],
                                          start=t == 0, stop=t == TT - 1)
                nums = PE.mark(mm)
                VE.after(summed, g)
                s = VE.mark(nc.vector.scalar_tensor_tensor(parts[:, :], den[:, :], -1.0, guard[:, :], ALU.mult,
                                                           ALU.max))
                VE.after(s)
                s = VE.mark(nc.vector.tensor_tensor(parts[:, :], den[:, :], parts[:, :], ALU.max))
                VE.after(s)
                freed[5] = s
                s = VE.mark(nc.vector.reciprocal(parts[:, :], parts[:, :]))
                VE.after(s, nums)
                s = freed[4] = VE.mark(nc.vector.tensor_tensor(parts[:, :], scores[:, :], parts[:, :], ALU.mult))
                VE.after(s)
                return VE.mark(nc.vector.tensor_tensor(hm[:, h, :], parts[:, 0:T], parts[:, T:2 * T], ALU.add))

            mlstm_head(0)
            PE.after(s4)
            for t in range(TT):
                at = slice(t * P, (t + 1) * P)
                free(t)
                for n, (mat, y) in enumerate(((inv_cos, yr), (inv_sin, yi))):
                    for f in range(TT):
                        mm = nc.tensor.matmul(banks[t][:, :], mat[:, f, at], y[:, f, :], start=n + f == 0,
                                              stop=n + f == TT)
                mm = PE.mark(mm)
                VE.after(mm)
                z_ready = freed[t] = VE.mark(nc.vector.tensor_tensor(zx[:, 0, t, :], banks[t][:, :], zx[:, 1, t, :],
                                                                     ALU.mult))
            mlstm_head(1)
            s4 = multiply_spectra(1, forward(zx[:, 0, :, :], z_ready))
            mlstm_head(2)
            hm_ready = mlstm_head(3)
            SE.after(VE.last())
            VE.after(SE.mark(nc.scalar.activation(og[:, :, :], og[:, :, :], ACT.Sigmoid)), hm_ready)
            load_table(ACT.Sqrt)
            hm_ready = VE.mark(nc.vector.tensor_tensor(hm[:, :, :], hm[:, :, :], og[:, :, :], ALU.mult))

            group_root = {"head": rows["lf"][:, 0, :], "group": rows["row_a"][:, 0, :]}

            def add_group_squares(name, bank, src, c, sq, ready):
                SE.after(ready)
                PE.after(SE.mark(nc.scalar.activation(sq[:, c, :], src[:, c, :], ACT.Square)))
                sums = c1v(name + "_sums", HC * GROUPS)[:, c * GROUPS:(c + 1) * GROUPS]
                if c == 0:
                    free(bank)
                return PE.mark(nc.tensor.matmul(banks[bank][0:GROUPS, 0:T], sums, sq[:, c, :], start=c == 0,
                                                stop=c == HC - 1))

            def inverse_roots(name, bank, summed, n):
                SE.after(summed)
                root = group_root[name][0:GROUPS, :]
                freed[bank] = SE.mark(nc.scalar.activation(root, banks[bank][0:GROUPS, 0:T], ACT.Sqrt,
                                                           bias=eps_col[0:GROUPS, :], scale=1.0 / n))
                VE.after(freed[bank])
                return VE.mark(nc.vector.reciprocal(root, root))

            def group_normalise(name, src, dst_at, room, gain_name, ready):
                PE.after(ready)
                free(room, room + 1)
                steps = []
                for c in range(HC):
                    mm = nc.tensor.matmul(banks[room + c // 2][:, (c % 2) * T:(c % 2 + 1) * T],
                                          c1v("group_rows", HC * P, GROUPS)[:, c * P:(c + 1) * P],
                                          group_root[name][0:GROUPS, :], start=True, stop=True)
                    if c % 2:
                        steps.append(PE.mark(mm))
                for b in range(2):
                    VE.after(steps[b])
                    for c in (2 * b, 2 * b + 1):
                        s = VE.mark(nc.vector.scalar_tensor_tensor(
                            mixT[:, dst_at + c, :], src[:, c, :], col(gain_name, c),
                            banks[room + b][:, (c % 2) * T:(c % 2 + 1) * T], ALU.mult, ALU.mult))
                    freed[room + b] = s
                    at = dst_at + 2 * b
                    done = into_parts(mixT[:, at:at + 2, :], at, [s])
                return done

            for c in range(HC):
                summed = add_group_squares("head", 6, hm, c, square, hm_ready)
            heads_root = inverse_roots("head", 6, summed, HALF // M_HEADS)
            PE.after(s4)
            zT = scratch[:, 4:8, :]
            z_ready = []
            for c in range(HC + 1):
                if c < HC:
                    dst = banks[c][:, 0:T]
                    free(c)
                    for n, (mat, y) in enumerate(((inv_cos, yr), (inv_sin, yi))):
                        for f in range(TT):
                            mm = nc.tensor.matmul(dst, y[:, f, c * P:(c + 1) * P], mat[:, f, :], start=n + f == 0,
                                                  stop=n + f == TT)
                    VE.after(PE.mark(mm))
                    freed[c] = VE.mark(nc.vector.tensor_tensor(zT[:, c, :], dst, cv[:, 8 + c, :], ALU.mult))
                    z_ready.append(freed[c])
                if c:
                    summed = add_group_squares("group", 7, zT, c - 1, scratch, z_ready[c - 1])
            heads_done = group_normalise("head", hm, 0, 4, "mlstm_norm", heads_root)
            groups_root = inverse_roots("group", 7, summed, HALF // GROUPS)
            h_ready = [heads_done, group_normalise("group", zT, HC, 0, "hyena_norm", groups_root)]

            yT = cv[:, 0:DC, :]

            clear_sumsq()
            y_ready, summed = copied_layer("out", DC, yT, squares=True, inputs=h_ready)
            VE.after(y_ready)
            normed = inverse_rms(4, summed)
            VE.after(normed)
            steps, parts, lag = [], [], 2
            for c in range(DC + lag):
                if c < DC:
                    steps.append(residual_chunk(yT, c, col("norm_mix_post", c)))
                if c >= lag:
                    parts.append(part_chunk(xT, c - lag, col("norm_mlp_pre", c - lag), steps[c - lag]))
                    summed = chunk_square(xT, c - lag, 5, steps[c - lag])
            normed = inverse_root(summed, 5)
            h_ready = [parts[DC // 2 - 1], parts[DC - 1]]
            mix_done = normed
        with ExitStack() as two:
            ff_hi, ff_lo = (sb(n, [FF // P, T], two, F32R) for n in ("ff_hi", "ff_lo"))
            yT = sb("yT2", [DC, T], two)
            scratch = sb("scratch2", [DC, T], two)
            NQ = N_MOD * D // (2 * RING)
            ada_w = [sb(f"ada_w{b}", [NQ], two) for b in range(RING)]
            acc = sb("acc", [N_MOD * D], two)
            sc = sb("silu_c", [DC], two)
            ada_loaded = [sem(f"ada_loaded{b}") for b in range(RING)]
            SE.after(mix_done)
            VE.after(SE.mark(nc.scalar.activation(sc[:, :], col("c", 0, DC), ACT.Silu)))
            load_table(ACT.Sqrt)
            GP.after(mix_done)
            VE.after(GP.mark(nc.gpsimd.memset(acc[:, :], 0.0)))
            begun = SE.last()

            def added(half, b):
                return VE.before(b + 1 if half else 2 * b + 2)

            def ada_load(half, i, b):
                q = RING * half + b
                for step in (begun, added(half, b)):
                    nc.sync.wait_ge(*step)
                nc.sync.dma_start(ada_w[b][:, :], ada_d[bass.ds(i, 1), :, q * NQ:(q + 1) * NQ]
                                  .rearrange("a p n -> p (a n)")).then_inc(ada_loaded[b], 16)

            def ada_add(half, i, b):
                VE.after(added(half, b))
                q = RING * half + b
                VE.after((ada_loaded[b], i * 16 + 16 + half * DC * 16))
                dst = acc[:, q * NQ:(q + 1) * NQ]
                VE.mark(nc.vector.scalar_tensor_tensor(dst, ada_w[b][:, :], sc[:, bass.ds(i, 1)], dst,
                                                       ALU.mult, ALU.add))

            relu = sb("relu", [RING, T], two)

            class Relu2:
                frees = [(VE, 2 * k + 1) for k in range(RING)]

                def __call__(self, k, chunk, psum, done):
                    VE.after(done, GP.before(2 * k + 2))
                    s = VE.mark(nc.vector.scalar_tensor_tensor(relu[:, k, :], psum, 0.0, rstd[:, :], ALU.max,
                                                               ALU.mult))
                    GP.after(s)
                    squared = GP.mark(nc.gpsimd.tensor_tensor(square[:, k, :], relu[:, k, :], relu[:, k, :],
                                                              ALU.mult))
                    SE.after(s)
                    rounded = SE.mark(nc.scalar.activation(ff_hi[:, bass.ds(chunk, 1), :], relu[:, k:k + 1, :],
                                                           ACT.Square))
                    GP.after(squared, rounded)
                    GP.mark(nc.gpsimd.tensor_tensor(ff_lo[:, bass.ds(chunk, 1), :], square[:, k:k + 1, :],
                                                    ff_hi[:, bass.ds(chunk, 1), :], ALU.subtract))
                    ada_add(0, VE.i, k)

            VE.after(normed)
            steps = linear("mlp_in", FF // P, Relu2(), [(SE, RING), (VE, 2 * RING), (GP, 2 * RING)],
                           lambda i, k: ada_load(0, i, k), inputs=h_ready)
            PE.after(*steps)
            VE.after(VE.last())
            clear_sumsq()

            base = STREAM["mlp_out"]
            free(4)
            with nc.Fori(0, DC) as i:
                SE.enter(i, 2)
                GP.enter(i, 1)
                VE.enter(i, RING)
                for k in range(RING):
                    fetch(k, base + i * RING + k, tiles_d[bass.ds(base + i * RING + k, 1)])
                    ada_load(1, i, k)
                PE.after(SE.before(SE.per))
                for k in range(RING):
                    j = base + i * RING + k
                    split((k + 1) % RING, j + 1)
                    product3(banks[4][:, 0:T], k, j, lambda c: (ff_hi[:, k * DC + c, :], ff_lo[:, k * DC + c, :]),
                             first=k == 0, last=k == RING - 1)
                    ada_add(1, i, k)
                SE.after(used(base + i * RING + RING - 1))
                SE.mark(nc.scalar.copy(yT[:, bass.ds(i, 1), :], banks[4][:, 0:T].unsqueeze(1)))
                add_square(0, banks[4][:, 0:T])
            y_ready = freed[4] = SE.leave(DC)
            summed = GP.leave(DC)
            acc_ready = VE.leave(DC)
            normed = inverse_rms(5, summed)

            PE.after(acc_ready)
            free(6)
            for n in range(N_MOD * DC):
                mm = nc.tensor.matmul(banks[6][:, n:n + 1], acc[:, n * P:(n + 1) * P], ones[:, 0:1], start=True,
                                      stop=True)
            mm = PE.mark(mm)

            VE.after(y_ready, normed)
            steps = []
            for c in range(DC):
                steps.append(residual_chunk(yT, c, col("norm_mlp_post", c)))
                summed = chunk_square(xT, c, 4, steps[c])
            VE.after(mm)
            freed[6] = VE.mark(nc.vector.tensor_tensor(mod[:, :], banks[6][:, 0:N_MOD * DC],
                                                       col("b_ada", 0, N_MOD * DC), ALU.add))
            VE.after(freed[6])
            VE.after(adaptive_gain("norm1", 1))
            h_ready = adaptive_parts(scratch, inverse_root(summed, 4), 0)

        with ExitStack() as three:
            qk = sb("qk", [DC, T], three)
            v_sb = sb("v2_sb", [TT, HALF], three)
            up = sb("up", [HC, PAD + T], three)
            sums = [sb(f"sums{b}", [PAD + T], three) for b in range(2)]
            mixed = sb("mixed", [HC, T], three)
            mixT = sb("mixT2", [DC, T], three)
            scratch = sb("scratch3", [DC, T], three)
            att = sb("att", [ATT_COLS], three)
            poolw = sb("poolw", [HC, P], three)
            probs = [sb(f"probs{t}", [A_HEADS, (t + 1) * P], three) for t in range(TT)]
            pT = [sb(f"pT{t}", [t + 1, A_HEADS, P], three) for t in range(TT)]
            stats = [sb(f"stats{t}", [3, A_HEADS], three) for t in range(TT)]
            memory_free = (h_ready[1], SE.last(), PE.last())
            GP.after(*memory_free)
            SE.after(h_ready[1])
            loaded_att = load(nc.gpsimd, "att", att[:, :], att_d)
            loaded_poolw = load(nc.gpsimd, "poolw", poolw[:, :, :], poolw_d)
            padded = GP.mark(nc.gpsimd.memset(up[:, :, 0:PAD], 0.0))
            for b in range(2):
                padded = GP.mark(nc.gpsimd.memset(sums[b][:, 0:PAD], 0.0))

            (qk_ready,) = copied_layer("qk", DC, qk, inputs=h_ready)
            PE.after(qk_ready)
            base = STREAM["pool_in"]
            for k in range(RING):
                free(k)
                fetch(k, base + k, tiles_d[base + k:base + k + 1])
                split((k + 1) % RING, base + k + 1)
                product3(banks[k][:, 0:T], k, base + k, h_parts)
                SE.after(used(base + k))
                up_ready = freed[k] = SE.mark(nc.scalar.copy(up[:, k, PAD:PAD + T], banks[k][:, 0:T]))
            PE.after(up_ready)

            def scores(t, first_bank):
                S = (t + 1) * P
                per_bank = 512 // S
                at = A_HEADS * P * t
                bias = att[:, at:at + A_HEADS * S].rearrange("p (h s) -> p h s", h=A_HEADS)
                for n_bank in range(A_HEADS // per_bank):
                    b = first_bank + n_bank
                    free(b)
                    for n in range(per_bank):
                        h = HEAD_ORDER[n_bank * per_bank + n]
                        lo = A_DIM * (h % 2)
                        mm = nc.tensor.matmul(banks[b][:, n * S:(n + 1) * S],
                                              qk[lo:lo + A_DIM, h // 2, t * P:(t + 1) * P],
                                              qk[lo:lo + A_DIM, HC + h // 2, 0:S], start=True, stop=True)
                    VE.after(PE.mark(mm))
                    hs = slice(n_bank * per_bank, (n_bank + 1) * per_bank)
                    s = freed[b] = VE.mark(nc.vector.scalar_tensor_tensor(
                        probs[t][:, hs, :], banks[b][:, :].rearrange("p (h s) -> p h s", s=S), A_DIM ** -0.5,
                        bias[:, hs, :], ALU.mult, ALU.add))
                return s

            def exponentials(t, ready):
                p, st = probs[t], stats[t]
                VE.after(ready)
                VE.after(VE.mark(nc.vector.tensor_reduce(st[:, 0, :], p[:, :, :], AX.X, ALU.max)))
                s = VE.mark(nc.vector.tensor_scalar(st[:, 0, :], st[:, 0, :], -1.0, None, ALU.mult))
                SE.after(s)
                for h in range(A_HEADS):
                    s = SE.mark(nc.scalar.activation(p[:, h, :], p[:, h, :], ACT.Exp, bias=st[:, 0, h:h + 1],
                                                     accum_out=st[:, 1, h:h + 1]))
                return s

            def divide_by_sums(t, ready):
                p, st = probs[t], stats[t]
                VE.after(ready)
                VE.after(VE.mark(nc.vector.reciprocal(st[:, 2, :], st[:, 1, :])))
                return VE.mark(nc.vector.tensor_tensor(p[:, :, :], p[:, :, :], st[:, 2, :].unsqueeze(2)
                                                       .to_broadcast([P, A_HEADS, (t + 1) * P]), ALU.mult))

            def transpose_probs(t, room, ready):
                PE.after(ready)
                for k in range(t + 1):
                    for g in range(2):
                        b = room[2 * k + g]
                        free(b)
                        for n in range(4):
                            mm = nc.tensor.transpose(banks[b][:, n * P:(n + 1) * P],
                                                     probs[t][:, 4 * g + n, k * P:(k + 1) * P], ident)
                        SE.after(PE.mark(mm))
                        freed[b] = SE.mark(nc.scalar.copy(pT[t][:, k, 4 * g:4 * g + 4, :],
                                                          banks[b][:, :].rearrange("p (h s) -> p h s", h=4)))
                return freed[b]

            out_banks = (6, 7)

            def attend(t, ready):
                PE.after(ready)
                for n, h in enumerate(HEAD_ORDER):
                    lo = A_DIM * (h % 2)
                    bank, at = banks[out_banks[h // 4]], (h // 2 % 2) * T + t * P
                    for k in range(t + 1):
                        mm = nc.tensor.matmul(bank[lo:lo + A_DIM, at:at + P],
                                              v_sb[:, k, h * A_DIM:(h + 1) * A_DIM], pT[t][:, k, n, :],
                                              start=k == 0, stop=k == t)
                return PE.mark(mm)

            VE.after(loaded_att)
            value_tiles = values("value2", v_sb)
            biased = scores(1, 2)
            next(value_tiles)
            exps = exponentials(1, biased)
            next(value_tiles)
            biased = scores(0, 2)
            next(value_tiles)
            normed = divide_by_sums(1, exps)
            v_ready = next(value_tiles)
            exps = exponentials(0, biased)
            transposed = transpose_probs(1, (0, 1, 4, 5), normed)
            normed = divide_by_sums(0, exps)

            VE.after(up_ready, padded)
            for g in range(HC):
                src = up[:, g, :]
                for n in range(g + 1):
                    dst, w = sums[n % 2], 2**n
                    s = VE.mark(nc.vector.tensor_tensor(dst[:, PAD:PAD + T], src[:, PAD:PAD + T],
                                                        src[:, PAD - w:PAD + T - w], ALU.add))
                    VE.after(s)
                    src = dst[:, :]
                at = COUNT_AT + g * T
                s = VE.mark(nc.vector.tensor_tensor(mixed[:, g, :], src[:, PAD:PAD + T], att[:, at:at + T],
                                                    ALU.mult))
                VE.after(s)
                mixed_ready = VE.mark(nc.vector.tensor_tensor(mixed[:, g, :], mixed[:, g, :],
                                                              up[:, g, PAD:PAD + T], ALU.subtract))

            PE.after(v_ready)
            free(*out_banks)
            attend(1, transposed)
            transposed = transpose_probs(0, (2, 3), normed)
            att_done = attend(0, transposed)
            load_table(ACT.Sqrt)
            PE.after(mixed_ready, loaded_poolw)
            for g in range(HC):
                free(g)
                pooled = PE.mark(nc.tensor.matmul(banks[g][:, 0:T], poolw[:, g, :], mixed[:, g, :], start=True,
                                                  stop=True))
                VE.after(pooled)
                pool_ready = freed[g] = VE.mark(nc.vector.tensor_scalar(mixT[:, HC + g, :], banks[g][:, 0:T],
                                                                        col("pool_scale", g), None, ALU.mult))

            SE.after(att_done)
            for n, b in enumerate(out_banks):
                s = freed[b] = SE.mark(nc.scalar.copy(mixT[:, 2 * n:2 * n + 2, :],
                                                      banks[b][:, :].rearrange("p (a n) -> p a n", a=2)))
                att_ready = into_parts(mixT[:, 2 * n:2 * n + 2, :], 2 * n, [s])
            for c in (HC, HC + 2):
                pool_ready = into_parts(mixT[:, c:c + 2, :], c, [pool_ready])
            h_ready = [att_ready, pool_ready]

            class AddGated:
                frees = [(VE, k + 1) for k in range(RING)]

                def __call__(self, k, chunk, psum, done):
                    VE.after(done)
                    dst = xT[:, bass.ds(chunk, 1), :]
                    s = VE.mark(nc.vector.scalar_tensor_tensor(dst, psum.unsqueeze(1),
                                                               mod[:, bass.ds(chunk + 2 * DC, 1)], dst,
                                                               ALU.mult, ALU.add))
                    SE.after(s)
                    add_square(k, dst[:, 0, :])

            clear_sumsq()
            x_ready, _, summed = linear("out2", DC, AddGated(), [(VE, RING), (SE, RING), (GP, RING)],
                                        inputs=h_ready)
            VE.after(x_ready, adaptive_gain("norm2", 4))
            h_ready = adaptive_parts(scratch, inverse_rms(5, summed), 3)
            SE.after(h_ready[1])

        before_peer.close()
        acts = sb("acts", [NKEYS, T])
        pq = acts[:, 0:2 * PEER_HEADS, :]
        keys = sb("keys", [2, P])
        slotT = sb("slotT", [3, T + GROUP])

        def view(at, a, b):
            return acts[:, at:at + DC, :].rearrange("p n t -> p (n t)").rearrange("p (a b) -> p a b", a=a)

        score, second = view(96, 2 * PEER_HEADS, NKEYS), view(104, 2 * PEER_HEADS, NKEYS)
        left = view(112, 2 * PEER_HEADS, NKEYS)
        h_whole = view(120, DC, T)
        GP.after(h_ready[1], SE.last(), PE.last())
        loaded_keys = load(nc.gpsimd, "keys", keys[:, :, :], keys_d)

        (pq_ready,) = copied_layer("peer_q", 2 * PEER_HEADS, pq, last=True, inputs=h_ready)
        PE.after(pq_ready, loaded_keys)

        with ExitStack() as four:
            cand, pairs = score, left
            top_v = sb("top_v", [2 * PEER_HEADS, TOPK], four)
            top_i = sb("top_i", [2 * PEER_HEADS, TOPK], four, U32)
            best2 = sb("best2", [TT, PEER_HEADS, TOPK], four)
            best_i = sb("best_i", [PEER_HEADS, TOPK], four, U32)
            pos_i = sb("pos_i", [PEER_HEADS, TOPK], four, U32)
            key_f = sb("key_f", [2 * PEER_HEADS, TOPK], four)
            pos_f = sb("pos_f", [2, PEER_HEADS, TOPK], four)
            peak = sb("best_peak", [PEER_HEADS], four)
            zsum = sb("zsum", [TT, PEER_HEADS], four)
            slot2 = sb("slot2", [TT, 3, SLOTS], four)

            VE.after(pq_ready)
            whole_ready = VE.mark(nc.vector.tensor_tensor(h_whole, h_hi[:, :, :], h_lo[:, :, :], ALU.add))

            free(*range(8))
            for t in range(TT):
                for g in range(4):
                    for n in range(4):
                        hp = 4 * g + n
                        mm = nc.tensor.matmul(banks[4 * t + g][:, n * P:(n + 1) * P], pq[:, hp, t * P:(t + 1) * P],
                                              keys[:, hp % 2, :], start=True, stop=True)
                scored = PE.mark(mm)
            SE.after(scored)
            for t, dst in ((0, score), (1, second)):
                for g in range(4):
                    s = freed[4 * t + g] = SE.mark(nc.scalar.copy(
                        dst[:, 4 * g:4 * g + 4, :], banks[4 * t + g][:, :].rearrange("p (h s) -> p h s", h=4)))
            scores_ready = s
            PE.after(scores_ready, whole_ready)

            def activate(first, n, in_parts):
                base = N_TILES + first
                with nc.Fori(0, n // RING) as i:
                    SE.enter(i, RING)
                    for k in range(RING):
                        fetch(k, base + i * RING + k, u_d[bass.ds(i * RING + first + k, 1)])
                    for k in range(RING):
                        j = base + i * RING + k
                        PE.after(SE.before(k + 1))
                        if in_parts:
                            split((k + 1) % RING, j + 1)
                            product3(banks[k][:, 0:T], k, j, h_parts)
                        else:
                            product(banks[k][:, 0:T], k, j, lambda c: h_whole[:, c, :])
                        SE.after(used(j))
                        SE.mark(nc.scalar.activation(acts[:, bass.ds(i * RING + first + k, 1), :],
                                                     banks[k][:, 0:T].unsqueeze(1), ACT.Gelu))
                return SE.leave(n // RING)

            load_table(ACT.Gelu)
            activate(0, BESIDE, False)
            whole[0] += BESIDE

            def top16(n, src, rest, values, indices, ready):
                VE.after(*ready)
                for r in range(n):
                    s = VE.mark(nc.vector.max(values(r, 0), src(r)))
                VE.after(s)
                for r in range(n):
                    VE.mark(nc.vector.max_index(indices(r, 0), values(r, 0), src(r)))
                    s = VE.mark(nc.vector.match_replace(rest(r), values(r, 0), src(r), LOWEST))
                VE.after(s)
                for r in range(n):
                    s = VE.mark(nc.vector.max(values(r, 1), rest(r)))
                VE.after(s)
                for r in range(n):
                    s = VE.mark(nc.vector.max_index(indices(r, 1), values(r, 1), rest(r)))
                return s

            def eight(a):
                return lambda r, half: a[:, r, 8 * half:8 * half + 8]

            for t in range(TT):
                src = score if t == 0 else second
                best_v, slot = best2[:, t, :, :], slot2[:, t, :, :]
                s = top16(2 * PEER_HEADS, lambda r: src[:, r, :], lambda r: left[:, r, :], eight(top_v),
                          eight(top_i), [scores_ready])
                VE.after(s)
                v4 = top_v[:, :, :].rearrange("p (h c) k -> p h c k", c=2)
                cand4 = cand[:, :, :].rearrange("p r k -> p (r k)").rearrange("p (h a b) -> p h a b", a=TOPK, b=TOPK)
                first = v4[:, :, 0, :].unsqueeze(3).to_broadcast([P, PEER_HEADS, TOPK, TOPK])
                other = v4[:, :, 1, :].unsqueeze(2).to_broadcast([P, PEER_HEADS, TOPK, TOPK])
                s = VE.mark(nc.vector.tensor_tensor(cand4, first, other, ALU.add))
                kf_ready = VE.mark(nc.vector.tensor_copy(key_f[:, :, :], top_i[:, :, :]))
                cand_r = cand[:, :, :].rearrange("p r k -> p (r k)").rearrange("p (h n) -> p h n", h=PEER_HEADS)
                left_r = left[:, :, :].rearrange("p r k -> p (r k)").rearrange("p (h n) -> p h n", h=PEER_HEADS)
                s = top16(PEER_HEADS, lambda r: cand_r[:, r, :], lambda r: left_r[:, r, :], eight(best_v),
                          eight(best_i), [s])
                VE.after(s)
                s = VE.mark(nc.vector.tensor_copy(peak[:, :].unsqueeze(2), best_v[:, :, 0:1]))
                VE.after(s)
                s = VE.mark(nc.vector.tensor_tensor(best_v, best_v,
                                                    peak[:, :].unsqueeze(2).to_broadcast([P, PEER_HEADS, TOPK]),
                                                    ALU.subtract))
                for c, (op, n) in enumerate(((ALU.logical_shift_right, 4), (ALU.bitwise_and, TOPK - 1))):
                    s = VE.mark(nc.vector.tensor_single_scalar(pos_i[:, :, :], best_i[:, :, :], n, op))
                    VE.after(s)
                    s = VE.mark(nc.vector.tensor_copy(pos_f[:, c, :, :], pos_i[:, :, :]))
                    VE.after(s)
                VE.after(kf_ready)
                k4 = key_f[:, :, :].rearrange("p (h c) k -> p h c k", c=2)
                pairs4 = left[:, :, :].rearrange("p r k -> p (r k)").rearrange("p (h a b) -> p h a b", a=TOPK,
                                                                              b=TOPK)
                count = iota[:, 0:TOPK].unsqueeze(1).unsqueeze(1).to_broadcast([P, PEER_HEADS, TOPK, TOPK])
                for c in range(2):
                    place = pos_f[:, c, :, :].unsqueeze(3).to_broadcast([P, PEER_HEADS, TOPK, TOPK])
                    table = k4[:, :, c, :].unsqueeze(2).to_broadcast([P, PEER_HEADS, TOPK, TOPK])
                    s = VE.mark(nc.vector.tensor_tensor(pairs4, place, count, ALU.is_equal))
                    VE.after(s)
                    s = VE.mark(nc.vector.tensor_tensor(pairs4, pairs4, table, ALU.mult))
                    VE.after(s)
                    s = VE.mark(nc.vector.tensor_reduce(
                        slot[:, 2 * c, :].rearrange("p (h k) -> p h k", h=PEER_HEADS), pairs4, AX.X, ALU.add))
                    VE.after(s)
            split(0, N_TILES + BESIDE)
            SE.after(s)
            flat = best2[:, :, :, :].rearrange("p t h k -> p (t h) k")
            s = SE.mark(nc.scalar.activation(flat, flat, ACT.Exp))
            VE.after(s)
            zs = zsum[:, :, :].rearrange("p t h -> p (t h)")
            s = VE.mark(nc.vector.tensor_reduce(zs, flat, AX.X, ALU.add))
            VE.after(s)
            s = VE.mark(nc.vector.reciprocal(zs, zs))
            VE.after(s)
            for t in range(TT):
                s = VE.mark(nc.vector.tensor_tensor(
                    slot2[:, t, 1, :].rearrange("p (h k) -> p h k", h=PEER_HEADS), best2[:, t, :, :],
                    zsum[:, t, :].unsqueeze(2).to_broadcast([P, PEER_HEADS, TOPK]), ALU.mult))

            load_table(ACT.Gelu)
            acts_ready = activate(BESIDE, NKEYS - BESIDE, True)

            PE.after(s)
            for t in range(TT):
                free(4 + t)
                for n in range(3):
                    mm = nc.tensor.transpose(banks[4 + t][:, n * P:(n + 1) * P], slot2[:, t, n, :], ident)
                mm = PE.mark(mm)
                VE.after(mm)
                slots_ready = freed[4 + t] = VE.mark(nc.vector.tensor_copy(
                    slotT[:, 0:3, t * P:(t + 1) * P], banks[4 + t][:, 0:3 * P].rearrange("p (n k) -> p n k", n=3)))

        BODY = 4
        five = ctx.enter_context(ExitStack())
        hot1 = [sb(f"hot1_{b}", [GROUP, NKEYS], five) for b in range(2)]
        hot2 = [sb(f"hot2_{b}", [GROUP, NKEYS], five) for b in range(BODY)]
        now = sb("now", [2, BODY * GROUP], five)

        def gated_rows(b, group, *wait_for):
            VE.after(*wait_for)
            for n in range(GROUP):
                at = group * GROUP + n
                VE.mark(nc.vector.tensor_scalar(hot1[b][:, n, :], iota, now[:, 0, at:at + 1],
                                                now[:, 1, at:at + 1], ALU.is_equal, ALU.mult))

        GP.after(slots_ready)
        VE.after(slots_ready, acts_ready)
        PE.after(acts_ready)
        free(*range(BODY))
        gated_rows(0, 0, VE.mark(nc.vector.tensor_copy(now[:, :, 0:GROUP], slotT[:, 0:2, 0:GROUP])))
        VE.mark(nc.vector.memset(slotT[:, :, T:T + GROUP], 0.0))
        VE.after(VE.last())
        per = GROUP + 1
        trips = T // (BODY * GROUP)
        with nc.Fori(0, trips) as i:
            PE.enter(i, BODY)
            VE.enter(i, 1 + BODY * per)
            GP.enter(i, BODY)
            SE.enter(i, 2 * BODY)
            VE.after(VE.before(BODY * per))
            VE.after(VE.mark(nc.vector.tensor_copy(now[:, :, :],
                                                   slotT[:, 0:2, bass.ds(i * (BODY * GROUP) + GROUP, BODY * GROUP)])))
            for b in range(BODY):
                at = i * (BODY * GROUP) + b * GROUP
                made1 = VE.before(BODY * per) if b == 0 else VE.here(b * per)
                GP.after(PE.before(b + 1))
                diff = GP.mark(nc.gpsimd.tensor_tensor(
                    hot2[b][:, :, :], iota.unsqueeze(1).to_broadcast([P, GROUP, NKEYS]),
                    slotT[:, 2, bass.ds(at, GROUP)].unsqueeze(2).to_broadcast([P, GROUP, NKEYS]), ALU.subtract))
                SE.after(diff)
                SE.after(SE.mark(nc.scalar.activation(hot2[b][:, :, :], hot2[b][:, :, :], ACT.Square)))
                made2 = SE.mark(nc.scalar.activation(hot2[b][:, :, :], hot2[b][:, :, :], ACT.Relu, scale=-1.0,
                                                     bias=1.0))
                PE.after(made1, made2, VE.before((b + 1) * per + 1))
                for n in range(GROUP):
                    mm = nc.tensor.matmul(banks[b][:, n * P:(n + 1) * P], hot2[b][:, n, :], hot1[b % 2][:, n, :],
                                          start=True, stop=True)
                ahead = PE.before(BODY) if b == 0 else PE.last_at()
                multiplied = PE.mark(mm)
                gated_rows((b + 1) % 2, b, ahead)
                VE.after(multiplied)
                dst = acts[:, :, bass.ds(at, GROUP)]
                VE.mark(nc.vector.tensor_tensor(dst, banks[b][:, :].rearrange("p (n e) -> p e n", n=GROUP), dst,
                                                ALU.mult))
        PE.leave(trips)
        gated = VE.leave(trips)
        GP.leave(trips)
        SE.leave(trips)

        PE.after(gated)
        zeros = cst("zeros", HALF)
        for b in range(4):
            nc.tensor.matmul(banks[b][:, :], zeros[:, 0:P], zeros, start=True, stop=False, skip_group_check=True)
        base = N_TILES + NKEYS
        five.close()
        g_hi, g_lo = sb("g_hi", [2, T], dt=F32R), sb("g_lo", [2, T], dt=F32R)

        def split_acts(k, n):
            src = acts[:, bass.ds(n, 1), :]
            b = slice(k % 2, k % 2 + 1)
            nc.scalar.copy(g_hi[:, b, :], src)
            return lambda: nc.vector.tensor_tensor(g_lo[:, b, :], src, g_hi[:, b, :], ALU.subtract)

        load_table(ACT.Sqrt)
        SE.after(gated)
        VE.after(SE.mark(nc.scalar.copy(g_hi[:, 0:1, :], acts[:, 0:1, :])))
        PE.after(VE.mark(nc.vector.tensor_tensor(g_lo[:, 0:1, :], acts[:, 0:1, :], g_hi[:, 0:1, :], ALU.subtract)))

        def add_experts(i, follow=True):
            for k in range(RING):
                fetch(k, base + i * RING + k, v_d[bass.ds(i * RING + k, 1)])
            for k in range(RING):
                j = base + i * RING + k
                if follow or k < RING - 1:
                    split((k + 1) % RING, j + 1, lambda: split_acts(k + 1, i * RING + k + 1))
                product_of_half_banks(k, j, (g_hi[:, k % 2, :], g_lo[:, k % 2, :]))

        def product_of_half_banks(k, j, gates):
            for half in range(2):
                PE.after(parts_of(j, half))
                for c in range(half * DC // 2, (half + 1) * DC // 2):
                    at = slice(c * P, (c + 1) * P)
                    out = banks[c // 2][:, (c % 2) * T:(c % 2 + 1) * T]
                    for w, g in ((w_hi, gates[0]), (w_hi, gates[1]), (w_lo, gates[0])):
                        mm = nc.tensor.matmul(out, w[:, k % 2, at], g, start=False, stop=False,
                                              skip_group_check=True)
                mm.then_inc(half_used, 1)

        with nc.Fori(0, NKEYS // RING - 1) as i:
            add_experts(i)
        add_experts(NKEYS // RING - 1, False)
        for b in range(4):
            mm = nc.tensor.matmul(banks[b][:, :], zeros[:, 0:P], zeros, start=False, stop=True,
                                  skip_group_check=True)
        y_done = PE.mark(mm)
        VE.after(y_done)
        for c in range(DC):
            x_ready = VE.mark(nc.vector.scalar_tensor_tensor(
                xT[:, c, :], banks[c // 2][:, (c % 2) * T:(c % 2 + 1) * T], mod[:, 5 * DC + c:5 * DC + c + 1],
                xT[:, c, :], ALU.mult, ALU.add))
            summed = chunk_square(xT, c, 4, x_ready, acts[:, 2 * DC:2 * DC + RING, :])
        VE.after(inverse_root(summed, 4))
        outT = acts[:, 0:DC, :]
        stored = sem("stored")
        for c in range(DC):
            out_ready = VE.mark(nc.vector.scalar_tensor_tensor(outT[:, c, :], xT[:, c, :], col("final", c),
                                                               rstd[:, :], ALU.mult, ALU.mult))
            if c % 2:
                nc.sync.wait_ge(*out_ready)
                nc.sync.dma_start(out_d[:, c - 1:c + 1, :], outT[:, c - 1:c + 1, :]).then_inc(stored, 16)
        nc.sync.wait_ge(stored, 16 * DC // 2)


def constants():
    def pack(table, n_cols, parts):
        out = np.zeros((P, n_cols), np.float32)
        for name, a in parts.items():
            a = np.asarray(a, np.float64).astype(np.float32)
            out[:a.shape[0], table[name]:table[name] + a.shape[1]] = a
        return out

    lanes = np.arange(P)
    tok = np.arange(T)
    rows = np.zeros((M_HEADS, M_HEADS, P))
    for h in range(M_HEADS):
        rows[h, h] = 1
    group = (np.arange(HALF) // (HALF // GROUPS)).reshape(HC, P)
    group_rows = (np.arange(GROUPS)[:, None] == group.reshape(-1)) * 1.0
    group_sums = np.stack([group[c][:, None] == np.arange(GROUPS) for c in range(HC)], axis=1).reshape(P, -1)
    head_sums = np.tile((np.arange(HC)[:, None] == np.arange(GROUPS) // 2).reshape(1, -1), (P, 1))
    const = pack(CONST, N_CONST, {
        "ident": np.eye(P), "ones": np.ones((P, P)), 
        "iota": np.tile(lanes, (P, 1)), "eps": np.full((P, 1), EPS),
        "zeros": np.zeros((P, HALF)),
    })

    f32 = np.float32
    bands = (FILTER_EMB - 1) // 2
    t = np.linspace(0.0, 1.0, T, dtype=f32)
    ang = (f32(2.0 * math.pi) * tok.astype(f32) / f32(T))[:, None]
    f = np.linspace(1e-4, bands - 1, bands, dtype=f32)[None, :]
    phase = (f * ang).astype(np.float64)
    emb = np.concatenate([t[:, None], np.cos(phase), -np.sin(phase)], axis=1).T
    deltas = np.linspace(math.log(1e-2) / 1.5, math.log(1e-2) / 0.3, HALF, dtype=f32)
    window = np.exp(-t[:, None].astype(np.float64) * np.abs(deltas))

    def by_tile(a):
        return a.reshape(TT, P, -1).transpose(1, 0, 2).reshape(P, -1)

    theta = 2 * math.pi * ((tok[:, None] * tok[None, :]) % (2 * T)) / (2 * T)
    alt = (-1.0) ** tok
    cos, sin = np.cos(theta), -np.sin(theta)
    sin_nyq, cos_nyq, sin_a = sin.copy(), cos[:, :P].copy(), sin[:, :P].copy()
    sin_nyq[:, 0] = alt
    cos_nyq[:, 0] = alt
    sin_a[:, 0] = 0
    inv_cos, inv_sin = 2 * cos.T / (2 * T), 2 * sin.T / (2 * T)
    inv_cos[0] = 1.0 / (2 * T)
    inv_sin[0] = alt / (2 * T)
    mask = np.zeros((TT, P, 2, T))
    for n in range(TT):
        key = n * P + lanes[:, None]
        mask[n, :, 0] = np.where(key <= tok, 0, NEG)
        mask[n, :, 1] = np.where(key >= tok, 0, NEG)
    const1 = pack(CONST1, N_CONST1, {
        "emb": emb, "window": by_tile(window), "fwd_cos": by_tile(cos), "fwd_sin": by_tile(sin_nyq),
        "fwd_cos_a": by_tile(cos_nyq), "fwd_sin_a": by_tile(sin_a), "inv_cos": by_tile(inv_cos),
        "inv_sin": by_tile(inv_sin), "dir_mask": mask.transpose(1, 0, 2, 3).reshape(P, -1),
        "head_sums": head_sums, "group_sums": group_sums, "group_rows": group_rows,
        "head_rows": rows.reshape(M_HEADS, -1),
    })

    att = []
    for n in range(TT):
        S = (n + 1) * P
        dist = (n * P + lanes[:, None]) - np.arange(S)[None, :]
        times = sum(((dist >= 0) & (dist <= w) & (dist % d == 0)).astype(np.float64) for w, d in BRANCHES)
        kept = np.log(np.maximum(times, 1))
        for h in HEAD_ORDER:
            slope = 2.0 ** (-8.0 * (h + 1) / A_HEADS)
            att.append(np.where(times > 0, kept - slope * dist, NEG))
    counts = np.stack([1.0 / np.minimum(tok + 1, w) for w in WINDOWS])
    att.append(np.tile(counts.reshape(1, -1), (P, 1)))
    return const, const1, np.concatenate(att, axis=1).astype(np.float32)


def kernel(**inputs):
    import concourse.bacc as bacc
    from concourse.bass_utils import run_bass_kernel_spmd

    a = {k: np.asarray(v) for k, v in inputs.items()}

    def by_chunk(w):
        return w.reshape(DC, P, -1, P).transpose(2, 1, 0, 3).reshape(-1, P, TILE)

    def by_rows(w):
        return w.reshape(RING, 2, P, HALF).transpose(0, 2, 1, 3).reshape(RING, P, TILE)

    w = a["w_in"]
    conv = np.r_[1024:1536, 1536:2048, 2048:2560, 0:512, 512:1024]
    w2 = a["w_in_2"][0]
    mlp_out = a["w_mlp_out"].reshape(4, DC, P, DC, P).transpose(3, 0, 2, 1, 4).reshape(-1, P, TILE)
    tiles = np.concatenate([
        by_chunk(w[:, conv]), by_rows(w[:, 2560:3072]), by_chunk(w[:, 3072:3584]), by_chunk(a["w_out"]),
        by_chunk(a["w_mlp_in"]), mlp_out, by_chunk(w2[:, 0:1024]), by_chunk(w2[:, 1536:2048]),
        by_rows(w2[:, 1024:1536]), by_chunk(a["w_out_2"][0]), by_chunk(a["peer_wq_2"][0])])

    cols = np.zeros((P, N_COLS), np.float32)

    def put(name, v, rows=P):
        v = v.reshape(-1, rows).T
        cols[:rows, COLS[name]:COLS[name] + v.shape[1]] = v

    for name, key in (("norm_mix_pre", "norm_mix_pre"), ("norm_mix_post", "norm_mix_post"),
                      ("norm_mlp_pre", "norm_mlp_pre"), ("norm_mlp_post", "norm_mlp_post"),
                      ("mlstm_norm", "mlstm_norm_w"), ("hyena_norm", "hyena_norm_w"), ("norm1", "norm1_g_2"),
                      ("pool_scale", "pool_scale_2"), ("norm2", "norm2_g_2"), ("final", "final_g_2"),
                      ("b_ada", "b_ada_2"), ("c", "c_2")):
        put(name, a[key])
    for n in range(3):
        put(f"tap{n}", a["conv_w"][n, conv])
    put("conv_b", a["conv_b"][conv])
    put("b_gates", a["b_gates"], 16)
    put("filt_b", np.stack([a["filt_b1"], a["filt_b2"], a["filt_b3"]]), FILTER_HIDDEN)
    put("filt_freq", a["filt_freq"], FILTER_HIDDEN)

    const, const1, att = constants()
    arrays = {
        "x": a["x"][0].T.reshape(DC, P, T).transpose(1, 0, 2),
        "tiles": tiles,
        "experts_u": a["peer_u_2"][0].reshape(NKEYS, P, DC, P).transpose(0, 3, 2, 1).reshape(NKEYS, P, TILE),
        "experts_v": a["peer_v_2"][0].reshape(NKEYS, P, TILE),
        "w_ada": a["w_ada_2"][0].reshape(DC, P, N_MOD * D),
        "cols": cols, "const": const, "const1": const1, "att": att,
        "gate_w": w[:, 3584:3600].reshape(DC, P, 16).transpose(1, 0, 2),
        "filt_w1": a["filt_w1"],
        "filt_w23": np.stack([a["filt_w2"], a["filt_w3"]], axis=1),
        "filt_w4": a["filt_w4"],
        "filt_bias": a["filt_bias"].reshape(1, 2, HALF),
        "pool_w": a["pool_w_2"][0].transpose(1, 0, 2),
        "keys": a["peer_subkeys_2"][0].transpose(2, 0, 1),
    }
    arrays = {f"in_{k}": np.ascontiguousarray(v) for k, v in arrays.items()}
    nc = bacc.Bacc("TRN2", target_bir_lowering=False, num_devices=1)
    args = [nc.dram_tensor(k, v.shape, F32, kind="ExternalInput").ap() for k, v in arrays.items()]
    args.append(nc.dram_tensor("out", (P, DC, T), F32, kind="ExternalOutput").ap())
    build(nc, *args)
    result = run_bass_kernel_spmd(nc, [arrays], core_ids=[0]).results[0]["out"]
    return result.transpose(1, 0, 2).reshape(D, T).T.reshape(1, T, D)
```
